# Optimizing a Trainium2 kernel written in Bass

```python
import jax, jax.numpy as jnp
from jax import lax
import numpy as np

D_MODEL = 1024
BATCH = 1
SEQ = 2048
DEPTH = 1
DEC_BATCH = 8
DEC_SEQ = 4
PAST_LEN = 4096
PAGE_SIZE = 128

HEAD_DIM = 64
D_MIX = D_MODEL
D_CONV = (3 * D_MIX) // 8
N_MEM_HEADS = 4
D_MEMQ = N_MEM_HEADS * HEAD_DIM
D_SWA = D_MIX - D_CONV - D_MEMQ
N_SWA_HEADS = D_SWA // HEAD_DIM
N_SWA_KV = 2
SWA_GROUP = N_SWA_HEADS // N_SWA_KV
D_SWA_KV = N_SWA_KV * HEAD_DIM
N_MEM = 256
CONV_WIDTH = 3
WINDOW = 128
BLOCK = 128
RMS_EPS = 1e-6
NEG_INF = -1e30
SPLIT_SIZES = (D_CONV, D_CONV, D_CONV, D_CONV, D_SWA, D_SWA_KV, D_SWA_KV, D_SWA, D_MEMQ, D_MEMQ)
D_IN = sum(SPLIT_SIZES)

kernel_name = "hymba_conv_swa_sink_alibi_memxattn_step"

def rms_norm(x, g):
    xf = x.astype(jnp.float32)
    y = xf * lax.rsqrt(jnp.mean(xf * xf, axis=-1, keepdims=True) + RMS_EPS) * g.astype(jnp.float32)
    return y.astype(x.dtype)

def alibi_slopes():
    h = np.arange(1, N_SWA_HEADS + 1, dtype=np.float32)
    return jnp.asarray(np.power(np.float32(2.0), -8.0 * h / N_SWA_HEADS).astype(np.float32))

def project_in(x, pre_g, w_in):
    h = rms_norm(x, pre_g)
    z = h @ w_in
    points = [int(p) for p in np.cumsum(SPLIT_SIZES)[:-1]]
    return jnp.split(z, points, axis=-1)

def project_out(x, y_conv, y_swa, y_mem, post_g, w_out):
    y = jnp.concatenate([y_conv, y_swa, y_mem], axis=-1) @ w_out
    return x + rms_norm(y, post_g)

def short_conv(u_full, conv_w):
    T = u_full.shape[1] - (CONV_WIDTH - 1)
    out = conv_w[0] * u_full[:, 0:T]
    for j in range(1, CONV_WIDTH):
        out = out + conv_w[j] * u_full[:, j:j + T]
    return out

def swa_attention(q, k, v, q_pos, k_pos, sinks):
    N, nb, Tq = q.shape[:3]
    qg = q.reshape(N, nb, Tq, N_SWA_KV, SWA_GROUP, HEAD_DIM).astype(jnp.float32)
    s = jnp.einsum('nbqkgd,nbskd->nbkgqs', qg, k.astype(jnp.float32)) * (HEAD_DIM ** -0.5)
    dist = q_pos[:, :, None] - k_pos[:, None, :]
    valid = (dist >= 0) & (dist < WINDOW) & (k_pos[:, None, :] >= 0)
    slopes = alibi_slopes().reshape(N_SWA_KV, SWA_GROUP)
    s = s - slopes[None, None, :, :, None, None] * jnp.abs(dist).astype(jnp.float32)[None, :, None, None]
    s = jnp.where(valid[None, :, None, None], s, NEG_INF)
    sink = sinks.astype(jnp.float32).reshape(N_SWA_KV, SWA_GROUP)[None, None, :, :, None, None]
    sink = jnp.broadcast_to(sink, s.shape[:-1] + (1,))
    p = jax.nn.softmax(jnp.concatenate([s, sink], axis=-1), axis=-1)[..., :-1]
    o = jnp.einsum('nbkgqs,nbskd->nbqkgd', p, v.astype(jnp.float32))
    return o.reshape(N, nb, Tq, D_SWA).astype(q.dtype)

def mem_attention(q, mk, mv):
    N, T = q.shape[:2]
    qh = q.reshape(N, T, N_MEM_HEADS, HEAD_DIM).astype(jnp.float32)
    s = jnp.einsum('nthd,nmhd->nhtm', qh, mk.astype(jnp.float32)) * (HEAD_DIM ** -0.5)
    p = jax.nn.softmax(s, axis=-1)
    o = jnp.einsum('nhtm,nmhd->nthd', p, mv.astype(jnp.float32))
    return o.reshape(N, T, D_MEMQ).astype(q.dtype)

def mem_kv(mem, mem_g, w_mk, w_mv):
    N, M = mem.shape[:2]
    m = rms_norm(mem, mem_g)
    mk = (m @ w_mk).reshape(N, M, N_MEM_HEADS, HEAD_DIM)
    mv = (m @ w_mv).reshape(N, M, N_MEM_HEADS, HEAD_DIM)
    return mk, mv

def prompt_layer(x, mem, pre_g, post_g, w_in, conv_w, sinks, mem_g, w_mk, w_mv, w_out):
    B, T = x.shape[:2]
    cb, cc, ch, cz, q, k, v, sz, mq, mz = project_in(x, pre_g, w_in)
    u = cc * ch
    u_full = jnp.pad(u, ((0, 0), (CONV_WIDTH - 1, 0), (0, 0)))
    y_conv = cb * short_conv(u_full, conv_w) * jax.nn.silu(cz)
    conv_state = u[:, T - (CONV_WIDTH - 1):]
    nb = T // BLOCK
    k = k.reshape(B, T, N_SWA_KV, HEAD_DIM)
    v = v.reshape(B, T, N_SWA_KV, HEAD_DIM)
    pad = ((0, 0), (BLOCK, 0), (0, 0), (0, 0))
    kb = jnp.pad(k, pad).reshape(B, nb + 1, BLOCK, N_SWA_KV, HEAD_DIM)
    vb = jnp.pad(v, pad).reshape(B, nb + 1, BLOCK, N_SWA_KV, HEAD_DIM)
    k_band = jnp.concatenate([kb[:, :-1], kb[:, 1:]], axis=2)
    v_band = jnp.concatenate([vb[:, :-1], vb[:, 1:]], axis=2)
    qb = q.reshape(B, nb, BLOCK, N_SWA_HEADS, HEAD_DIM)
    q_pos = jnp.arange(T, dtype=jnp.int32).reshape(nb, BLOCK)
    k_pos = (jnp.arange(nb, dtype=jnp.int32)[:, None] * BLOCK - BLOCK
             + jnp.arange(2 * BLOCK, dtype=jnp.int32)[None, :])
    y_swa = swa_attention(qb, k_band, v_band, q_pos, k_pos, sinks).reshape(B, T, D_SWA) * jax.nn.silu(sz)
    keep = min(WINDOW, T)
    swa_k_state = k[:, T - keep:]
    swa_v_state = v[:, T - keep:]
    mk, mv = mem_kv(mem, mem_g, w_mk, w_mv)
    y_mem = mem_attention(mq, mk, mv) * jax.nn.silu(mz)
    y = project_out(x, y_conv, y_swa, y_mem, post_g, w_out)
    return y, conv_state, swa_k_state, swa_v_state, mk, mv

def sample_layer(x, conv_past, swa_k_past, swa_v_past, mk, mv, pre_g, post_g, w_in, conv_w, sinks, w_out):
    N, T = x.shape[:2]
    cb, cc, ch, cz, q, k, v, sz, mq, mz = project_in(x, pre_g, w_in)
    u = cc * ch
    u_full = jnp.concatenate([conv_past.astype(u.dtype), u], axis=1)
    y_conv = cb * short_conv(u_full, conv_w) * jax.nn.silu(cz)
    conv_state = u_full[:, u_full.shape[1] - (CONV_WIDTH - 1):]
    buf = swa_k_past.shape[1]
    k = k.reshape(N, T, N_SWA_KV, HEAD_DIM)
    v = v.reshape(N, T, N_SWA_KV, HEAD_DIM)
    k_all = jnp.concatenate([swa_k_past.astype(k.dtype), k], axis=1)
    v_all = jnp.concatenate([swa_v_past.astype(v.dtype), v], axis=1)
    q_pos = (PAST_LEN + jnp.arange(T, dtype=jnp.int32))[None]
    k_pos = jnp.concatenate([PAST_LEN - buf + jnp.arange(buf, dtype=jnp.int32),
                             PAST_LEN + jnp.arange(T, dtype=jnp.int32)])[None]
    qb = q.reshape(N, 1, T, N_SWA_HEADS, HEAD_DIM)
    y_swa = swa_attention(qb, k_all[:, None], v_all[:, None], q_pos, k_pos, sinks).reshape(N, T, D_SWA)
    y_swa = y_swa * jax.nn.silu(sz)
    swa_k_state = k_all[:, k_all.shape[1] - buf:]
    swa_v_state = v_all[:, v_all.shape[1] - buf:]
    y_mem = mem_attention(mq, mk, mv) * jax.nn.silu(mz)
    y = project_out(x, y_conv, y_swa, y_mem, post_g, w_out)
    return y, conv_state, swa_k_state, swa_v_state

def setup_inputs(seed: int = 0) -> dict:
    key = jax.random.key(seed)
    ks = jax.random.split(key, 20)
    f32 = jnp.float32
    swa_buf = min(WINDOW, PAST_LEN)
    nrm = lambda k, shape, s=1.0: jax.random.normal(k, shape, f32) * s
    return {
        "x_prompt": nrm(ks[0], (BATCH, SEQ, D_MODEL)),
        "x_sample": nrm(ks[1], (DEC_BATCH, DEC_SEQ, D_MODEL)),
        "mem_prompt": nrm(ks[2], (BATCH, N_MEM, D_MODEL)),
        "state_conv": nrm(ks[3], (DEPTH, DEC_BATCH, CONV_WIDTH - 1, D_CONV)),
        "cache_swa_k": nrm(ks[4], (DEPTH, DEC_BATCH, swa_buf, N_SWA_KV, HEAD_DIM)),
        "cache_swa_v": nrm(ks[5], (DEPTH, DEC_BATCH, swa_buf, N_SWA_KV, HEAD_DIM)),
        "cache_mem_k": nrm(ks[6], (DEPTH, DEC_BATCH, N_MEM, N_MEM_HEADS, HEAD_DIM)),
        "cache_mem_v": nrm(ks[7], (DEPTH, DEC_BATCH, N_MEM, N_MEM_HEADS, HEAD_DIM)),
        "pre_norm_g": 1.0 + nrm(ks[8], (DEPTH, D_MODEL), 0.05),
        "post_norm_g": 1.0 + nrm(ks[9], (DEPTH, D_MODEL), 0.05),
        "w_in": nrm(ks[10], (DEPTH, D_MODEL, D_IN), D_MODEL ** -0.5),
        "conv_w": nrm(ks[11], (DEPTH, CONV_WIDTH, D_CONV), CONV_WIDTH ** -0.5),
        "attn_sinks": nrm(ks[12], (DEPTH, N_SWA_HEADS), 0.5),
        "mem_norm_g": 1.0 + nrm(ks[13], (DEPTH, D_MODEL), 0.05),
        "w_mem_k": nrm(ks[14], (DEPTH, D_MODEL, D_MEMQ), D_MODEL ** -0.5),
        "w_mem_v": nrm(ks[15], (DEPTH, D_MODEL, D_MEMQ), D_MODEL ** -0.5),
        "w_out": nrm(ks[16], (DEPTH, D_MIX, D_MODEL), D_MIX ** -0.5),
    }

def reference(x_prompt, x_sample, mem_prompt, state_conv, cache_swa_k, cache_swa_v, cache_mem_k, cache_mem_v,
              pre_norm_g, post_norm_g, w_in, conv_w, attn_sinks, mem_norm_g, w_mem_k, w_mem_v, w_out):
    xp, xs = x_prompt, x_sample
    cp, kp, vp, mkp, mvp, cs, ks_, vs_ = [], [], [], [], [], [], [], []
    for l in range(DEPTH):
        xp, c1, k1, v1, mk1, mv1 = prompt_layer(xp, mem_prompt, pre_norm_g[l], post_norm_g[l], w_in[l], conv_w[l],
                                                attn_sinks[l], mem_norm_g[l], w_mem_k[l], w_mem_v[l], w_out[l])
        xs, c2, k2, v2 = sample_layer(xs, state_conv[l], cache_swa_k[l], cache_swa_v[l], cache_mem_k[l],
                                      cache_mem_v[l], pre_norm_g[l], post_norm_g[l], w_in[l], conv_w[l],
                                      attn_sinks[l], w_out[l])
        cp.append(c1); kp.append(k1); vp.append(v1); mkp.append(mk1); mvp.append(mv1)
        cs.append(c2); ks_.append(k2); vs_.append(v2)
    return (xp, xs, jnp.stack(cp), jnp.stack(kp), jnp.stack(vp), jnp.stack(mkp), jnp.stack(mvp),
            jnp.stack(cs), jnp.stack(ks_), jnp.stack(vs_))


_drawn_inputs = setup_inputs


def setup_inputs(seed=0):
    import zlib

    import numpy as np

    out = dict(_drawn_inputs(seed))
    spreads = {}
    factors = {'attn_sinks': 8.0}
    for name, (base, spread) in spreads.items():
        noise = np.random.default_rng([zlib.crc32(name.encode()), seed]).standard_normal(out[name].shape)
        drawn = base * np.exp(spread * noise) if base else spread * noise
        out[name] = __import__('jax').numpy.asarray(drawn.astype(out[name].dtype))
    for name, factor in factors.items():
        out[name] = (out[name] * factor).astype(out[name].dtype)
    return out
```

```python
from contextlib import ExitStack

import concourse.bass as bass
import numpy as np
from concourse import mybir

F32 = mybir.dt.float32
F32R = mybir.dt.float32r
ALU = mybir.AluOpType
ACT = mybir.ActivationFunctionType
AX = mybir.AxisListType

P = 128
D = 1024
KT = D // P
HD = 64
NQ = 4
TP = 512
NBLK = TP // P
SQ = 2
ST = 4
TS = SQ * ST
T = TP + TS
CW = T // 2
NH, NKV, G = 6, 2, 3
MH = 4
NM = 256
W = 128
DC = 384
EPS = 1e-6
SCALE = HD ** -0.5
NEG = -1e30

TILES = ["K", "M0", "M1", "Q0", "Q1", "Q2", "V", "Z3", "Z0", "Z1", "Z2", "Z4"]
for _j in range(3):
    TILES += [f"CC{_j}", f"CH{_j}", f"CB{_j}", f"CZ{_j}"]
NIN = len(TILES)
NOUT = D // P
NW = NIN + NOUT
NC = 2 * NW
OFF = {"CB": 0, "CC": DC, "CH": 2 * DC, "CZ": 3 * DC, "Q": 4 * DC, "K": 5 * DC, "V": 5 * DC + P, "Z": 5 * DC + 2 * P,
       "M": 6 * DC + 2 * P, "ZM": 6 * DC + 2 * P + NM}

AT_CACHE, AT_NAT = 1, 15
AT_SAMPLE = [13, 16, 17, 18]
AT_S = [19 + 7 * i for i in range(NBLK)]
AT_T = [23 + 7 * i for i in range(NBLK)]
AT_PV = [25 + 7 * i for i in range(NBLK)]


def role(n):
    return TILES[n // 2] if n < 2 * NIN else f"O{n // 2 - NIN}"


def freed_by_act(n):
    return role(n)[0] in "VO" or role(n)[:2] == "CC"


FREE_ACT = [sum(freed_by_act(m) for m in range(n + 1)) for n in range(NC)]
FREE_DVE = [n + 1 - FREE_ACT[n] for n in range(NC)]

Y_PARTS = 3 + NBLK + 1 + 1
NL_X = 10
PRO_W = 4
DVE_Q, POOL_Q = 73, NW


def layer(nc, x_prompt, x_sample, mem_prompt, state_conv, cache_k, cache_v, cache_mk, cache_mv, pre_g, post_g, w_in,
          conv_w, sinks, mem_g, w_mk, w_mv, w_out, ident_d, bias_d, bias_s_d, y_prompt, y_sample, conv_p, k_p, v_p,
          mk_p, mv_p, conv_s, k_s, v_s):
    with ExitStack() as ctx:
        def sb(name, shape, dt=F32):
            return ctx.enter_context(nc.sbuf_tensor(name, shape, dt))

        def at(name, shape, dt, offset):
            return nc.alloc_sbuf_tensor_at(name, shape, dt, offset=offset)

        def sem(name):
            return ctx.enter_context(nc.semaphore(name))

        h_hi, h_lo = sb("h_hi", [P, KT, T], F32R), sb("h_lo", [P, KT, T], F32R)
        y_at = nc.sbuf_base
        y_hi, y_lo = sb("y_hi", [P, KT, T], F32R), sb("y_lo", [P, KT, T], F32R)
        memk_c = at("memk_c", [P, 2, SQ, NM], F32, y_at)
        memv_c = at("memv_c", [P, 2, SQ, NM], F32, y_at + KT * T * 4)
        SR = 32 * SQ
        spot = [y_at + 3 * T * 4]

        def early(name, shape):
            t = at(name, shape, F32, spot[0])
            spot[0] += -(-int(np.prod(shape[1:])) * 4 // 32) * 32
            return t

        mkt_s = early("mkt_s", [P, SQ, 2, NM])
        kt_s = early("kt_s", [P, SQ, P + TS])
        prob_s, mprob_s = early("prob_s", [SR, P + TS]), early("mprob_s", [SR, NM])
        pt_s, ptn_s, mpt_s = early("pt_s", [P, SR]), early("ptn_s", [TS, SR]), early("mpt_s", [P, 2, SR])
        o_s, mo_s = early("o_s", [SR, P]), early("mo_s", [SR, NM])
        assert spot[0] <= y_at + KT * T * 4
        spot = [y_at + (KT + 3) * T * 4]
        k_raw, v_raw = early("k_raw", [P, P + TS]), early("v_raw", [P, T])
        w_raw = [sb(f"w_raw{s}", [P, KT, P]) for s in range(2)]
        w_hi = [sb(f"w_hi{s}", [P, KT, P], F32R) for s in range(2)]
        w_lo = [sb(f"w_lo{s}", [P, KT, P], F32R) for s in range(2)]
        q_st = sb("q_st", [P, NH, TP], F32R)
        mq_st = sb("mq_st", [P, MH, TP], F32R)
        k_hh, k_ll = sb("k_hh", [P, NKV, W + TP], F32R), sb("k_ll", [P, NKV, W + TP], F32R)
        v_st = sb("v_st", [P, 1 + NBLK, NKV, 2 * HD], F32R)
        mk_hh, mk_ll = sb("mk_hh", [P, MH, NM], F32R), sb("mk_ll", [P, MH, NM], F32R)
        mv_st = sb("mv_st", [P, 2, MH, 2 * HD], F32R)
        bias = sb("bias", [P, NH, 2 * W])
        bias_first = sb("bias_first", [P, NH, W])
        att_at = nc.sbuf_base
        prob = sb("prob", [P, NH, 2 * W])
        mprob = sb("mprob", [P, 4, NM])
        pt_hi, pt_lo = sb("pt_hi", [P, 2 * NH, P], F32R), sb("pt_lo", [P, 2 * NH, P], F32R)
        mpt_hi, mpt_lo = sb("mpt_hi", [P, 8, P], F32R), sb("mpt_lo", [P, 8, P], F32R)
        o_nat = at("o_nat", [P, NBLK, D], F32, att_at)
        o_nat_s = at("o_nat_s", [TS, D], F32, att_at + NBLK * D * 4)
        o_t = at("o_t", [P, 2, T], F32, att_at + (NBLK + 1) * D * 4)
        mkv_raw = at("mkv_raw", [P, 4, NM], F32, att_at)
        mkv_nat = at("mkv_nat", [P, 2, 2 * NM], F32, att_at + 4 * NM * 4)
        g_mem = at("g_mem", [P, D], F32, att_at + 8 * NM * 4)
        assert (NBLK + 1) * D * 4 + 2 * T * 4 <= nc.sbuf_base - att_at
        gate_at = nc.sbuf_base
        gate = sb("gate", [P, 5, T])
        cc_t, c_t, g_t = sb("cc_t", [P, T]), sb("c_t", [P, T]), sb("g_t", [P, T])
        x_rows = at("x_rows", [P, 2, D], F32, gate_at)
        x_norm = at("x_norm", [P, 2, D], F32, gate_at + 2 * D * 4)
        assert 4 * D * 4 <= nc.sbuf_base - gate_at
        tanh_t = sb("tanh_t", [P, 2, CW])
        u_buf = sb("u_buf", [P, 3, 2 + TP])
        u_s = sb("u_s", [P, 3, SQ, 2 + ST])
        cwt = sb("cwt", [P, 3, 3])
        g_pre, g_post = sb("g_pre", [P, D]), sb("g_post", [P, D])
        sq_sum, mean, rstd, neg_half = (sb(n, [P, 1]) for n in ("sq_sum", "mean", "rstd", "neg_half"))
        ident = sb("ident", [P, P])
        sink = sb("sink", [P, NH])
        mx, nmx, sums, sexp, den, rden = (sb(n, [P, NH]) for n in ("mx", "nmx", "sums", "sexp", "den", "rden"))
        mmx, nmmx, msums, mrden = (sb(n, [P, 4]) for n in ("mmx", "nmmx", "msums", "mrden"))
        o_half, o_sum = sb("o_half", [P, G, P]), sb("o_sum", [P, G, P])
        mo_half, mo_sum = sb("mo_half", [P, 2 * P]), sb("mo_sum", [P, 2 * P])
        k_nat, v_nat = sb("k_nat", [P, P]), sb("v_nat", [P, P])
        kn_s, vn_s = sb("kn_s", [TS, P]), sb("vn_s", [TS, P])
        tail = sb("tail", [P, 3, 2 + 2 * SQ])
        tail_nat = sb("tail_nat", [2 + 2 * SQ, DC])
        st_c = sb("st_c", [2 * SQ, DC])
        k_c, v_c = sb("k_c", [P, SQ, P]), sb("v_c", [P, SQ, P])
        q_bd = sb("q_bd", [P, SQ, 32])
        mq_bd = sb("mq_bd", [P, SQ, 2, 32])
        bias_s = sb("bias_s", [SR, P + TS])
        sink_s = sb("sink_s", [SR, 1])
        smx, snmx, ssum, ssexp, sden, srden = (sb("s_" + n, [SR, 1]) for n in ("mx", "nmx", "sum", "sexp", "den", "rden"))
        tmx, tnmx, tsum, trden = (sb("t_" + n, [SR, 1]) for n in ("mx", "nmx", "sum", "rden"))
        osel, mosel = sb("osel", [P, G, TS]), sb("mosel", [P, 2, TS])

        pj = [ctx.enter_context(nc.psum_tensor(f"pj{i}", [P, 512], F32)) for i in range(3)]
        pa = [ctx.enter_context(nc.psum_tensor(f"pa{i}", [P, 512], F32)) for i in range(5)]

        const_loaded, mem_g_loaded = sem("const_loaded"), sem("mem_g_loaded")
        x_loaded = [sem(f"x_loaded{s}") for s in range(2)]
        w_loaded = [sem(f"w_loaded{s}") for s in range(2)]
        cache_loaded, memc_loaded = sem("cache_loaded"), sem("memc_loaded")
        zeroed = sem("zeroed")
        w_split = sem("w_split")
        squares, means, rstds, normed = sem("squares"), sem("means"), sem("rstds"), sem("normed")
        x_turned, h_his, h_ready = sem("x_turned"), sem("h_his"), sem("h_ready")
        proj_done, free_act, free_dve = sem("proj_done"), sem("free_act"), sem("free_dve")
        act_half = sem("act_half")
        mkv_evac, mkv_turned, mkv_nat_done, mkv_hi, mkv_ready = (sem(n) for n in (
            "mkv_evac", "mkv_turned", "mkv_nat_done", "mkv_hi", "mkv_ready"))
        cache_turned, cache_out, state_out = sem("cache_turned"), sem("cache_out"), sem("state_out")
        nat_turned, v_his, nat_out = sem("nat_turned"), sem("v_his"), sem("nat_out")
        s_done, s_max, exps, p_ready = sem("s_done"), sem("s_max"), sem("exps"), sem("p_ready")
        p_turned, pt_his, pt_ready, pv_done = sem("p_turned"), sem("pt_his"), sem("pt_ready"), sem("pv_done")
        o_halves, o_taken, y32, y_his, y_ready = (sem(n) for n in ("o_halves", "o_taken", "y32", "y_his", "y_ready"))
        ss_done, ss_max, ss_exp, sp_ready = sem("ss_done"), sem("ss_max"), sem("ss_exp"), sem("sp_ready")
        sp_turned, spt_ready, so_done, so_out, so_turned, so_sel = (sem(n) for n in (
            "sp_turned", "spt_ready", "so_done", "so_out", "so_turned", "so_sel"))
        tail_ready, tail_turned, tail_out = sem("tail_ready"), sem("tail_turned"), sem("tail_out")
        o_turned, o_rows, o_squares, o_means, o_rstds, y_rows = (sem(n) for n in (
            "o_turned", "o_rows", "o_squares", "o_means", "o_rstds", "y_rows"))
        y_stored, s_stored, mkv_stored, last_stored = (sem(n) for n in (
            "y_stored", "s_stored", "mkv_stored", "last_stored"))
        dve_step, act_step, pool_step = sem("dve_step"), sem("act_step"), sem("pool_step")

        pe_past, pool_past, sp_past = sem("pe_past"), sem("pool_past"), sem("sp_past")

        def chain(eng, semaphore, base):
            n = [0]

            def step(ins):
                n[0] += 1
                ins.then_inc(semaphore, 1)
                return n[0]

            def need(token):
                eng.wait_ge(semaphore, base + token)

            return step, need, n

        def chunk_cols(c):
            return slice(c * CW, (c + 1) * CW)

        def xl(q, i):
            return (q * (NL_X // 2) + (1 + i // 2 + 1)) * 16

        block = ctx.enter_context(nc.Block())

        @block.sync
        def _(sp):
            def w_tile(slot, srcs):
                for dst, src in srcs:
                    sp.dma_start(dst, src).then_inc(w_loaded[slot], 16)

            def in_srcs(t):
                name, slot = TILES[t], t % 2
                col = {"K": OFF["K"], "V": OFF["V"], "Z3": OFF["ZM"], "Z4": OFF["ZM"] + P, "M0": OFF["M"],
                       "M1": OFF["M"] + P}.get(name)
                if name[0] == "C":
                    col = OFF[name[:2]] + int(name[2]) * P
                if col is not None:
                    a = w_in[0, :, col:col + P].rearrange("(k p) f -> p k f", p=P)
                    return [(w_raw[slot][:], a)]
                g, base = int(name[1]), OFF[name[0]]
                return [(w_raw[slot][:, :, kv * HD:(kv + 1) * HD],
                         w_in[0, :, base + (kv * G + g) * HD:base + (kv * G + g + 1) * HD].rearrange(
                             "(k p) f -> p k f", p=P)) for kv in range(NKV)]

            def out_srcs(f):
                slot, cols = (NIN + f) % 2, slice(f * P, (f + 1) * P)
                srcs = [(w_raw[slot][:, 0:3, :], w_out[0, 0:DC, cols].rearrange("(k p) f -> p k f", p=P))]
                for kv in range(NKV):
                    r = DC + kv * G * HD
                    srcs.append((w_raw[slot][kv * HD:(kv + 1) * HD, 3:6, :],
                                 w_out[0, r:r + G * HD, cols].rearrange("(k p) f -> p k f", p=HD)))
                srcs.append((w_raw[slot][:, 6:8, :], w_out[0, 2 * DC:D, cols].rearrange("(k p) f -> p k f", p=P)))
                return srcs

            for b in range(2):
                sp.dma_start(x_rows[:, b, :], mem_prompt[0, b * P:(b + 1) * P, :]).then_inc(x_loaded[b], 16)
            sp.dma_start(g_mem[:], mem_g.to_broadcast([P, D])).then_inc(mem_g_loaded, 16)
            sp.dma_start(ident[:], ident_d).then_inc(const_loaded, 16)
            for i in range(PRO_W):
                if i >= 2:
                    sp.wait_ge(w_split, i - 1)
                src = (w_mk if i < 2 else w_mv)[0, :, (i % 2) * P:(i % 2 + 1) * P]
                w_tile(i % 2, [(w_raw[i % 2][:], src.rearrange("(k p) f -> p k f", p=P))])
            sp.dma_start(g_pre[:], pre_g.to_broadcast([P, D])).then_inc(const_loaded, 16)
            sp.dma_start(g_post[:], post_g.to_broadcast([P, D])).then_inc(const_loaded, 16)
            sp.dma_start(bias[:], bias_d).then_inc(const_loaded, 16)
            sp.dma_start(bias_s[:], bias_s_d).then_inc(const_loaded, 16)
            sp.dma_start(sink[:], sinks.to_broadcast([P, NH])).then_inc(const_loaded, 16)
            with nc.allow_non_contiguous_dma(reason="a few hundred single values, once"):
                for j in range(3):
                    sp.dma_start(cwt[:, j, :], conv_w[0, :, j * P:(j + 1) * P].rearrange("w c -> c w")).then_inc(
                        const_loaded, 16)
                sp.wait_ge(zeroed, 1)
                for s in range(SQ):
                    for t in range(ST):
                        sp.dma_start(sink_s[32 * s + t:32 * s + t + ST * (NH - 1) + 1:ST, :],
                                     sinks.rearrange("a h -> h a")).then_inc(const_loaded, 16)
            sp.dma_start(k_s[0, :, 0:W - ST].rearrange("n w k d -> n w (k d)"),
                         cache_k[0, :, ST:W].rearrange("n w k d -> n w (k d)")).then_inc(last_stored, 16)
            sp.dma_start(v_s[0, :, 0:W - ST].rearrange("n w k d -> n w (k d)"),
                         cache_v[0, :, ST:W].rearrange("n w k d -> n w (k d)")).then_inc(last_stored, 16)
            sp.wait_ge(mkv_nat_done, 2)
            sp.dma_start(mk_p[0, 0].rearrange("(t p) h d -> p t (h d)", p=P), mkv_nat[:, :, 0:NM]).then_inc(
                mkv_stored, 16)
            sp.dma_start(mv_p[0, 0].rearrange("(t p) h d -> p t (h d)", p=P), mkv_nat[:, :, NM:2 * NM]).then_inc(
                mkv_stored, 16)

            with sp.Fori(0, NQ) as q:
                def load_x(i, b):
                    if b < NBLK:
                        sp.dma_start(x_rows[:, i % 2, :],
                                     x_prompt[0, bass.ds(q * TP + b * P, P), :]).then_inc(x_loaded[i % 2], 16)
                    else:
                        sp.dma_start(x_rows[0:TS, i % 2, :], x_sample[bass.ds(q * SQ, SQ), :, :].rearrange(
                            "s t d -> (s t) d")).then_inc(x_loaded[i % 2], 16)

                def load_w(t):
                    sp.wait_ge(w_split, q * NW + (PRO_W + t - 1))
                    w_tile(t % 2, in_srcs(t) if t < NIN else out_srcs(t - NIN))

                sp.wait_ge(y_rows, 1 + q * 5)
                sp.sem_inc(sp_past, 1)
                for b in range(2):
                    if b == 0:
                        sp.wait_ge(normed, q * 5 + 2)
                    load_x(b, b)
                load_w(0)
                load_w(1)
                sp.wait_ge(proj_done, q * NC + PRO_W)
                for s in range(SQ):
                    sp.dma_start(k_c[:, s, :], cache_k[0, bass.ds(q * SQ + s, 1)].rearrange(
                        "n w k d -> (n w) (k d)")).then_inc(cache_loaded, 16)
                    sp.dma_start(v_c[:, s, :], cache_v[0, bass.ds(q * SQ + s, 1)].rearrange(
                        "n w k d -> (n w) (k d)")).then_inc(cache_loaded, 16)
                    sp.dma_start(memk_c[:, :, s, :], cache_mk[0, bass.ds(q * SQ + s, 1)].rearrange(
                        "n (t p) h d -> p (n t) (h d)", p=P)).then_inc(memc_loaded, 16)
                    sp.dma_start(memv_c[:, :, s, :], cache_mv[0, bass.ds(q * SQ + s, 1)].rearrange(
                        "n (t p) h d -> p (n t) (h d)", p=P)).then_inc(memc_loaded, 16)
                sp.dma_start(st_c[:], state_conv[0, bass.ds(q * SQ, SQ)].rearrange("n j c -> (n j) c")).then_inc(
                    cache_loaded, 16)
                for b in range(2, NBLK + 1):
                    sp.wait_ge(normed, q * 5 + (2 + b - 1))
                    load_x(b, b)
                for t in range(2, NW):
                    load_w(t)
                    if t == AT_NAT // 2 + 3:
                        sp.wait_ge(nat_out, q + 1)
                        for s in range(SQ):
                            for dst, src in ((k_s, kn_s), (v_s, vn_s)):
                                sp.dma_start(dst[0, bass.ds(q * SQ + s, 1), W - ST:W].rearrange(
                                    "n w k d -> (n w) (k d)"), src[s * ST:(s + 1) * ST, :]).then_inc(s_stored, 16)
                    if t == NIN + 3:
                        sp.wait_ge(y_ready, 1 + (q + 1) * Y_PARTS)
                        load_x(5, 0)
                        load_x(6, 1)
                        sp.wait_ge(tail_out, q + 1)
                        sp.dma_start(conv_s[0, bass.ds(q * SQ, SQ)].rearrange("n j c -> (n j) c"),
                                     tail_nat[2:2 + 2 * SQ, :]).then_inc(s_stored, 16)
                for b in range(NBLK + 1):
                    sp.wait_ge(y_rows, 1 + q * 5 + (b + 1))
                    if b < NBLK:
                        sp.dma_start(y_prompt[0, bass.ds(q * TP + b * P, P), :], o_nat[:, b, :]).then_inc(y_stored, 16)
                    else:
                        sp.dma_start(y_sample[bass.ds(q * SQ, SQ), :, :].rearrange("s t d -> (s t) d"),
                                     o_nat_s[:]).then_inc(y_stored, 16)
                    if b + 2 <= NBLK:
                        load_x(7 + b, b + 2)

            sp.dma_start(conv_p[0, 0], tail_nat[0:2, :]).then_inc(last_stored, 16)
            sp.dma_start(k_p[0, 0].rearrange("w k d -> w (k d)"), k_nat[:]).then_inc(last_stored, 16)
            sp.dma_start(v_p[0, 0].rearrange("w k d -> w (k d)"), v_nat[:]).then_inc(last_stored, 16)
            sp.wait_ge(y_stored, 1 + NQ * 5 * 16)
            sp.wait_ge(s_stored, 1 + NQ * 5 * 16)
            sp.wait_ge(mkv_stored, 2 * 16)
            sp.wait_ge(last_stored, 5 * 16)

        N_CONST = (6 + 3 + SQ * ST) * 16

        @block.gpsimd
        def _(pool):
            load_counts = [0, 0]

            def split_tile(tile_no, first_chunk_after, n_dma, base_w, step, need):
                slot = tile_no % 2
                load_counts[slot] += n_dma
                pool.wait_ge(w_loaded[slot], base_w[slot] + load_counts[slot] * 16)
                if first_chunk_after is not None:
                    pool.wait_ge(proj_done, first_chunk_after)
                pool.sem_inc(pool_past, 1)
                tok = step(pool.tensor_scalar(w_hi[slot][:], w_raw[slot][:], 1.0, 1.0, ALU.mult, ALU.mult))
                need(tok)
                pool.tensor_tensor(w_lo[slot][:], w_raw[slot][:], w_hi[slot][:].bitcast(F32),
                                   ALU.subtract).then_inc(w_split, 1)

            def power(mean_sem, value, out_sem, free_value=None):
                pool.wait_ge(mean_sem, value)
                pool.tensor_tensor(rstd[:], mean[:], neg_half[:], ALU.pow).then_inc(out_sem, 1)

            step, need, n = chain(pool, pool_step, 0)
            need(step(pool.memset(neg_half[:], -0.5)))
            for b in range(2):
                power(means, b + 1, rstds)
            for i in range(PRO_W):
                split_tile(i, None if i < 2 else i - 1, 1, (0, 0), step, need)
            pro_loads = list(load_counts)
            n_pro = n[0]

            n_dmas = [2 if TILES[t][0] == "Q" or TILES[t] in ("Z0", "Z1", "Z2") else 1 for t in range(NIN)] + [4] * NOUT
            per_q = [sum(n_dmas[s::2]) for s in range(2)]
            with pool.Fori(0, NQ) as q:
                step, need, n = chain(pool, pool_step, q * POOL_Q + n_pro)
                load_counts[:] = [0, 0]
                base_w = [(q * per_q[s] + pro_loads[s]) * 16 for s in range(2)]
                for t in range(NW):
                    if t == 2:
                        for b in range(NBLK + 1):
                            power(means, q * 5 + (2 + b + 1), rstds)
                    used = q * NC + (PRO_W + 2 * (t - 1)) if t >= 2 else q * NC + PRO_W - (1 - t)
                    if t < 2:
                        used = q * NC + PRO_W
                    split_tile(t, used, n_dmas[t], base_w, step, need)
                for b in range(NBLK + 1):
                    power(o_means, 1 + q * 5 + (b + 1), o_rstds)
                assert n[0] == POOL_Q, n

        @block.tensor
        def _(pe):
            def mm(out, lhsT, rhs, start, stop):
                return pe.matmul(out, lhsT, rhs, start=start, stop=stop)

            def project(bank, slot, hi, lo, cols, width):
                for k in range(KT):
                    for n, (w, a) in enumerate(((w_hi, hi), (w_hi, lo), (w_lo, hi))):
                        last = mm(pj[bank][:, 0:width], w[slot][:, k, :], a[:, k, cols], k == 0 and n == 0,
                                  k == KT - 1 and n == 2)
                last.then_inc(proj_done, 1)

            def turn_x(b):
                for k in range(KT):
                    last = pe.transpose(pa[2 * (b % 2) + k // 4][:, (k % 4) * P:(k % 4 + 1) * P],
                                        x_norm[:, b % 2, k * P:(k + 1) * P], ident[:])
                last.then_inc(x_turned, 1)

            def alone():
                pe.sem_inc(pe_past, 1)

            pe.wait_ge(const_loaded, N_CONST)
            for b in range(2):
                pe.wait_ge(normed, b + 1)
                turn_x(b)
            for i in range(PRO_W):
                pe.wait_ge(w_split, i + 1)
                if i == 0:
                    pe.wait_ge(h_ready, 2)
                if i == 3:
                    pe.wait_ge(mkv_evac, 1)
                project(i % 3, i % 2, h_hi, h_lo, slice(0, NM), NM)
            for half in range(2):
                for i in range(2):
                    for kt in range(2):
                        if half == 0 and i == 0 and kt == 0:
                            pe.wait_ge(mkv_evac, PRO_W)
                        last = pe.transpose(pa[kt][:, (2 * half + i) * P:(2 * half + i + 1) * P],
                                            mkv_raw[:, 2 * half + i, kt * P:(kt + 1) * P], ident[:])
            last.then_inc(mkv_turned, 1)

            with pe.Fori(0, NQ) as q:
                for b in range(NBLK + 1):
                    pe.wait_ge(normed, q * 5 + (2 + b + 1))
                    if b == 0:
                        pe.wait_ge(o_rows, 1 + q * NOUT)
                        pe.wait_ge(mkv_nat_done, 2)
                    if b >= 2:
                        pe.wait_ge(h_ready, q * 5 + (2 + b - 1))
                    turn_x(b)

                def cache_turn():
                    pe.wait_ge(cache_loaded, (q + 1) * 5 * 16)
                    pe.wait_ge(memc_loaded, (q + 1) * 4 * 16)
                    for s in range(SQ):
                        for p in range(2):
                            for kt in range(2):
                                pe.transpose(pa[2 + s][:, (p * 2 + kt) * P:(p * 2 + kt + 1) * P],
                                             memk_c[:, kt, s, p * P:(p + 1) * P], ident[:])
                    for j in range(3):
                        pe.transpose(pa[1][:, j * 4:(j + 1) * 4], st_c[:, j * P:(j + 1) * P], ident[0:4, 0:4])
                    for s in range(SQ):
                        last = pe.transpose(pa[4][:, s * P:(s + 1) * P], k_c[:, s, :], ident[:])
                    last.then_inc(cache_turned, 1)

                def nat_turn():
                    pe.wait_ge(free_act, 1 + q * FREE_ACT[-1] + FREE_ACT[13])
                    pe.wait_ge(cache_out, q + 1)
                    for b in range(NBLK):
                        pe.transpose(pa[2][:, b * P:(b + 1) * P], v_raw[:, b * P:(b + 1) * P], ident[:])
                    pe.transpose(pa[3][0:TS, 0:P], v_raw[:, TP:T], ident[:])
                    pe.transpose(pa[3][:, P:2 * P], k_raw[:, 0:P], ident[:])
                    pe.transpose(pa[3][0:TS, 2 * P:3 * P], k_raw[:, P:P + TS], ident[:]).then_inc(nat_turned, 1)

                def sample_scores():
                    pe.wait_ge(free_dve, 1 + q * FREE_DVE[-1] + FREE_DVE[11])
                    pe.wait_ge(cache_out, q + 1)
                    pe.wait_ge(state_out, q + 1)
                    for s in range(SQ):
                        mm(pa[0][32 * s:32 * s + 32, 0:P + TS], q_bd[:, s, :], kt_s[:, s, :], True, True)
                    for s in range(SQ):
                        for p in range(2):
                            last = mm(pa[1][32 * s:32 * s + 32, 0:NM], mq_bd[:, s, p, :], mkt_s[:, s, p, :], p == 0,
                                      p == 1)
                    last.then_inc(ss_done, 1)

                def sample_turn():
                    pe.wait_ge(sp_ready, q + 1)
                    alone()
                    pe.transpose(pa[4][:, 0:SR], prob_s[:, 0:P], ident[0:SR, 0:SR])
                    pe.transpose(pa[4][0:TS, SR:2 * SR], prob_s[:, P:P + TS], ident[0:SR, 0:SR])
                    for kt in range(2):
                        last = pe.transpose(pa[4][:, (2 + kt) * SR:(3 + kt) * SR], mprob_s[:, kt * P:(kt + 1) * P],
                                            ident[0:SR, 0:SR])
                    last.then_inc(sp_turned, 1)

                def sample_values():
                    pe.wait_ge(spt_ready, q + 1)
                    pe.wait_ge(nat_out, q + 1)
                    for s in range(SQ):
                        r = slice(32 * s, 32 * s + 32)
                        mm(pa[0][r, 0:P], pt_s[:, r], v_c[:, s, :], True, False)
                        mm(pa[0][r, 0:P], ptn_s[:, r], vn_s[:], False, True)
                    for s in range(SQ):
                        r = slice(32 * s, 32 * s + 32)
                        for kt in range(2):
                            last = mm(pa[1][r, 0:NM], mpt_s[:, kt, r], memv_c[:, kt, s, :], kt == 0, kt == 1)
                    last.then_inc(so_done, 1)

                def sample_back():
                    pe.wait_ge(so_out, q + 1)
                    alone()
                    pe.transpose(pa[4][:, 0:SR], o_s[:], ident[0:SR, 0:SR])
                    for p in range(2):
                        last = pe.transpose(pa[4][:, (1 + p) * SR:(2 + p) * SR], mo_s[:, p * P:(p + 1) * P],
                                            ident[0:SR, 0:SR])
                    last.then_inc(so_turned, 1)

                def scores(i):
                    if i == 0:
                        pe.wait_ge(so_sel, q + 1)
                        pe.wait_ge(v_his, q + 1)
                        pe.wait_ge(nat_out, q + 1)
                    else:
                        pe.wait_ge(o_taken, q * NBLK + i)
                    for h in range(NH):
                        out = pa[h // 2][:, (h % 2) * 2 * W:(h % 2 + 1) * 2 * W]
                        for n, keys in enumerate((k_hh, k_ll)):
                            last = mm(out, q_st[:, h, i * P:(i + 1) * P], keys[:, h // G, i * P:i * P + 2 * W], n == 0,
                                      n == 1)
                    last.then_inc(s_done, 1)
                    gr, p = i // 2, i % 2
                    for hh in range(2):
                        for tb in range(2):
                            at_q = gr * 2 * P + tb * P
                            for n, keys in enumerate((mk_hh, mk_ll)):
                                last = mm(pa[3 + hh][:, tb * NM:(tb + 1) * NM], mq_st[:, 2 * p + hh, at_q:at_q + P],
                                          keys[:, 2 * p + hh, :], n == 0, n == 1)
                    last.then_inc(s_done, 1)

                def turn_probs(i):
                    pe.wait_ge(p_ready, q * 2 * NBLK + (2 * i + 1))
                    for kt in range(2):
                        for h in range(NH):
                            n = kt * NH + h
                            last = pe.transpose(pa[n // 4][:, (n % 4) * P:(n % 4 + 1) * P],
                                                prob[:, h, kt * P:(kt + 1) * P], ident[:])
                    last.then_inc(p_turned, 1)
                    pe.wait_ge(p_ready, q * 2 * NBLK + (2 * i + 2))
                    for kt in range(2):
                        for u in range(4):
                            last = pe.transpose(pa[3 + kt][:, u * P:(u + 1) * P], mprob[:, u, kt * P:(kt + 1) * P],
                                                ident[:])
                    last.then_inc(p_turned, 1)

                def values(i):
                    pe.wait_ge(pt_ready, q * 2 * NBLK + (2 * i + 1))
                    for kv in range(NKV):
                        for kt in range(2):
                            for n, pt in enumerate((pt_hi, pt_lo)):
                                a = kt * NH + kv * G
                                last = mm(pa[kv][:, 0:G * P], v_st[:, i + kt, kv, :], pt[:, a:a + G, :].rearrange(
                                    "p a b -> p (a b)"), kt == 0 and n == 0, kt == 1 and n == 1)
                    pe.wait_ge(pt_ready, q * 2 * NBLK + (2 * i + 2))
                    p = i % 2
                    for hh in range(2):
                        for kt in range(2):
                            for n, pt in enumerate((mpt_hi, mpt_lo)):
                                a = kt * 4 + hh * 2
                                last = mm(pa[2][:, hh * 2 * P:(hh + 1) * 2 * P], mv_st[:, kt, 2 * p + hh, :],
                                          pt[:, a:a + 2, :].rearrange("p a b -> p (a b)"), kt == 0 and n == 0,
                                          kt == 1 and n == 1)
                    last.then_inc(pv_done, 1)

                def tail_turn():
                    pe.wait_ge(tail_ready, q + 1)
                    pe.wait_ge(o_taken, q * NBLK + NBLK)
                    for j in range(3):
                        last = pe.transpose(pa[4][0:2 + 2 * SQ, j * P:(j + 1) * P], tail[:, j, :], ident[:])
                    last.then_inc(tail_turned, 1)

                def out_turn(f):
                    pe.wait_ge(free_act, 1 + q * FREE_ACT[-1] + FREE_ACT[2 * (NIN + f) + 1])
                    if f >= 2:
                        pe.wait_ge(o_rows, 1 + q * NOUT + (f - 1))
                    a = 2 * (f % 2)
                    for b in range(NBLK):
                        pe.transpose(pa[a][:, b * P:(b + 1) * P], o_t[:, f % 2, b * P:(b + 1) * P], ident[:])
                    pe.transpose(pa[a + 1][0:TS, 0:P], o_t[:, f % 2, TP:T], ident[:]).then_inc(o_turned, 1)

                for n in range(NC):
                    t, c = n // 2, n % 2
                    if c == 0:
                        pe.wait_ge(w_split, q * NW + (PRO_W + t + 1))
                    if n == 0:
                        pe.wait_ge(h_ready, q * 5 + (2 + 3))
                    if n == 1:
                        pe.wait_ge(h_ready, q * 5 + (2 + 5))
                    if n == 2 * NIN:
                        pe.wait_ge(y_ready, 1 + (q + 1) * Y_PARTS)
                    if n < 3:
                        if n == 0:
                            pe.wait_ge(free_act, 1 + q * FREE_ACT[-1])
                            pe.wait_ge(free_dve, 1 + q * FREE_DVE[-1])
                    elif freed_by_act(n - 3):
                        pe.wait_ge(free_act, 1 + q * FREE_ACT[-1] + FREE_ACT[n - 3])
                    else:
                        pe.wait_ge(free_dve, 1 + q * FREE_DVE[-1] + FREE_DVE[n - 3])
                    if n < 2 * NIN:
                        project(n % 3, t % 2, h_hi, h_lo, chunk_cols(c), CW)
                    else:
                        project(n % 3, t % 2, y_hi, y_lo, chunk_cols(c), CW)
                    if n == AT_CACHE:
                        cache_turn()
                    if n == AT_NAT:
                        nat_turn()
                    for stage, fn in zip(AT_SAMPLE, (sample_scores, sample_turn, sample_values, sample_back)):
                        if n == stage:
                            fn()
                    for i in range(NBLK):
                        if n == AT_PV[i]:
                            values(i)
                        if n == AT_S[i]:
                            scores(i)
                        if n == AT_T[i]:
                            turn_probs(i)
                    if n == 2 * NIN:
                        tail_turn()
                    f = (n - 2 * NIN) // 2 - 1
                    if f >= 0 and c == 0:
                        out_turn(f)
                out_turn(NOUT - 1)

        @block.scalar
        def _(act):
            def copy(out, in_):
                return act.activation(out, in_, ACT.Copy)

            def square(b, rows, count):
                act.activation(x_norm[0:rows, b % 2, :], x_rows[0:rows, b % 2, :], ACT.Square,
                               accum_out=sq_sum[0:rows, :]).then_inc(squares, 1)

            def h_hi_of(b, rows):
                for half in range(2):
                    last = copy(h_hi[:, 4 * half:4 * half + 4, b * P:b * P + rows],
                                pa[2 * (b % 2) + half][:].rearrange("p (k t) -> p k t", k=4)[:, :, 0:rows])
                last.then_inc(h_his, 1)

            for b in range(2):
                act.wait_ge(x_loaded[b], 16)
                if b == 1:
                    act.wait_ge(means, 1)
                square(b, P, None)
            for b in range(2):
                act.wait_ge(x_turned, b + 1)
                h_hi_of(b, P)
            for i in range(PRO_W):
                act.wait_ge(proj_done, i + 1)
                copy(mkv_raw[:, i, :], pj[i % 3][:, 0:NM]).then_inc(mkv_evac, 1)
            act.wait_ge(mkv_evac, PRO_W)
            for h in range(MH):
                for d in range(2):
                    last = copy(mk_hh[d * HD:(d + 1) * HD, h, :], mkv_raw[(h % 2) * HD:(h % 2 + 1) * HD, h // 2, :])
            last.then_inc(mkv_hi, 1)
            act.wait_ge(mkv_nat_done, 2)
            for kt in range(2):
                last = copy(mv_st[:, kt, :, 0:HD], mkv_nat[:, kt, NM:2 * NM].rearrange("p (h d) -> p h d", h=MH))
            last.then_inc(mkv_hi, 1)

            with act.Fori(0, NQ) as q:
                def sq(b):
                    act.wait_ge(x_loaded[b % 2], xl(q, b))
                    act.wait_ge(means, q * 5 + (2 + b))
                    if b == 0:
                        act.wait_ge(o_means, 1 + q * 5)
                    act.wait_ge(x_turned, q * 5 + (2 + max(b - 1, 0)))
                    square(b, P if b < NBLK else TS, None)

                def hi(b):
                    act.wait_ge(x_turned, q * 5 + (2 + b + 1))
                    h_hi_of(b, P if b < NBLK else TS)

                sq(0)
                for b in range(NBLK):
                    sq(b + 1)
                    hi(b)
                hi(NBLK)

                def evac(n):
                    name, c, ps = role(n), n % 2, pj[n % 3]
                    act.wait_ge(proj_done, q * NC + (PRO_W + n + 1))
                    pc = CW if c == 0 else CW - TS
                    cols = slice(c * CW, c * CW + pc)
                    if name == "K":
                        if n == 0:
                            act.wait_ge(y_ready, 1 + q * Y_PARTS)
                        for kv in range(NKV):
                            for d in range(2):
                                last = copy(k_hh[d * HD:(d + 1) * HD, kv, W + c * CW:W + c * CW + pc],
                                            ps[kv * HD:(kv + 1) * HD, 0:pc])
                        last.then_inc(act_half, 1)
                    elif name[0] in "QM":
                        for a in range(2):
                            h = a * G + int(name[1]) if name[0] == "Q" else 2 * int(name[1]) + a
                            st = q_st if name[0] == "Q" else mq_st
                            last = copy(st[0:HD, h, cols], ps[a * HD:(a + 1) * HD, 0:pc])
                        last.then_inc(act_half, 1)
                    elif name == "V":
                        copy(v_raw[:, chunk_cols(c)], ps[:, 0:CW]).then_inc(free_act, 1)
                    elif name[0] == "Z" or name[:2] == "CZ":
                        prev = max(m for m in range(n) if m % 2 == c and (role(m)[0] == "Z" or role(m)[:2] == "CZ")
                                   ) if n > 15 else None
                        if prev is not None:
                            act.wait_ge(free_dve, 1 + q * FREE_DVE[-1] + FREE_DVE[prev])
                        act.activation(tanh_t[:, c, :], ps[:, 0:CW], ACT.Tanh, scale=0.5).then_inc(act_half, 1)
                    elif name[:2] == "CC":
                        if name != "CC0":
                            act.wait_ge(free_dve, 1 + q * FREE_DVE[-1] + FREE_DVE[n - 5 if c else n - 5])
                        copy(cc_t[:, chunk_cols(c)], ps[:, 0:CW]).then_inc(free_act, 1)
                    elif name[0] == "O":
                        f = int(name[1])
                        if f >= 2:
                            act.wait_ge(o_turned, q * NOUT + (f - 1))
                        copy(o_t[:, f % 2, chunk_cols(c)], ps[:, 0:CW]).then_inc(free_act, 1)

                def caches():
                    act.wait_ge(cache_turned, q + 1)
                    for s in range(SQ):
                        copy(mkt_s[:, s, :, :], pa[2 + s][:].rearrange("p (a m) -> p a m", a=2))
                    copy(kt_s[:, :, 0:P], pa[4][:, 0:SQ * P].rearrange("p (s k) -> p s k", s=SQ)).then_inc(
                        cache_out, 1)

                def v_hi():
                    act.wait_ge(nat_turned, q + 1)
                    for b in range(NBLK):
                        last = copy(v_st[:, 1 + b, :, 0:HD], pa[2][:, b * P:(b + 1) * P].rearrange(
                            "p (v d) -> p v d", v=NKV))
                    last.then_inc(v_his, 1)

                def sample_exp():
                    act.wait_ge(ss_max, q + 1)
                    act.activation(prob_s[:], prob_s[:], ACT.Exp, bias=snmx[:], accum_out=ssum[:])
                    act.activation(ssexp[:], sink_s[:], ACT.Exp, bias=snmx[:])
                    act.activation(mprob_s[:], pa[1][0:SR, 0:NM], ACT.Exp, bias=tnmx[:], scale=SCALE,
                                   accum_out=tsum[:]).then_inc(ss_exp, 1)

                def sample_out():
                    act.wait_ge(so_done, q + 1)
                    copy(o_s[:], pa[0][0:SR, 0:P])
                    copy(mo_s[:], pa[1][0:SR, 0:NM]).then_inc(so_out, 1)

                def exp(i):
                    act.wait_ge(s_max, q * 2 * NBLK + (2 * i + 1))
                    for h in range(NH):
                        act.activation(prob[:, h, :], prob[:, h, :], ACT.Exp, bias=nmx[:, h:h + 1],
                                       accum_out=sums[:, h:h + 1])
                    act.activation(sexp[:], sexp[:], ACT.Exp).then_inc(exps, 1)
                    act.wait_ge(s_max, q * 2 * NBLK + (2 * i + 2))
                    for u in range(4):
                        last = act.activation(mprob[:, u, :], pa[3 + u // 2][:, (u % 2) * NM:(u % 2 + 1) * NM], ACT.Exp,
                                              bias=nmmx[:, u:u + 1], scale=SCALE, accum_out=msums[:, u:u + 1])
                    last.then_inc(exps, 1)

                def pt_hi_of(i):
                    act.wait_ge(p_turned, q * 2 * NBLK + (2 * i + 1))
                    for a in range(3):
                        last = copy(pt_hi[:, 4 * a:4 * a + 4, :], pa[a][:].rearrange("p (a b) -> p a b", a=4))
                    last.then_inc(pt_his, 1)
                    act.wait_ge(p_turned, q * 2 * NBLK + (2 * i + 2))
                    for a in range(2):
                        last = copy(mpt_hi[:, 4 * a:4 * a + 4, :], pa[3 + a][:].rearrange("p (a b) -> p a b", a=4))
                    last.then_inc(pt_his, 1)

                def halves(i):
                    act.wait_ge(pv_done, q * NBLK + (i + 1))
                    for kv in range(NKV):
                        copy(o_half[kv * HD:(kv + 1) * HD, :, :], pa[kv][HD:P, 0:G * P].rearrange(
                            "p (g t) -> p g t", g=G))
                    for hh in range(2):
                        last = copy(mo_half[hh * HD:(hh + 1) * HD, :], pa[2][HD:P, hh * 2 * P:(hh + 1) * 2 * P])
                    last.then_inc(o_halves, 1)

                def y_hi_of(i):
                    act.wait_ge(y32, q * 11 + Y32["a", i])
                    copy(y_hi[:, 3:6, i * P:(i + 1) * P], o_sum[:])
                    gr, p = i // 2, i % 2
                    copy(y_hi[:, 6 + p, gr * 2 * P:(gr + 1) * 2 * P], mo_sum[:]).then_inc(y_his, 1)

                def conv_hi(j):
                    act.wait_ge(y32, q * 11 + Y32["c", j])
                    copy(y_hi[:, j, :], g_t[:]).then_inc(y_his, 1)

                for n in range(NC):
                    evac(n)
                    if n == AT_CACHE:
                        caches()
                    if n == AT_NAT:
                        v_hi()
                    if n == AT_SAMPLE[0]:
                        sample_exp()
                    if n == AT_SAMPLE[2]:
                        sample_out()
                    if n in CONV_END:
                        conv_hi(CONV_END.index(n))
                    for i in range(NBLK):
                        if n == AT_S[i]:
                            exp(i)
                        if n == AT_T[i]:
                            pt_hi_of(i)
                        if n == AT_PV[i]:
                            halves(i)
                            y_hi_of(i)

                for b in range(NBLK + 1):
                    act.wait_ge(o_rows, 1 + (q + 1) * NOUT)
                    if b:
                        act.wait_ge(o_means, 1 + q * 5 + b)
                    rows = P if b < NBLK else TS
                    src = o_nat[:, b, :] if b < NBLK else o_nat_s[:]
                    act.activation(x_norm[0:rows, 0, :], src, ACT.Square, accum_out=sq_sum[0:rows, :]).then_inc(
                        o_squares, 1)

        @block.vector
        def _(dve):
            def sub(out, whole, high):
                return dve.tensor_tensor(out, whole, high.bitcast(F32), ALU.subtract)

            def norm_rows(b, rows, g, count, free):
                dve.wait_ge(squares, count)
                dve.tensor_scalar(mean[0:rows, :], sq_sum[0:rows, :], 1.0 / D, EPS, ALU.mult, ALU.add).then_inc(
                    means, 1)
                dve.wait_ge(rstds, count)
                dve.scalar_tensor_tensor(out=x_norm[0:rows, b % 2, :], in0=x_rows[0:rows, b % 2, :],
                                         scalar=rstd[0:rows, :], in1=g[0:rows, :], op0=ALU.mult,
                                         op1=ALU.mult).then_inc(normed, 1)

            def h_lo_of(b, rows):
                for half in range(2):
                    a, cols = slice(4 * half, 4 * half + 4), slice(b * P, b * P + rows)
                    last = sub(h_lo[:, a, cols], pa[2 * (b % 2) + half][:].rearrange(
                        "p (k t) -> p k t", k=4)[:, :, 0:rows], h_hi[:, a, cols])
                last.then_inc(h_ready, 1)

            for started in (y_rows, o_rows, free_act, free_dve, o_means, y_ready, y_stored, s_stored):
                dve.sem_inc(started, 1)
            dve.memset(sink_s[:], 0.0)
            dve.memset(mean[:], 1.0)
            for z in (k_hh[:, :, 0:W], k_ll[:, :, 0:W], v_st[:, 0, :, :]):
                dve.memset(z.bitcast(F32), 0.0)
            dve.memset(u_buf[:, :, 0:2], 0.0)
            dve.memset(q_bd[:], 0.0)
            dve.memset(mq_bd[:], 0.0)
            dve.memset(bias_first[:], NEG).then_inc(zeroed, 1)
            dve.wait_ge(zeroed, 1)
            step, need, n_ = chain(dve, dve_step, 0)
            dve.wait_ge(mem_g_loaded, 16)
            for b in range(2):
                norm_rows(b, P, g_mem, b + 1, None)
            for b in range(2):
                dve.wait_ge(h_his, b + 1)
                h_lo_of(b, P)
            dve.wait_ge(mkv_hi, 1)
            for h in range(MH):
                src = mkv_raw[(h % 2) * HD:(h % 2 + 1) * HD, h // 2, :]
                r = slice((h % 2) * HD, (h % 2 + 1) * HD)
                for d in range(2):
                    last = sub(mk_ll[d * HD:(d + 1) * HD, h, :], src, mk_hh[r, h, :])
            dve.wait_ge(mkv_turned, 1)
            for kt in range(2):
                dve.tensor_copy(mkv_nat[:, kt, :], pa[kt][:]).then_inc(mkv_nat_done, 1)
            dve.wait_ge(mkv_hi, 2)
            dve.wait_ge(mkv_nat_done, 2)
            for kt in range(2):
                last = sub(mv_st[:, kt, :, HD:2 * HD], mkv_nat[:, kt, NM:2 * NM].rearrange("p (h d) -> p h d", h=MH),
                           mv_st[:, kt, :, 0:HD])
            last.then_inc(mkv_ready, 1)
            dve.wait_ge(const_loaded, N_CONST)

            with dve.Fori(0, NQ) as q:
                step, need, n_ = chain(dve, dve_step, q * DVE_Q)

                for b in range(NBLK + 2):
                    if b <= NBLK:
                        norm_rows(b, P if b < NBLK else TS, g_pre, q * 5 + (2 + b + 1), None)
                    if b >= 1:
                        dve.wait_ge(h_his, q * 5 + (2 + b))
                        h_lo_of(b - 1, P if b - 1 < NBLK else TS)

                def evac(n):
                    name, c, ps = role(n), n % 2, pj[n % 3]
                    pc = CW if c == 0 else CW - TS
                    cols = slice(c * CW, c * CW + pc)
                    if freed_by_act(n):
                        return
                    if name[:2] in ("CH", "CB"):
                        dve.wait_ge(proj_done, q * NC + (PRO_W + n + 1))
                    else:
                        dve.wait_ge(act_half, q * HALF_Q + HALF[n])
                    if name == "K":
                        for kv in range(NKV):
                            for d in range(2):
                                kc = slice(W + c * CW, W + c * CW + pc)
                                r = slice(d * HD, (d + 1) * HD)
                                last = sub(k_ll[r, kv, kc], ps[kv * HD:(kv + 1) * HD, 0:pc], k_hh[r, kv, kc])
                        if c == 1:
                            dve.tensor_copy(k_raw[:], ps[:, CW - TS - P:CW])
                            for s in range(SQ):
                                last = dve.tensor_copy(kt_s[:, s, P:P + TS], ps[:, pc:CW])
                    elif name[0] in "QM":
                        for a in range(2):
                            r = slice(a * HD, (a + 1) * HD)
                            h = a * G + int(name[1]) if name[0] == "Q" else 2 * int(name[1]) + a
                            st = q_st if name[0] == "Q" else mq_st
                            last = sub(st[HD:P, h, cols], ps[r, 0:pc], st[0:HD, h, cols])
                            if c == 1:
                                new = ps[r, pc:CW].rearrange("p (s t) -> p s t", s=SQ)
                                dst = (q_bd[r, :, h * ST:(h + 1) * ST] if name[0] == "Q" else
                                       mq_bd[r, :, int(name[1]), h * ST:(h + 1) * ST])
                                last = dve.tensor_copy(dst, new)
                    elif name[0] == "Z":
                        last = dve.scalar_tensor_tensor(out=gate[:, int(name[1]), chunk_cols(c)], in0=tanh_t[:, c, :],
                                                        scalar=1.0, in1=ps[:, 0:CW], op0=ALU.add, op1=ALU.mult)
                    elif name[:2] == "CH":
                        j = int(name[2])
                        dve.wait_ge(free_act, 1 + q * FREE_ACT[-1] + FREE_ACT[n])
                        last = dve.tensor_tensor(u_buf[:, j, 2 + c * CW:2 + c * CW + pc], ps[:, 0:pc], cc_t[:, cols],
                                                 ALU.mult)
                        if c == 1:
                            last = dve.tensor_tensor(u_s[:, j, :, 2:2 + ST], ps[:, pc:CW].rearrange(
                                "p (s t) -> p s t", s=SQ), cc_t[:, TP:T].rearrange("p (s t) -> p s t", s=SQ), ALU.mult)
                    elif name[:2] == "CB":
                        need(taps[-1])
                        last = dve.tensor_tensor(c_t[:, chunk_cols(c)], ps[:, 0:CW], c_t[:, chunk_cols(c)], ALU.mult)
                    else:
                        last = dve.scalar_tensor_tensor(out=g_t[:, chunk_cols(c)], in0=tanh_t[:, c, :], scalar=1.0,
                                                        in1=ps[:, 0:CW], op0=ALU.add, op1=ALU.mult)
                    last.then_inc(free_dve, 1)

                taps = []

                def conv(j):
                    dve.wait_ge(free_dve, 1 + q * FREE_DVE[-1] + FREE_DVE[CH_END[j]])
                    for tap in range(3):
                        for out, src in ((c_t[:, 0:TP], u_buf[:, j, tap:tap + TP]),
                                         (c_t[:, TP:T].rearrange("p (s t) -> p s t", s=SQ),
                                          u_s[:, j, :, tap:tap + ST])):
                            w = cwt[:, j, tap:tap + 1]
                            if tap == 0:
                                tok = step(dve.tensor_scalar(out, src, w, None, ALU.mult))
                            else:
                                tok = step(dve.scalar_tensor_tensor(out=out, in0=src, scalar=w, in1=out, op0=ALU.mult,
                                                                    op1=ALU.add))
                        if tap < 2:
                            need(tok)
                    taps.append(tok)
                    dve.tensor_copy(tail[:, j, 0:2], u_buf[:, j, TP:TP + 2])
                    last = dve.tensor_copy(tail[:, j, 2:2 + 2 * SQ].rearrange("p (s t) -> p s t", s=SQ),
                                           u_s[:, j, :, ST:ST + 2])
                    tok = step(last)
                    if j == 2:
                        need(tok)
                        dve.tensor_copy(u_buf[:, :, 0:2], u_buf[:, :, TP:TP + 2]).then_inc(tail_ready, 1)

                def conv_y(j):
                    dve.wait_ge(free_dve, 1 + q * FREE_DVE[-1] + FREE_DVE[CONV_END[j]])
                    dve.scalar_tensor_tensor(out=g_t[:], in0=g_t[:], scalar=0.5, in1=c_t[:], op0=ALU.mult,
                                             op1=ALU.mult).then_inc(y32, 1)

                def conv_lo(j):
                    dve.wait_ge(y_his, q * 7 + YHI["c", j])
                    sub(y_lo[:, j, :], g_t[:], y_hi[:, j, :]).then_inc(y_ready, 1)

                def states():
                    dve.wait_ge(cache_turned, q + 1)
                    dve.tensor_copy(u_s[:, :, :, 0:2], pa[1][:, 0:3 * 2 * SQ].rearrange(
                        "p (j s t) -> p j s t", j=3, s=SQ)).then_inc(state_out, 1)

                def naturals():
                    dve.wait_ge(nat_turned, q + 1)
                    dve.wait_ge(s_stored, 1 + q * 5 * 16)
                    dve.tensor_copy(vn_s[:], pa[3][0:TS, 0:P])
                    dve.tensor_copy(k_nat[:], pa[3][:, P:2 * P])
                    dve.tensor_copy(kn_s[:], pa[3][0:TS, 2 * P:3 * P])
                    dve.wait_ge(v_his, q + 1)
                    for b in range(NBLK):
                        sub(v_st[:, 1 + b, :, HD:2 * HD], pa[2][:, b * P:(b + 1) * P].rearrange(
                            "p (v d) -> p v d", v=NKV), v_st[:, 1 + b, :, 0:HD])
                    dve.tensor_copy(v_nat[:], pa[2][:, (NBLK - 1) * P:NBLK * P]).then_inc(nat_out, 1)

                def sample_max():
                    dve.wait_ge(ss_done, q + 1)
                    need(step(dve.scalar_tensor_tensor(out=prob_s[:], in0=pa[0][0:SR, 0:P + TS], scalar=SCALE,
                                                       in1=bias_s[:], op0=ALU.mult, op1=ALU.add)))
                    a = step(dve.tensor_reduce(smx[:], prob_s[:], AX.X, ALU.max))
                    b = step(dve.tensor_reduce(tmx[:], pa[1][0:SR, 0:NM], AX.X, ALU.max))
                    need(b)
                    need(step(dve.tensor_tensor(smx[:], smx[:], sink_s[:], ALU.max)))
                    dve.tensor_scalar(snmx[:], smx[:], -1.0, None, ALU.mult)
                    dve.tensor_scalar(tnmx[:], tmx[:], -SCALE, None, ALU.mult).then_inc(ss_max, 1)

                def sample_norm():
                    dve.wait_ge(ss_exp, q + 1)
                    need(step(dve.tensor_tensor(sden[:], ssum[:], ssexp[:], ALU.add)))
                    step(dve.reciprocal(srden[:], sden[:]))
                    need(step(dve.reciprocal(trden[:], tsum[:])))
                    dve.tensor_scalar(prob_s[:], prob_s[:], srden[:], None, ALU.mult)
                    dve.tensor_scalar(mprob_s[:], mprob_s[:], trden[:], None, ALU.mult).then_inc(sp_ready, 1)

                def sample_pt():
                    dve.wait_ge(sp_turned, q + 1)
                    dve.tensor_copy(pt_s[:], pa[4][:, 0:SR])
                    dve.tensor_copy(ptn_s[:], pa[4][0:TS, SR:2 * SR])
                    dve.tensor_copy(mpt_s[:], pa[4][:, 2 * SR:4 * SR].rearrange("p (k r) -> p k r", k=2)).then_inc(
                        spt_ready, 1)

                def sample_select():
                    dve.wait_ge(so_turned, q + 1)
                    for kv in range(NKV):
                        r = slice(kv * HD, (kv + 1) * HD)
                        for s in range(SQ):
                            a = s * 32 + kv * G * ST
                            dve.tensor_copy(osel[r, :, s * ST:(s + 1) * ST], pa[4][r, a:a + G * ST].rearrange(
                                "p (g t) -> p g t", g=G))
                    for hh in range(2):
                        r = slice(hh * HD, (hh + 1) * HD)
                        for p in range(2):
                            a = (1 + p) * SR + (2 * p + hh) * ST
                            last = dve.tensor_copy(mosel[r, p, :].rearrange("p (s t) -> p s t", s=SQ), pa[4][
                                r, a:a + SR].rearrange("p (s t) -> p s t", s=SQ)[:, :, 0:ST])
                    last.then_inc(so_sel, 1)

                def sample_y():
                    dve.wait_ge(so_sel, q + 1)
                    dve.wait_ge(free_dve, 1 + q * FREE_DVE[-1] + FREE_DVE[23])
                    step(dve.scalar_tensor_tensor(out=osel[:], in0=osel[:], scalar=0.5, in1=gate[:, 0:3, TP:T],
                                                  op0=ALU.mult, op1=ALU.mult))
                    need(step(dve.scalar_tensor_tensor(out=mosel[:], in0=mosel[:], scalar=0.5, in1=gate[:, 3:5, TP:T],
                                                       op0=ALU.mult, op1=ALU.mult)))
                    step(dve.tensor_copy(y_hi[:, 3:6, TP:T], osel[:]))
                    need(step(dve.tensor_copy(y_hi[:, 6:8, TP:T], mosel[:])))
                    sub(y_lo[:, 3:6, TP:T], osel[:], y_hi[:, 3:6, TP:T])
                    sub(y_lo[:, 6:8, TP:T], mosel[:], y_hi[:, 6:8, TP:T]).then_inc(y_ready, 1)

                def soft_max(i):
                    dve.wait_ge(s_done, q * 2 * NBLK + (2 * i + 1))
                    if i == 0:
                        dve.wait_ge(y_stored, 1 + q * 5 * 16)
                        dve.wait_ge(mkv_stored, 32)
                    for a in range(3):
                        ps = pa[a][:].rearrange("p (h k) -> p h k", h=2)
                        hs = slice(2 * a, 2 * a + 2)
                        if i == 0:
                            dve.scalar_tensor_tensor(out=prob[:, hs, 0:W], in0=ps[:, :, 0:W], scalar=SCALE,
                                                     in1=bias_first[:, hs, :], op0=ALU.mult, op1=ALU.add)
                            last = dve.scalar_tensor_tensor(out=prob[:, hs, W:2 * W], in0=ps[:, :, W:2 * W],
                                                            scalar=SCALE, in1=bias[:, hs, W:2 * W], op0=ALU.mult,
                                                            op1=ALU.add)
                        else:
                            last = dve.scalar_tensor_tensor(out=prob[:, hs, :], in0=ps, scalar=SCALE, in1=bias[:, hs, :],
                                                            op0=ALU.mult, op1=ALU.add)
                    tok = step(last)
                    dve.wait_ge(s_done, q * 2 * NBLK + (2 * i + 2))
                    for hh in range(2):
                        last = dve.tensor_reduce(mmx[:, 2 * hh:2 * hh + 2], pa[3 + hh][:].rearrange(
                            "p (t k) -> p t k", t=2), AX.X, ALU.max)
                    mtok = step(last)
                    need(tok)
                    tok = step(dve.tensor_reduce(mx[:], prob[:], AX.X, ALU.max))
                    need(tok)
                    need(step(dve.tensor_tensor(mx[:], mx[:], sink[:], ALU.max)))
                    dve.tensor_scalar(nmx[:], mx[:], -1.0, None, ALU.mult)
                    dve.tensor_tensor(sexp[:], sink[:], mx[:], ALU.subtract).then_inc(s_max, 1)
                    dve.tensor_scalar(nmmx[:], mmx[:], -SCALE, None, ALU.mult).then_inc(s_max, 1)
                    if i == 0:
                        dve.tensor_copy(bias_first[:], bias[:, :, 0:W])

                def soft_norm(i):
                    dve.wait_ge(exps, q * 2 * NBLK + (2 * i + 1))
                    need(step(dve.tensor_tensor(den[:], sums[:], sexp[:], ALU.add)))
                    need(step(dve.reciprocal(rden[:], den[:])))
                    for h in range(NH):
                        last = dve.tensor_scalar(prob[:, h, :], prob[:, h, :], rden[:, h:h + 1], None, ALU.mult)
                    last.then_inc(p_ready, 1)
                    dve.wait_ge(exps, q * 2 * NBLK + (2 * i + 2))
                    need(step(dve.reciprocal(mrden[:], msums[:])))
                    for u in range(4):
                        last = dve.tensor_scalar(mprob[:, u, :], mprob[:, u, :], mrden[:, u:u + 1], None, ALU.mult)
                    last.then_inc(p_ready, 1)

                def pt_lo_of(i):
                    dve.wait_ge(pt_his, q * 2 * NBLK + (2 * i + 1))
                    for a in range(3):
                        s = slice(4 * a, 4 * a + 4)
                        last = sub(pt_lo[:, s, :], pa[a][:].rearrange("p (a b) -> p a b", a=4), pt_hi[:, s, :])
                    last.then_inc(pt_ready, 1)
                    dve.wait_ge(pt_his, q * 2 * NBLK + (2 * i + 2))
                    for a in range(2):
                        s = slice(4 * a, 4 * a + 4)
                        last = sub(mpt_lo[:, s, :], pa[3 + a][:].rearrange("p (a b) -> p a b", a=4), mpt_hi[:, s, :])
                    last.then_inc(pt_ready, 1)

                def attn_y(i):
                    gr, p = i // 2, i % 2
                    dve.wait_ge(o_halves, q * NBLK + (i + 1))
                    for kv in range(NKV):
                        r = slice(kv * HD, (kv + 1) * HD)
                        tok = step(dve.tensor_tensor(o_sum[r, :, :], pa[kv][0:HD, 0:G * P].rearrange(
                            "p (g t) -> p g t", g=G), o_half[r, :, :], ALU.add))
                    for hh in range(2):
                        r = slice(hh * HD, (hh + 1) * HD)
                        last = dve.tensor_tensor(mo_sum[r, :], pa[2][0:HD, hh * 2 * P:(hh + 1) * 2 * P], mo_half[r, :],
                                                 ALU.add)
                    last.then_inc(o_taken, 1)
                    need(tok)
                    dve.scalar_tensor_tensor(out=o_sum[:], in0=o_sum[:], scalar=0.5, in1=gate[:, 0:3, i * P:(i + 1) * P],
                                             op0=ALU.mult, op1=ALU.mult).then_inc(y32, 1)
                    dve.wait_ge(o_taken, q * NBLK + (i + 1))
                    dve.scalar_tensor_tensor(out=mo_sum[:], in0=mo_sum[:], scalar=0.5, in1=gate[
                        :, 3 + p, gr * 2 * P:(gr + 1) * 2 * P], op0=ALU.mult, op1=ALU.mult).then_inc(y32, 1)

                def attn_lo(i):
                    gr, p = i // 2, i % 2
                    dve.wait_ge(y_his, q * 7 + YHI["a", i])
                    cols, mcols = slice(i * P, (i + 1) * P), slice(gr * 2 * P, (gr + 1) * 2 * P)
                    sub(y_lo[:, 3:6, cols], o_sum[:], y_hi[:, 3:6, cols])
                    sub(y_lo[:, 6 + p, mcols], mo_sum[:], y_hi[:, 6 + p, mcols]).then_inc(y_ready, 1)

                def carry():
                    for t in (k_hh, k_ll):
                        dve.tensor_copy(t[:, :, 0:W].bitcast(F32) if False else t[:, :, 0:W], t[:, :, TP:TP + W])
                    dve.tensor_copy(v_st[:, 0, :, :], v_st[:, NBLK, :, :]).then_inc(y_ready, 1)

                def out_rows(f):
                    dve.wait_ge(o_turned, q * NOUT + (f + 1))
                    a, cols = 2 * (f % 2), slice(f * P, (f + 1) * P)
                    dve.tensor_copy(o_nat[:, :, cols], pa[a][:].rearrange("p (b c) -> p b c", b=NBLK))
                    dve.tensor_copy(o_nat_s[:, cols], pa[a + 1][0:TS, 0:P]).then_inc(o_rows, 1)

                for n in range(NC):
                    evac(n)
                    for j in range(3):
                        if n == CH_END[j]:
                            conv(j)
                        if n == CONV_END[j]:
                            conv_y(j)
                            conv_lo(j)
                    if n == AT_CACHE:
                        states()
                    if n == AT_NAT:
                        naturals()
                    if n == AT_SAMPLE[0]:
                        sample_max()
                    if n == AT_SAMPLE[0] + 1:
                        sample_norm()
                    if n == AT_SAMPLE[1]:
                        sample_pt()
                    if n == AT_SAMPLE[3]:
                        sample_select()
                    if n == 23:
                        sample_y()
                    for i in range(NBLK):
                        if n == AT_S[i]:
                            soft_max(i)
                        if n == AT_S[i] + 1:
                            soft_norm(i)
                        if n == AT_T[i]:
                            pt_lo_of(i)
                        if n == AT_PV[i]:
                            attn_y(i)
                            attn_lo(i)
                    if n == 2 * NIN - 1:
                        carry()
                    if n == 2 * NIN:
                        dve.wait_ge(tail_turned, q + 1)
                        dve.tensor_copy(tail_nat[:], pa[4][0:2 + 2 * SQ, 0:DC]).then_inc(tail_out, 1)
                    f = (n - 2 * NIN) // 2 - 1
                    if f >= 0 and n % 2 == 0:
                        out_rows(f)
                out_rows(NOUT - 1)

                for b in range(NBLK + 1):
                    rows = P if b < NBLK else TS
                    o = o_nat[:, b, :] if b < NBLK else o_nat_s[:]
                    dve.wait_ge(o_squares, q * 5 + (b + 1))
                    dve.tensor_scalar(mean[0:rows, :], sq_sum[0:rows, :], 1.0 / D, EPS, ALU.mult, ALU.add).then_inc(
                        o_means, 1)
                    dve.wait_ge(o_rstds, q * 5 + (b + 1))
                    tok = step(dve.scalar_tensor_tensor(out=o, in0=o, scalar=rstd[0:rows, :], in1=g_post[0:rows, :],
                                                        op0=ALU.mult, op1=ALU.mult))
                    dve.wait_ge(x_loaded[(5 + b) % 2], xl(q, 5 + b))
                    need(tok)
                    dve.tensor_tensor(o, o, x_rows[0:rows, (5 + b) % 2, :], ALU.add).then_inc(y_rows, 1)
                assert n_[0] == DVE_Q, n_


CH_END = [2 * TILES.index(f"CH{j}") + 1 for j in range(3)]
CONV_END = [2 * TILES.index(f"CZ{j}") + 1 for j in range(3)]


def _order():
    y32, yhi, a, b = {}, {}, 0, 0
    for n in range(NC):
        for j in range(3):
            if n == CONV_END[j]:
                a, b = a + 1, b + 1
                y32["c", j], yhi["c", j] = a, b
        for i in range(NBLK):
            if n == AT_PV[i]:
                a, b = a + 2, b + 1
                y32["a", i], yhi["a", i] = a, b
    return y32, yhi


Y32, YHI = _order()
HALF, _n = {}, 0
for _c in range(2 * NIN):
    if not freed_by_act(_c) and role(_c)[:2] not in ("CH", "CB"):
        _n += 1
        HALF[_c] = _n
HALF_Q = _n


def constants():
    slopes = np.power(np.float32(2.0), -8.0 * np.arange(1, NH + 1, dtype=np.float32) / NH).astype(np.float32)

    def table(dist, valid):
        b = -(slopes[:, None, None] * np.abs(dist).astype(np.float32)[None])
        return np.where(valid[None], b, np.float32(NEG)).astype(np.float32)

    i, c = np.arange(W)[:, None], np.arange(2 * W)[None]
    dist = i + W - c
    bias = table(dist, (dist >= 0) & (dist < W)).transpose(1, 0, 2)
    bias_s = np.zeros((32 * SQ, P + TS), np.float32)
    t = np.arange(ST)[:, None]
    for s in range(SQ):
        old = W + t - np.arange(W)[None]
        new = t - np.arange(TS)[None] % ST
        d = np.concatenate([old, new], 1)
        own = np.concatenate([np.ones((1, W), bool), np.arange(TS)[None] // ST == s], 1)
        bias_s[32 * s:32 * s + NH * ST] = table(d, (d >= 0) & (d < W) & own).reshape(NH * ST, P + TS)
    return {"ident": np.eye(P, dtype=np.float32), "bias": np.ascontiguousarray(bias), "bias_s": bias_s}


_INS = ["x_prompt", "x_sample", "mem_prompt", "state_conv", "cache_swa_k", "cache_swa_v", "cache_mem_k", "cache_mem_v",
        "pre_norm_g", "post_norm_g", "w_in", "conv_w", "attn_sinks", "mem_norm_g", "w_mem_k", "w_mem_v", "w_out"]
_OUTS = [(1, 2048, 1024), (8, 4, 1024), (1, 1, 2, 384), (1, 1, 128, 2, 64), (1, 1, 128, 2, 64), (1, 1, 256, 4, 64),
         (1, 1, 256, 4, 64), (1, 8, 2, 384), (1, 8, 128, 2, 64), (1, 8, 128, 2, 64)]


def kernel(**inputs):
    import concourse.bacc as bacc
    from concourse.bass_utils import run_bass_kernel_spmd

    nc = bacc.Bacc("TRN2", target_bir_lowering=False, num_devices=1, dynamic_dma_scratch_size=1024)
    arrays, args = {}, []
    given = {name: np.ascontiguousarray(inputs[name]) for name in _INS}
    for name, a in list(given.items()) + list(constants().items()):
        arrays[f"in_{name}"] = a
        args.append(nc.dram_tensor(f"in_{name}", a.shape, mybir.dt.from_np(a.dtype), kind="ExternalInput").ap())
    for i, shape in enumerate(_OUTS):
        args.append(nc.dram_tensor(f"out_{i}", shape, F32, kind="ExternalOutput").ap())
    layer(nc, *args)
    r = run_bass_kernel_spmd(nc, [arrays], core_ids=[0])
    return tuple(r.results[0][f"out_{i}"] for i in range(len(_OUTS)))
```

```python
from contextlib import ExitStack

import concourse.bass as bass
import numpy as np
from concourse import mybir

F32 = mybir.dt.float32
F32R = mybir.dt.float32r
ALU = mybir.AluOpType
ACT = mybir.ActivationFunctionType
AX = mybir.AxisListType

P = 128
D = 1024
KT = D // P
HD = 64
NQ = 4
TP = 512
NBLK = TP // P
SQ = 2
ST = 4
TS = SQ * ST
T = TP + TS
CW = T // 2
NH, NKV, G = 6, 2, 3
MH = 4
NM = 256
W = 128
DC = 384
EPS = 1e-6
SCALE = HD ** -0.5
NEG = -1e30

TILES = ["K", "M0", "M1", "Q0", "Q1", "Q2", "V", "Z3", "Z0", "Z1", "Z2", "Z4"]
for _j in range(3):
    TILES += [f"CC{_j}", f"CH{_j}", f"CB{_j}", f"CZ{_j}"]
NIN = len(TILES)
NOUT = D // P
NW = NIN + NOUT
NC = 2 * NW
OFF = {"CB": 0, "CC": DC, "CH": 2 * DC, "CZ": 3 * DC, "Q": 4 * DC, "K": 5 * DC, "V": 5 * DC + P, "Z": 5 * DC + 2 * P,
       "M": 6 * DC + 2 * P, "ZM": 6 * DC + 2 * P + NM}

AT_CACHE, AT_NAT = 7, 15
AT_SAMPLE = [13, 16, 17, 18]
AT_S = [19 + 7 * i for i in range(NBLK)]
AT_T = [23 + 7 * i for i in range(NBLK)]
AT_PV = [25 + 7 * i for i in range(NBLK)]
AT_NORM = [49, 50, 52, 54, 56]
AT_TURN = [51, 53, 55, 57, 59]


def role(n):
    return TILES[n // 2] if n < 2 * NIN else f"O{n // 2 - NIN}"


def freed_by_act(n):
    return role(n)[0] in "VO" or role(n)[:2] == "CC"


FREE_ACT = [sum(freed_by_act(m) for m in range(n + 1)) for n in range(NC)]
FREE_DVE = [n + 1 - FREE_ACT[n] for n in range(NC)]

Y_PARTS = 3 + NBLK + 1 + 1
NX = NBLK + 1
PRO_W = 4
DVE_Q, POOL_Q = 69, NW


def layer(nc, x_prompt, x_sample, mem_prompt, state_conv, cache_k, cache_v, cache_mk, cache_mv, pre_g, post_g, w_in,
          conv_w, sinks, mem_g, w_mk, w_mv, w_out, ident_d, bias_d, bias_s_d, y_prompt, y_sample, conv_p, k_p, v_p,
          mk_p, mv_p, conv_s, k_s, v_s):
    with ExitStack() as ctx:
        def sb(name, shape, dt=F32):
            return ctx.enter_context(nc.sbuf_tensor(name, shape, dt))

        def at(name, shape, dt, offset):
            return nc.alloc_sbuf_tensor_at(name, shape, dt, offset=offset)

        def sem(name):
            return ctx.enter_context(nc.semaphore(name))

        h_hi, h_lo = sb("h_hi", [P, KT, T], F32R), sb("h_lo", [P, KT, T], F32R)
        y_at = nc.sbuf_base
        y_hi, y_lo = sb("y_hi", [P, KT, T], F32R), sb("y_lo", [P, KT, T], F32R)
        memk_c = at("memk_c", [P, 2, SQ, NM], F32, y_at)
        memv_c = at("memv_c", [P, 2, SQ, NM], F32, y_at + KT * T * 4)
        SR = 32 * SQ
        spot = [y_at + 3 * T * 4]

        def early(name, shape):
            t = at(name, shape, F32, spot[0])
            spot[0] += -(-int(np.prod(shape[1:])) * 4 // 32) * 32
            return t

        mkt_s = early("mkt_s", [P, SQ, 2, NM])
        kt_s = early("kt_s", [P, SQ, P + TS])
        prob_s, mprob_s = early("prob_s", [SR, P + TS]), early("mprob_s", [SR, NM])
        pt_s, ptn_s, mpt_s = early("pt_s", [P, SR]), early("ptn_s", [TS, SR]), early("mpt_s", [P, 2, SR])
        o_s, mo_s = early("o_s", [SR, P]), early("mo_s", [SR, NM])
        assert spot[0] <= y_at + KT * T * 4
        spot = [y_at + (KT + 3) * T * 4]
        k_raw, v_raw = early("k_raw", [P, P + TS]), early("v_raw", [P, T])
        w_raw = [sb(f"w_raw{s}", [P, KT, P]) for s in range(2)]
        w_hi = [sb(f"w_hi{s}", [P, KT, P], F32R) for s in range(2)]
        w_lo = [sb(f"w_lo{s}", [P, KT, P], F32R) for s in range(2)]
        q_st = sb("q_st", [P, NH, TP], F32R)
        mq_st = sb("mq_st", [P, MH, TP], F32R)
        k_hh, k_ll = sb("k_hh", [P, NKV, W + TP], F32R), sb("k_ll", [P, NKV, W + TP], F32R)
        v_st = sb("v_st", [P, 1 + NBLK, NKV, 2 * HD], F32R)
        mk_hh, mk_ll = sb("mk_hh", [P, MH, NM], F32R), sb("mk_ll", [P, MH, NM], F32R)
        mv_st = sb("mv_st", [P, 2, MH, 2 * HD], F32R)
        bias = sb("bias", [P, NH, 2 * W])
        bias_first = sb("bias_first", [P, NH, W])
        att_at = nc.sbuf_base
        prob = sb("prob", [P, NH, 2 * W])
        mprob = sb("mprob", [P, 4, NM])
        pt_hi, pt_lo = sb("pt_hi", [P, 2 * NH, P], F32R), sb("pt_lo", [P, 2 * NH, P], F32R)
        mpt_hi, mpt_lo = sb("mpt_hi", [P, 8, P], F32R), sb("mpt_lo", [P, 8, P], F32R)
        o_nat = at("o_nat", [P, NBLK, D], F32, att_at)
        o_nat_s = at("o_nat_s", [TS, D], F32, att_at + NBLK * D * 4)
        o_t = at("o_t", [P, 2, T], F32, att_at + (NBLK + 1) * D * 4)
        xs_res = at("xs_res", [TS, D], F32, att_at + (NBLK + 1) * D * 4 + 2 * T * 4)
        mkv_raw = at("mkv_raw", [P, 4, NM], F32, att_at)
        mkv_nat = at("mkv_nat", [P, 2, 2 * NM], F32, att_at + 4 * NM * 4)
        g_mem = at("g_mem", [P, D], F32, att_at + 8 * NM * 4)
        assert (NBLK + 2) * D * 4 + 2 * T * 4 <= nc.sbuf_base - att_at
        gate_at = nc.sbuf_base
        gate = sb("gate", [P, 5, T])
        cc_t, c_t, g_t = sb("cc_t", [P, T]), sb("c_t", [P, T]), sb("g_t", [P, T])
        x_rows = at("x_rows", [P, 2, D], F32, gate_at)
        x_norm = at("x_norm", [P, 2, D], F32, gate_at + 2 * D * 4)
        assert 4 * D * 4 <= nc.sbuf_base - gate_at
        residual = [x_rows[:, 1, :], x_norm[:, 1, :], x_rows[:, 0, :], x_norm[:, 0, :], xs_res[:]]
        tanh_at = nc.sbuf_base
        tanh_t = sb("tanh_t", [P, 2, CW])
        squared = at("squared", [P, NBLK, P], F32, tanh_at)
        u_buf = sb("u_buf", [P, 3, 2 + TP])
        u_s = sb("u_s", [P, 3, SQ, 2 + ST])
        cwt = sb("cwt", [P, 3, 3])
        g_pre, g_post = sb("g_pre", [P, D]), sb("g_post", [P, D])
        sq_sum, mean, rstd = (sb(n, [P, 1]) for n in ("sq_sum", "mean", "rstd"))
        o_parts = sb("o_parts", [P, NX, NOUT])
        o_mean, o_rstd, neg_half = (sb(n, [P, NX]) for n in ("o_mean", "o_rstd", "neg_half"))
        ident = sb("ident", [P, P])
        sink = sb("sink", [P, NH])
        mx, nmx, sums, sexp, den, rden = (sb(n, [P, NH]) for n in ("mx", "nmx", "sums", "sexp", "den", "rden"))
        mmx, nmmx, msums, mrden = (sb(n, [P, 4]) for n in ("mmx", "nmmx", "msums", "mrden"))
        o_half, o_sum = sb("o_half", [P, G, P]), sb("o_sum", [P, G, P])
        mo_half, mo_sum = sb("mo_half", [P, 2 * P]), sb("mo_sum", [P, 2 * P])
        k_nat, v_nat = sb("k_nat", [P, P]), sb("v_nat", [P, P])
        kn_s, vn_s = sb("kn_s", [TS, P]), sb("vn_s", [TS, P])
        tail = sb("tail", [P, 3, 2 + 2 * SQ])
        tail_nat = sb("tail_nat", [2 + 2 * SQ, DC])
        st_c = sb("st_c", [2 * SQ, DC])
        k_c, v_c = sb("k_c", [P, SQ, P]), sb("v_c", [P, SQ, P])
        q_bd = sb("q_bd", [P, SQ, 32])
        mq_bd = sb("mq_bd", [P, SQ, 2, 32])
        bias_s = sb("bias_s", [SR, P + TS])
        sink_s = sb("sink_s", [SR, 1])
        smx, snmx, ssum, ssexp, sden, srden = (sb("s_" + n, [SR, 1]) for n in ("mx", "nmx", "sum", "sexp", "den", "rden"))
        tmx, tnmx, tsum, trden = (sb("t_" + n, [SR, 1]) for n in ("mx", "nmx", "sum", "rden"))
        osel, mosel = sb("osel", [P, G, TS]), sb("mosel", [P, 2, TS])

        pj = [ctx.enter_context(nc.psum_tensor(f"pj{i}", [P, 512], F32)) for i in range(3)]
        pa = [ctx.enter_context(nc.psum_tensor(f"pa{i}", [P, 512], F32)) for i in range(5)]

        const_loaded, mem_g_loaded = sem("const_loaded"), sem("mem_g_loaded")
        ident_loaded, g_pre_loaded, res_loaded = sem("ident_loaded"), sem("g_pre_loaded"), sem("res_loaded")
        x_loaded = [sem(f"x_loaded{s}") for s in range(2)]
        w_loaded = [sem(f"w_loaded{s}") for s in range(2)]
        cache_loaded, memc_loaded = sem("cache_loaded"), sem("memc_loaded")
        zeroed = sem("zeroed")
        w_split = sem("w_split")
        squares, means, rstds, normed = sem("squares"), sem("means"), sem("rstds"), sem("normed")
        x_turned, h_his, h_ready = sem("x_turned"), sem("h_his"), sem("h_ready")
        proj_done, free_act, free_dve = sem("proj_done"), sem("free_act"), sem("free_dve")
        act_half = sem("act_half")
        mkv_evac, mkv_turned, mkv_nat_done, mkv_hi, mkv_ready = (sem(n) for n in (
            "mkv_evac", "mkv_turned", "mkv_nat_done", "mkv_hi", "mkv_ready"))
        cache_turned, cache_out, state_out = sem("cache_turned"), sem("cache_out"), sem("state_out")
        nat_turned, v_his, nat_out = sem("nat_turned"), sem("v_his"), sem("nat_out")
        s_done, s_max, exps, p_ready = sem("s_done"), sem("s_max"), sem("exps"), sem("p_ready")
        p_turned, pt_his, pt_ready, pv_done = sem("p_turned"), sem("pt_his"), sem("pt_ready"), sem("pv_done")
        o_halves, o_taken, y32, y_his, y_ready = (sem(n) for n in ("o_halves", "o_taken", "y32", "y_his", "y_ready"))
        ss_done, ss_max, ss_exp, sp_ready = sem("ss_done"), sem("ss_max"), sem("ss_exp"), sem("sp_ready")
        sp_turned, spt_ready, so_done, so_out, so_turned, so_sel = (sem(n) for n in (
            "sp_turned", "spt_ready", "so_done", "so_out", "so_turned", "so_sel"))
        tail_ready, tail_turned, tail_out = sem("tail_ready"), sem("tail_turned"), sem("tail_out")
        o_turned, o_rows, o_squares, o_means, o_rstds, y_rows = (sem(n) for n in (
            "o_turned", "o_rows", "o_squares", "o_means", "o_rstds", "y_rows"))
        y_stored, s_stored, mkv_stored, last_stored = (sem(n) for n in (
            "y_stored", "s_stored", "mkv_stored", "last_stored"))
        dve_step, act_step, pool_step = sem("dve_step"), sem("act_step"), sem("pool_step")

        pe_past, pool_past, sp_past = sem("pe_past"), sem("pool_past"), sem("sp_past")

        def chain(eng, semaphore, base):
            n = [0]

            def step(ins):
                n[0] += 1
                ins.then_inc(semaphore, 1)
                return n[0]

            def need(token):
                eng.wait_ge(semaphore, base + token)

            return step, need, n

        def chunk_cols(c):
            return slice(c * CW, (c + 1) * CW)

        def xl(qx, b):
            return (qx * (3 - b % 2) + (1 + b // 2 + 1)) * 16

        def xn(qx, b):
            return qx * NX + (2 + b + 1)

        block = ctx.enter_context(nc.Block())

        @block.sync
        def _(sp):
            def w_tile(slot, srcs):
                for dst, src in srcs:
                    sp.dma_start(dst, src).then_inc(w_loaded[slot], 16)

            def in_srcs(t):
                name, slot = TILES[t], t % 2
                col = {"K": OFF["K"], "V": OFF["V"], "Z3": OFF["ZM"], "Z4": OFF["ZM"] + P, "M0": OFF["M"],
                       "M1": OFF["M"] + P}.get(name)
                if name[0] == "C":
                    col = OFF[name[:2]] + int(name[2]) * P
                if col is not None:
                    a = w_in[0, :, col:col + P].rearrange("(k p) f -> p k f", p=P)
                    return [(w_raw[slot][:], a)]
                g, base = int(name[1]), OFF[name[0]]
                return [(w_raw[slot][:, :, kv * HD:(kv + 1) * HD],
                         w_in[0, :, base + (kv * G + g) * HD:base + (kv * G + g + 1) * HD].rearrange(
                             "(k p) f -> p k f", p=P)) for kv in range(NKV)]

            def out_srcs(f):
                slot, cols = (NIN + f) % 2, slice(f * P, (f + 1) * P)
                srcs = [(w_raw[slot][:, 0:3, :], w_out[0, 0:DC, cols].rearrange("(k p) f -> p k f", p=P))]
                for kv in range(NKV):
                    r = DC + kv * G * HD
                    srcs.append((w_raw[slot][kv * HD:(kv + 1) * HD, 3:6, :],
                                 w_out[0, r:r + G * HD, cols].rearrange("(k p) f -> p k f", p=HD)))
                srcs.append((w_raw[slot][:, 6:8, :], w_out[0, 2 * DC:D, cols].rearrange("(k p) f -> p k f", p=P)))
                return srcs

            def load_x(qx, b):
                if b < NBLK:
                    sp.dma_start(x_rows[:, b % 2, :],
                                 x_prompt[0, bass.ds(qx * TP + b * P, P), :]).then_inc(x_loaded[b % 2], 16)
                else:
                    sp.dma_start(x_rows[0:TS, b % 2, :], x_sample[bass.ds(qx * SQ, SQ), :, :].rearrange(
                        "s t d -> (s t) d")).then_inc(x_loaded[b % 2], 16)

            sp.dma_start(x_rows[:, 0, :], mem_prompt[0, 0:P, :]).then_inc(x_loaded[0], 16)
            sp.dma_start(x_rows[:, 1, :], mem_prompt[0, P:2 * P, :]).then_inc(x_loaded[1], 16)
            sp.dma_start(g_mem[:], mem_g.to_broadcast([P, D])).then_inc(mem_g_loaded, 16)
            sp.dma_start(ident[:], ident_d).then_inc(ident_loaded, 16)

            def load_mem_w(i):
                src = (w_mk if i < 2 else w_mv)[0, :, (i % 2) * P:(i % 2 + 1) * P]
                w_tile(i % 2, [(w_raw[i % 2][:], src.rearrange("(k p) f -> p k f", p=P))])

            load_mem_w(0)
            load_mem_w(1)
            sp.dma_start(g_pre[:], pre_g.to_broadcast([P, D])).then_inc(g_pre_loaded, 16)
            for b in range(2):
                sp.wait_ge(normed, b + 1)
                load_x(0, b)
            sp.dma_start(sink[:], sinks.to_broadcast([P, NH])).then_inc(const_loaded, 16)
            sp.dma_start(bias[:], bias_d).then_inc(const_loaded, 16)
            sp.dma_start(bias_s[:], bias_s_d).then_inc(const_loaded, 16)
            for i in range(2, PRO_W + 3):
                sp.wait_ge(w_split, i - 1)
                if i < PRO_W:
                    load_mem_w(i)
                else:
                    w_tile(i % 2, in_srcs(i - PRO_W))
                if i < NX:
                    sp.wait_ge(normed, xn(0, i - 2))
                    load_x(0, i)
            sp.dma_start(g_post[:], post_g.to_broadcast([P, D])).then_inc(const_loaded, 16)
            with nc.allow_non_contiguous_dma(reason="a few hundred single values, once"):
                for j in range(3):
                    sp.dma_start(cwt[:, j, :], conv_w[0, :, j * P:(j + 1) * P].rearrange("w c -> c w")).then_inc(
                        const_loaded, 16)
                sp.wait_ge(zeroed, 1)
                for s in range(SQ):
                    for t in range(ST):
                        sp.dma_start(sink_s[32 * s + t:32 * s + t + ST * (NH - 1) + 1:ST, :],
                                     sinks.rearrange("a h -> h a")).then_inc(const_loaded, 16)
            sp.wait_ge(mkv_nat_done, 2)
            sp.dma_start(mk_p[0, 0].rearrange("(t p) h d -> p t (h d)", p=P), mkv_nat[:, :, 0:NM]).then_inc(
                mkv_stored, 16)
            sp.dma_start(mv_p[0, 0].rearrange("(t p) h d -> p t (h d)", p=P), mkv_nat[:, :, NM:2 * NM]).then_inc(
                mkv_stored, 16)
            sp.dma_start(k_s[0, :, 0:W - ST].rearrange("n w k d -> n w (k d)"),
                         cache_k[0, :, ST:W].rearrange("n w k d -> n w (k d)")).then_inc(last_stored, 16)
            sp.dma_start(v_s[0, :, 0:W - ST].rearrange("n w k d -> n w (k d)"),
                         cache_v[0, :, ST:W].rearrange("n w k d -> n w (k d)")).then_inc(last_stored, 16)

            with sp.Fori(0, NQ) as q:
                def load_caches(s, part):
                    one = bass.ds(q * SQ + s, 1)
                    if part == 0:
                        sp.dma_start(memk_c[:, :, s, :], cache_mk[0, one].rearrange(
                            "n (t p) h d -> p (n t) (h d)", p=P)).then_inc(memc_loaded, 16)
                        sp.dma_start(k_c[:, s, :], cache_k[0, one].rearrange("n w k d -> (n w) (k d)")).then_inc(
                            cache_loaded, 16)
                    else:
                        sp.dma_start(memv_c[:, :, s, :], cache_mv[0, one].rearrange(
                            "n (t p) h d -> p (n t) (h d)", p=P)).then_inc(memc_loaded, 16)
                        sp.dma_start(v_c[:, s, :], cache_v[0, one].rearrange("n w k d -> (n w) (k d)")).then_inc(
                            cache_loaded, 16)

                qn = (q + 1) % NQ
                for t in range(3, NW + 3):
                    if t == 3:
                        sp.wait_ge(proj_done, q * NC + PRO_W)
                        sp.sem_inc(sp_past, 1)
                        load_caches(0, 0)
                        load_caches(1, 0)
                        sp.dma_start(st_c[:], state_conv[0, bass.ds(q * SQ, SQ)].rearrange(
                            "n j c -> (n j) c")).then_inc(cache_loaded, 16)
                    sp.wait_ge(w_split, q * NW + (PRO_W + t - 1))
                    w_tile(t % 2, in_srcs(t % NW) if t % NW < NIN else out_srcs(t - NIN))
                    if t in (3, 4):
                        load_caches(t - 3, 1)
                    if t == AT_NAT // 2 + 3:
                        sp.wait_ge(nat_out, q + 1)
                        for s in range(SQ):
                            for dst, src in ((k_s, kn_s), (v_s, vn_s)):
                                sp.dma_start(dst[0, bass.ds(q * SQ + s, 1), W - ST:W].rearrange(
                                    "n w k d -> (n w) (k d)"), src[s * ST:(s + 1) * ST, :]).then_inc(s_stored, 16)
                    if t == NIN + 1:
                        sp.wait_ge(y_ready, 1 + (q + 1) * Y_PARTS)
                        sp.sem_inc(sp_past, 1)
                        load_x(qn, 0)
                        load_x(qn, 1)
                    if t == NIN + 2:
                        sp.wait_ge(tail_out, q + 1)
                        sp.dma_start(conv_s[0, bass.ds(q * SQ, SQ)].rearrange("n j c -> (n j) c"),
                                     tail_nat[2:2 + 2 * SQ, :]).then_inc(s_stored, 16)
                    b = t - NIN - 1
                    if 2 <= b < NX:
                        sp.wait_ge(normed, (q + 1) * NX + (2 + b - 1))
                        load_x(qn, b)
                for b in range(NBLK):
                    if b % 2 == 0:
                        sp.wait_ge(normed, (q + 1) * NX + (2 + b // 2 + NBLK))
                    else:
                        sp.wait_ge(x_turned, (q + 1) * NX + (2 + b // 2 + NBLK))
                    sp.dma_start(residual[b], x_prompt[0, bass.ds(q * TP + b * P, P), :]).then_inc(res_loaded, 16)
                sp.dma_start(residual[NBLK], x_sample[bass.ds(q * SQ, SQ), :, :].rearrange(
                    "s t d -> (s t) d")).then_inc(res_loaded, 16)
                for b in range(NX):
                    sp.wait_ge(y_rows, 1 + q * NX + (b + 1))
                    if b < NBLK:
                        sp.dma_start(y_prompt[0, bass.ds(q * TP + b * P, P), :], o_nat[:, b, :]).then_inc(y_stored, 16)
                    else:
                        sp.dma_start(y_sample[bass.ds(q * SQ, SQ), :, :].rearrange("s t d -> (s t) d"),
                                     o_nat_s[:]).then_inc(y_stored, 16)

            sp.dma_start(conv_p[0, 0], tail_nat[0:2, :]).then_inc(last_stored, 16)
            sp.dma_start(k_p[0, 0].rearrange("w k d -> w (k d)"), k_nat[:]).then_inc(last_stored, 16)
            sp.dma_start(v_p[0, 0].rearrange("w k d -> w (k d)"), v_nat[:]).then_inc(last_stored, 16)
            for slot in range(2):
                sp.wait_ge(w_loaded[slot], loads_of(slot, NQ * NW + 2) * 16)
            sp.wait_ge(y_stored, 1 + NQ * 5 * 16)
            sp.wait_ge(s_stored, 1 + NQ * 5 * 16)
            sp.wait_ge(mkv_stored, 2 * 16)
            sp.wait_ge(last_stored, 5 * 16)

        N_CONST = (4 + 3 + SQ * ST) * 16

        @block.gpsimd
        def _(pool):
            def split_tile(slot, loaded, used, step, need):
                pool.wait_ge(w_loaded[slot], loaded)
                if used is not None:
                    pool.wait_ge(proj_done, used)
                pool.sem_inc(pool_past, 1)
                need(step(pool.tensor_scalar(w_hi[slot][:], w_raw[slot][:], 1.0, 1.0, ALU.mult, ALU.mult)))
                pool.tensor_tensor(w_lo[slot][:], w_raw[slot][:], w_hi[slot][:].bitcast(F32),
                                   ALU.subtract).then_inc(w_split, 1)

            def power(mean_count):
                pool.wait_ge(means, mean_count)
                pool.tensor_tensor(rstd[:], mean[:], neg_half[:, 0:1], ALU.pow).then_inc(rstds, 1)

            step, need, n = chain(pool, pool_step, 0)
            need(step(pool.memset(neg_half[:], -0.5)))
            split_tile(0, 16, None, step, need)
            power(1)
            power(2)
            split_tile(1, 16, None, step, need)
            power(xn(0, 0))
            power(xn(0, 1))
            split_tile(0, 32, 1, step, need)
            power(xn(0, 2))
            split_tile(1, 32, 2, step, need)
            power(xn(0, 3))
            power(xn(0, 4))
            split_tile(0, loads_of(0, 0) * 16, 3, step, need)
            n_pro = n[0]

            with pool.Fori(0, NQ) as q:
                step, need, n = chain(pool, pool_step, q * POOL_Q + n_pro)
                for t in range(1, NW + 1):
                    split_tile(t % 2, q * LOADS_Q[t % 2] * 16 + loads_of(t % 2, t) * 16,
                               q * NC + (PRO_W + 2 * (t - 1)), step, need)
                    for b, after in enumerate(POWER_AFTER):
                        if t == after:
                            power((q + 1) * NX + (2 + b + 1))
                pool.wait_ge(o_means, q + 1)
                pool.tensor_tensor(o_rstd[:], o_mean[:], neg_half[:], ALU.pow).then_inc(o_rstds, 1)
                assert n[0] == POOL_Q, n

        @block.tensor
        def _(pe):
            def mm(out, lhsT, rhs, start, stop):
                return pe.matmul(out, lhsT, rhs, start=start, stop=stop)

            def project(bank, slot, hi, lo, cols, width, order=range(KT), before_last=None):
                for i, k in enumerate(order):
                    if i == KT - 1 and before_last is not None:
                        before_last()
                    for n, (w, a) in enumerate(((w_hi, hi), (w_hi, lo), (w_lo, hi))):
                        last = mm(pj[bank][:, 0:width], w[slot][:, k, :], a[:, k, cols], i == 0 and n == 0,
                                  i == KT - 1 and n == 2)
                last.then_inc(proj_done, 1)

            def turn_x(slot, at_bank):
                for k in range(KT):
                    last = pe.transpose(pa[at_bank + k // 4][:, (k % 4) * P:(k % 4 + 1) * P],
                                        x_norm[:, slot, k * P:(k + 1) * P], ident[:])
                last.then_inc(x_turned, 1)

            def alone():
                pe.sem_inc(pe_past, 1)

            pe.wait_ge(ident_loaded, 16)
            for b in range(2):
                pe.wait_ge(normed, b + 1)
                turn_x(b, 2 * b)

            def first_x(b):
                pe.wait_ge(normed, xn(0, b))
                pe.wait_ge(h_ready, 1 + b + 1)
                turn_x(b % 2, 2)

            for i in range(PRO_W):
                pe.wait_ge(w_split, i + 1)
                if i == 0:
                    pe.wait_ge(h_ready, 2)
                if i == 3:
                    pe.wait_ge(mkv_evac, 1)
                project(i % 3, i % 2, y_hi, y_lo, slice(0, NM), NM)
                for b in FIRST_X[i]:
                    first_x(b)
            for half in range(2):
                for i in range(2):
                    for kt in range(2):
                        if half == 0 and i == 0 and kt == 0:
                            pe.wait_ge(mkv_evac, PRO_W)
                        last = pe.transpose(pa[kt][:, (2 * half + i) * P:(2 * half + i + 1) * P],
                                            mkv_raw[:, 2 * half + i, kt * P:(kt + 1) * P], ident[:])
            last.then_inc(mkv_turned, 1)

            with pe.Fori(0, NQ) as q:
                def cache_turn():
                    pe.wait_ge(cache_loaded, (q + 1) * 5 * 16)
                    pe.wait_ge(memc_loaded, (q + 1) * 4 * 16)
                    pe.wait_ge(mkv_nat_done, 2)
                    pe.wait_ge(o_rows, 1 + q * NOUT)
                    pe.wait_ge(h_ready, q * NX + (2 + NX))
                    for s in range(SQ):
                        for p in range(2):
                            for kt in range(2):
                                pe.transpose(pa[2 + s][:, (p * 2 + kt) * P:(p * 2 + kt + 1) * P],
                                             memk_c[:, kt, s, p * P:(p + 1) * P], ident[:])
                    for j in range(3):
                        pe.transpose(pa[1][:, j * 4:(j + 1) * 4], st_c[:, j * P:(j + 1) * P], ident[0:4, 0:4])
                    for s in range(SQ):
                        last = pe.transpose(pa[4][:, s * P:(s + 1) * P], k_c[:, s, :], ident[:])
                    last.then_inc(cache_turned, 1)

                def nat_turn():
                    pe.wait_ge(free_act, 1 + q * FREE_ACT[-1] + FREE_ACT[13])
                    pe.wait_ge(cache_out, q + 1)
                    for b in range(NBLK):
                        pe.transpose(pa[2][:, b * P:(b + 1) * P], v_raw[:, b * P:(b + 1) * P], ident[:])
                    pe.transpose(pa[3][0:TS, 0:P], v_raw[:, TP:T], ident[:])
                    pe.transpose(pa[3][:, P:2 * P], k_raw[:, 0:P], ident[:])
                    pe.transpose(pa[3][0:TS, 2 * P:3 * P], k_raw[:, P:P + TS], ident[:]).then_inc(nat_turned, 1)

                def sample_scores():
                    pe.wait_ge(free_dve, 1 + q * FREE_DVE[-1] + FREE_DVE[11])
                    pe.wait_ge(cache_out, q + 1)
                    pe.wait_ge(state_out, q + 1)
                    for s in range(SQ):
                        mm(pa[0][32 * s:32 * s + 32, 0:P + TS], q_bd[:, s, :], kt_s[:, s, :], True, True)
                    for s in range(SQ):
                        for p in range(2):
                            last = mm(pa[1][32 * s:32 * s + 32, 0:NM], mq_bd[:, s, p, :], mkt_s[:, s, p, :], p == 0,
                                      p == 1)
                    last.then_inc(ss_done, 1)

                def sample_turn():
                    pe.wait_ge(sp_ready, q + 1)
                    alone()
                    pe.transpose(pa[4][:, 0:SR], prob_s[:, 0:P], ident[0:SR, 0:SR])
                    pe.transpose(pa[4][0:TS, SR:2 * SR], prob_s[:, P:P + TS], ident[0:SR, 0:SR])
                    for kt in range(2):
                        last = pe.transpose(pa[4][:, (2 + kt) * SR:(3 + kt) * SR], mprob_s[:, kt * P:(kt + 1) * P],
                                            ident[0:SR, 0:SR])
                    last.then_inc(sp_turned, 1)

                def sample_values():
                    pe.wait_ge(spt_ready, q + 1)
                    pe.wait_ge(nat_out, q + 1)
                    for s in range(SQ):
                        r = slice(32 * s, 32 * s + 32)
                        mm(pa[0][r, 0:P], pt_s[:, r], v_c[:, s, :], True, False)
                        mm(pa[0][r, 0:P], ptn_s[:, r], vn_s[:], False, True)
                    for s in range(SQ):
                        r = slice(32 * s, 32 * s + 32)
                        for kt in range(2):
                            last = mm(pa[1][r, 0:NM], mpt_s[:, kt, r], memv_c[:, kt, s, :], kt == 0, kt == 1)
                    last.then_inc(so_done, 1)

                def sample_back():
                    pe.wait_ge(so_out, q + 1)
                    alone()
                    pe.transpose(pa[4][:, 0:SR], o_s[:], ident[0:SR, 0:SR])
                    for p in range(2):
                        last = pe.transpose(pa[4][:, (1 + p) * SR:(2 + p) * SR], mo_s[:, p * P:(p + 1) * P],
                                            ident[0:SR, 0:SR])
                    last.then_inc(so_turned, 1)

                def scores(i):
                    if i == 0:
                        pe.wait_ge(so_sel, q + 1)
                        pe.wait_ge(v_his, q + 1)
                        pe.wait_ge(nat_out, q + 1)
                    else:
                        pe.wait_ge(o_taken, q * NBLK + i)
                    for h in range(NH):
                        out = pa[h // 2][:, (h % 2) * 2 * W:(h % 2 + 1) * 2 * W]
                        for n, keys in enumerate((k_hh, k_ll)):
                            last = mm(out, q_st[:, h, i * P:(i + 1) * P], keys[:, h // G, i * P:i * P + 2 * W], n == 0,
                                      n == 1)
                    last.then_inc(s_done, 1)
                    gr, p = i // 2, i % 2
                    for hh in range(2):
                        for tb in range(2):
                            at_q = gr * 2 * P + tb * P
                            for n, keys in enumerate((mk_hh, mk_ll)):
                                last = mm(pa[3 + hh][:, tb * NM:(tb + 1) * NM], mq_st[:, 2 * p + hh, at_q:at_q + P],
                                          keys[:, 2 * p + hh, :], n == 0, n == 1)
                    last.then_inc(s_done, 1)

                def turn_probs(i):
                    pe.wait_ge(p_ready, q * 2 * NBLK + (2 * i + 1))
                    for kt in range(2):
                        for h in range(NH):
                            n = kt * NH + h
                            last = pe.transpose(pa[n // 4][:, (n % 4) * P:(n % 4 + 1) * P],
                                                prob[:, h, kt * P:(kt + 1) * P], ident[:])
                    last.then_inc(p_turned, 1)
                    pe.wait_ge(p_ready, q * 2 * NBLK + (2 * i + 2))
                    for kt in range(2):
                        for u in range(4):
                            last = pe.transpose(pa[3 + kt][:, u * P:(u + 1) * P], mprob[:, u, kt * P:(kt + 1) * P],
                                                ident[:])
                    last.then_inc(p_turned, 1)

                def values(i):
                    pe.wait_ge(pt_ready, q * 2 * NBLK + (2 * i + 1))
                    for kv in range(NKV):
                        for kt in range(2):
                            for n, pt in enumerate((pt_hi, pt_lo)):
                                a = kt * NH + kv * G
                                last = mm(pa[kv][:, 0:G * P], v_st[:, i + kt, kv, :], pt[:, a:a + G, :].rearrange(
                                    "p a b -> p (a b)"), kt == 0 and n == 0, kt == 1 and n == 1)
                    pe.wait_ge(pt_ready, q * 2 * NBLK + (2 * i + 2))
                    p = i % 2
                    for hh in range(2):
                        for kt in range(2):
                            for n, pt in enumerate((mpt_hi, mpt_lo)):
                                a = kt * 4 + hh * 2
                                last = mm(pa[2][:, hh * 2 * P:(hh + 1) * 2 * P], mv_st[:, kt, 2 * p + hh, :],
                                          pt[:, a:a + 2, :].rearrange("p a b -> p (a b)"), kt == 0 and n == 0,
                                          kt == 1 and n == 1)
                    last.then_inc(pv_done, 1)

                def tail_turn():
                    pe.wait_ge(tail_ready, q + 1)
                    pe.wait_ge(o_taken, q * NBLK + NBLK)
                    for j in range(3):
                        last = pe.transpose(pa[4][0:2 + 2 * SQ, j * P:(j + 1) * P], tail[:, j, :], ident[:])
                    last.then_inc(tail_turned, 1)

                def out_turn(f):
                    pe.wait_ge(free_act, 1 + q * FREE_ACT[-1] + FREE_ACT[2 * (NIN + f) + 1])
                    if f >= 2:
                        pe.wait_ge(o_rows, 1 + q * NOUT + (f - 1))
                    if f == 0:
                        pe.wait_ge(tail_out, q + 1)
                    for b in range(NBLK):
                        pe.transpose(pa[f % 2][:, b * P:(b + 1) * P], o_t[:, f % 2, b * P:(b + 1) * P], ident[:])
                    if f == NOUT // 2:
                        pe.wait_ge(o_rows, 1 + q * NOUT + f)
                    pe.transpose(pa[4][0:TS, (f % 4) * P:(f % 4 + 1) * P], o_t[:, f % 2, TP:T], ident[:]).then_inc(
                        o_turned, 1)

                def next_x(b):
                    pe.wait_ge(normed, (q + 1) * NX + (2 + b + 1))
                    if b:
                        pe.wait_ge(h_ready, (q + 1) * NX + (2 + b))
                    turn_x(b % 2, 2)

                def y_complete():
                    pe.wait_ge(y_ready, 1 + (q + 1) * Y_PARTS)

                for n in range(NC):
                    t, c = n // 2, n % 2
                    if c == 0:
                        pe.wait_ge(w_split, q * NW + (PRO_W + t + 1))
                    if n == 0:
                        pe.wait_ge(h_ready, q * NX + (2 + 3))
                    if n == 1:
                        pe.wait_ge(h_ready, q * NX + (2 + NX))
                    if n == 2 * NIN:
                        pe.wait_ge(y_ready, 1 + q * Y_PARTS + (Y_PARTS - 2))
                    if n < 3:
                        if n == 0:
                            pe.wait_ge(free_act, 1 + q * FREE_ACT[-1])
                            pe.wait_ge(free_dve, 1 + q * FREE_DVE[-1])
                    elif freed_by_act(n - 3):
                        pe.wait_ge(free_act, 1 + q * FREE_ACT[-1] + FREE_ACT[n - 3])
                    else:
                        pe.wait_ge(free_dve, 1 + q * FREE_DVE[-1] + FREE_DVE[n - 3])
                    if n < 2 * NIN:
                        project(n % 3, t % 2, h_hi, h_lo, chunk_cols(c), CW)
                    else:
                        project(n % 3, t % 2, y_hi, y_lo, chunk_cols(c), CW, (0, 1, 3, 4, 5, 6, 7, 2),
                                y_complete if n == 2 * NIN else None)
                    if n == AT_CACHE:
                        cache_turn()
                    if n == AT_NAT:
                        nat_turn()
                    for stage, fn in zip(AT_SAMPLE, (sample_scores, sample_turn, sample_values, sample_back)):
                        if n == stage:
                            fn()
                    for i in range(NBLK):
                        if n == AT_PV[i]:
                            values(i)
                        if n == AT_S[i]:
                            scores(i)
                        if n == AT_T[i]:
                            turn_probs(i)
                    if n == 2 * NIN:
                        tail_turn()
                    f = (n - 2 * NIN) // 2 - 1
                    if f >= 0 and c == 0:
                        out_turn(f)
                    for b in range(NX):
                        if n == AT_TURN[b]:
                            next_x(b)
                out_turn(NOUT - 1)

        @block.scalar
        def _(act):
            def copy(out, in_):
                return act.activation(out, in_, ACT.Copy)

            def square(b, rows):
                act.activation(x_norm[0:rows, b % 2, :], x_rows[0:rows, b % 2, :], ACT.Square,
                               accum_out=sq_sum[0:rows, :]).then_inc(squares, 1)

            def hi_of(dst, b, at_bank, rows):
                for half in range(2):
                    last = copy(dst[:, 4 * half:4 * half + 4, b * P:b * P + rows],
                                pa[at_bank + half][:].rearrange("p (k t) -> p k t", k=4)[:, :, 0:rows])
                last.then_inc(h_his, 1)

            for b in range(2):
                act.wait_ge(x_loaded[b], 16)
                if b == 1:
                    act.wait_ge(means, 1)
                square(b, P)
            for b in range(2):
                act.wait_ge(x_turned, b + 1)
                hi_of(y_hi, b, 2 * b, P)

            def first_sq(b):
                act.wait_ge(x_loaded[b % 2], xl(0, b))
                act.wait_ge(means, 2 + b)
                act.wait_ge(x_turned, 2 + max(b - 1, 0))
                square(b, P if b < NBLK else TS)

            def first_hi(b):
                act.wait_ge(x_turned, xn(0, b))
                hi_of(h_hi, b, 2, P if b < NBLK else TS)

            first_sq(0)
            first_sq(1)
            for i in range(PRO_W):
                act.wait_ge(proj_done, i + 1)
                copy(mkv_raw[:, i, :], pj[i % 3][:, 0:NM]).then_inc(mkv_evac, 1)
                for b in FIRST_X[i]:
                    first_hi(b)
                    if b + 2 < NX:
                        first_sq(b + 2)
            act.wait_ge(mkv_evac, PRO_W)
            for h in range(MH):
                for d in range(2):
                    last = copy(mk_hh[d * HD:(d + 1) * HD, h, :], mkv_raw[(h % 2) * HD:(h % 2 + 1) * HD, h // 2, :])
            last.then_inc(mkv_hi, 1)
            act.wait_ge(mkv_nat_done, 2)
            for kt in range(2):
                last = copy(mv_st[:, kt, :, 0:HD], mkv_nat[:, kt, NM:2 * NM].rearrange("p (h d) -> p h d", h=MH))
            last.then_inc(mkv_hi, 1)

            with act.Fori(0, NQ) as q:
                def next_sq(b):
                    act.wait_ge(x_loaded[b % 2], (q + 1) * (3 - b % 2) * 16 + (1 + b // 2 + 1) * 16)
                    act.wait_ge(means, (q + 1) * NX + (2 + b))
                    act.wait_ge(x_turned, (q + 1) * NX + (2 + max(b - 1, 0)))
                    square(b, P if b < NBLK else TS)

                def next_hi(b):
                    act.wait_ge(x_turned, (q + 1) * NX + (2 + b + 1))
                    hi_of(h_hi, b, 2, P if b < NBLK else TS)

                def evac(n):
                    name, c, ps = role(n), n % 2, pj[n % 3]
                    act.wait_ge(proj_done, q * NC + (PRO_W + n + 1))
                    pc = CW if c == 0 else CW - TS
                    cols = slice(c * CW, c * CW + pc)
                    if name == "K":
                        if n == 0:
                            act.wait_ge(y_ready, 1 + q * Y_PARTS)
                        for kv in range(NKV):
                            for d in range(2):
                                last = copy(k_hh[d * HD:(d + 1) * HD, kv, W + c * CW:W + c * CW + pc],
                                            ps[kv * HD:(kv + 1) * HD, 0:pc])
                        last.then_inc(act_half, 1)
                    elif name[0] in "QM":
                        for a in range(2):
                            h = a * G + int(name[1]) if name[0] == "Q" else 2 * int(name[1]) + a
                            st = q_st if name[0] == "Q" else mq_st
                            last = copy(st[0:HD, h, cols], ps[a * HD:(a + 1) * HD, 0:pc])
                        last.then_inc(act_half, 1)
                    elif name == "V":
                        copy(v_raw[:, chunk_cols(c)], ps[:, 0:CW]).then_inc(free_act, 1)
                    elif name[0] == "Z" or name[:2] == "CZ":
                        prev = max(m for m in range(n) if m % 2 == c and (role(m)[0] == "Z" or role(m)[:2] == "CZ")
                                   ) if n > 15 else None
                        if prev is not None:
                            act.wait_ge(free_dve, 1 + q * FREE_DVE[-1] + FREE_DVE[prev])
                        act.activation(tanh_t[:, c, :], ps[:, 0:CW], ACT.Tanh, scale=0.5).then_inc(act_half, 1)
                    elif name[:2] == "CC":
                        if name != "CC0":
                            act.wait_ge(free_dve, 1 + q * FREE_DVE[-1] + FREE_DVE[n - 5 if c else n - 5])
                        copy(cc_t[:, chunk_cols(c)], ps[:, 0:CW]).then_inc(free_act, 1)
                    elif name[0] == "O":
                        f = int(name[1])
                        if f >= 2:
                            act.wait_ge(o_turned, q * NOUT + (f - 1))
                        copy(o_t[:, f % 2, chunk_cols(c)], ps[:, 0:CW]).then_inc(free_act, 1)

                def caches():
                    act.wait_ge(cache_turned, q + 1)
                    for s in range(SQ):
                        copy(mkt_s[:, s, :, :], pa[2 + s][:].rearrange("p (a m) -> p a m", a=2))
                    copy(kt_s[:, :, 0:P], pa[4][:, 0:SQ * P].rearrange("p (s k) -> p s k", s=SQ)).then_inc(
                        cache_out, 1)

                def v_hi():
                    act.wait_ge(nat_turned, q + 1)
                    for b in range(NBLK):
                        last = copy(v_st[:, 1 + b, :, 0:HD], pa[2][:, b * P:(b + 1) * P].rearrange(
                            "p (v d) -> p v d", v=NKV))
                    last.then_inc(v_his, 1)

                def sample_exp():
                    act.wait_ge(ss_max, q + 1)
                    act.activation(prob_s[:], prob_s[:], ACT.Exp, bias=snmx[:], accum_out=ssum[:])
                    act.activation(ssexp[:], sink_s[:], ACT.Exp, bias=snmx[:])
                    act.activation(mprob_s[:], pa[1][0:SR, 0:NM], ACT.Exp, bias=tnmx[:], scale=SCALE,
                                   accum_out=tsum[:]).then_inc(ss_exp, 1)

                def sample_out():
                    act.wait_ge(so_done, q + 1)
                    copy(o_s[:], pa[0][0:SR, 0:P])
                    copy(mo_s[:], pa[1][0:SR, 0:NM]).then_inc(so_out, 1)

                def exp(i):
                    act.wait_ge(s_max, q * 2 * NBLK + (2 * i + 1))
                    for h in range(NH):
                        act.activation(prob[:, h, :], prob[:, h, :], ACT.Exp, bias=nmx[:, h:h + 1],
                                       accum_out=sums[:, h:h + 1])
                    act.activation(sexp[:], sexp[:], ACT.Exp).then_inc(exps, 1)
                    act.wait_ge(s_max, q * 2 * NBLK + (2 * i + 2))
                    for u in range(4):
                        last = act.activation(mprob[:, u, :], pa[3 + u // 2][:, (u % 2) * NM:(u % 2 + 1) * NM], ACT.Exp,
                                              bias=nmmx[:, u:u + 1], scale=SCALE, accum_out=msums[:, u:u + 1])
                    last.then_inc(exps, 1)

                def pt_hi_of(i):
                    act.wait_ge(p_turned, q * 2 * NBLK + (2 * i + 1))
                    for a in range(3):
                        last = copy(pt_hi[:, 4 * a:4 * a + 4, :], pa[a][:].rearrange("p (a b) -> p a b", a=4))
                    last.then_inc(pt_his, 1)
                    act.wait_ge(p_turned, q * 2 * NBLK + (2 * i + 2))
                    for a in range(2):
                        last = copy(mpt_hi[:, 4 * a:4 * a + 4, :], pa[3 + a][:].rearrange("p (a b) -> p a b", a=4))
                    last.then_inc(pt_his, 1)

                def halves(i):
                    act.wait_ge(pv_done, q * NBLK + (i + 1))
                    for kv in range(NKV):
                        copy(o_half[kv * HD:(kv + 1) * HD, :, :], pa[kv][HD:P, 0:G * P].rearrange(
                            "p (g t) -> p g t", g=G))
                    for hh in range(2):
                        last = copy(mo_half[hh * HD:(hh + 1) * HD, :], pa[2][HD:P, hh * 2 * P:(hh + 1) * 2 * P])
                    last.then_inc(o_halves, 1)

                def y_hi_of(i):
                    act.wait_ge(y32, q * 11 + Y32["a", i])
                    copy(y_hi[:, 3:6, i * P:(i + 1) * P], o_sum[:])
                    gr, p = i // 2, i % 2
                    copy(y_hi[:, 6 + p, gr * 2 * P:(gr + 1) * 2 * P], mo_sum[:]).then_inc(y_his, 1)

                def conv_hi(j):
                    act.wait_ge(y32, q * 11 + Y32["c", j])
                    copy(y_hi[:, j, :], g_t[:]).then_inc(y_his, 1)

                def out_squares(f):
                    act.wait_ge(o_turned, q * NOUT + (f + 1))
                    if f:
                        act.wait_ge(o_squares, q * NOUT + f)
                    for b in range(NBLK):
                        last = act.activation(squared[:, b, :], pa[f % 2][:, b * P:(b + 1) * P], ACT.Square,
                                              accum_out=o_parts[:, b, f:f + 1])
                    if f % 4 == 3:
                        for k, dump in enumerate((mo_half, mo_sum)):
                            last = act.activation(dump[0:TS, :], pa[4][0:TS, k * 2 * P:(k + 1) * 2 * P], ACT.Square,
                                                  accum_out=o_parts[0:TS, NBLK, f - 3 + k:f - 2 + k])
                    last.then_inc(o_squares, 1)

                for n in range(NC):
                    evac(n)
                    if n == AT_CACHE:
                        caches()
                    if n == AT_NAT:
                        v_hi()
                    if n == AT_SAMPLE[0]:
                        sample_exp()
                    if n == AT_SAMPLE[2]:
                        sample_out()
                    if n in CONV_END:
                        conv_hi(CONV_END.index(n))
                    for i in range(NBLK):
                        if n == AT_S[i]:
                            exp(i)
                        if n == AT_T[i]:
                            pt_hi_of(i)
                        if n == AT_PV[i]:
                            halves(i)
                            y_hi_of(i)
                    f = (n - 2 * NIN) // 2 - 1
                    if f >= 0 and n % 2 == 0:
                        out_squares(f)
                    for b in range(NX):
                        if n == AT_NORM[b]:
                            next_sq(b)
                        if n == AT_TURN[b]:
                            next_hi(b)
                out_squares(NOUT - 1)

        @block.vector
        def _(dve):
            def sub(out, whole, high):
                return dve.tensor_tensor(out, whole, high.bitcast(F32), ALU.subtract)

            def norm_rows(b, rows, g, count):
                dve.wait_ge(squares, count)
                dve.tensor_scalar(mean[0:rows, :], sq_sum[0:rows, :], 1.0 / D, EPS, ALU.mult, ALU.add).then_inc(
                    means, 1)
                dve.wait_ge(rstds, count)
                dve.scalar_tensor_tensor(out=x_norm[0:rows, b % 2, :], in0=x_rows[0:rows, b % 2, :],
                                         scalar=rstd[0:rows, :], in1=g[0:rows, :], op0=ALU.mult,
                                         op1=ALU.mult).then_inc(normed, 1)

            def lo_of(hi, lo, b, at_bank, rows, count):
                dve.wait_ge(h_his, count)
                for half in range(2):
                    a, cols = slice(4 * half, 4 * half + 4), slice(b * P, b * P + rows)
                    last = sub(lo[:, a, cols], pa[at_bank + half][:].rearrange(
                        "p (k t) -> p k t", k=4)[:, :, 0:rows], hi[:, a, cols])
                last.then_inc(h_ready, 1)

            def rows_of(b):
                return P if b < NBLK else TS

            for started in (y_rows, o_rows, free_act, free_dve, y_ready, y_stored, s_stored):
                dve.sem_inc(started, 1)
            dve.memset(sink_s[:], 0.0)
            dve.memset(mean[:], 1.0)
            dve.memset(o_parts[:], 0.0)
            for z in (k_hh[:, :, 0:W], k_ll[:, :, 0:W], v_st[:, 0, :, :]):
                dve.memset(z.bitcast(F32), 0.0)
            dve.memset(u_buf[:, :, 0:2], 0.0)
            dve.memset(q_bd[:], 0.0)
            dve.memset(mq_bd[:], 0.0)
            dve.memset(bias_first[:], NEG).then_inc(zeroed, 1)
            dve.wait_ge(zeroed, 1)
            step, need, n_ = chain(dve, dve_step, 0)
            dve.wait_ge(mem_g_loaded, 16)
            for b in range(2):
                norm_rows(b, P, g_mem, b + 1)
            for b in range(2):
                lo_of(y_hi, y_lo, b, 2 * b, P, b + 1)
            dve.wait_ge(g_pre_loaded, 16)
            norm_rows(0, P, g_pre, xn(0, 0))
            norm_rows(1, P, g_pre, xn(0, 1))
            for b in range(NX):
                lo_of(h_hi, h_lo, b, 2, rows_of(b), xn(0, b))
                if b + 2 < NX:
                    norm_rows(b + 2, rows_of(b + 2), g_pre, xn(0, b + 2))
            dve.wait_ge(mkv_hi, 1)
            for h in range(MH):
                src = mkv_raw[(h % 2) * HD:(h % 2 + 1) * HD, h // 2, :]
                r = slice((h % 2) * HD, (h % 2 + 1) * HD)
                for d in range(2):
                    last = sub(mk_ll[d * HD:(d + 1) * HD, h, :], src, mk_hh[r, h, :])
            dve.wait_ge(mkv_turned, 1)
            for kt in range(2):
                dve.tensor_copy(mkv_nat[:, kt, :], pa[kt][:]).then_inc(mkv_nat_done, 1)
            dve.wait_ge(mkv_hi, 2)
            dve.wait_ge(mkv_nat_done, 2)
            for kt in range(2):
                last = sub(mv_st[:, kt, :, HD:2 * HD], mkv_nat[:, kt, NM:2 * NM].rearrange("p (h d) -> p h d", h=MH),
                           mv_st[:, kt, :, 0:HD])
            last.then_inc(mkv_ready, 1)
            dve.wait_ge(const_loaded, N_CONST)

            with dve.Fori(0, NQ) as q:
                step, need, n_ = chain(dve, dve_step, q * DVE_Q)

                def evac(n):
                    name, c, ps = role(n), n % 2, pj[n % 3]
                    pc = CW if c == 0 else CW - TS
                    cols = slice(c * CW, c * CW + pc)
                    if freed_by_act(n):
                        return
                    if name[:2] in ("CH", "CB"):
                        dve.wait_ge(proj_done, q * NC + (PRO_W + n + 1))
                    else:
                        dve.wait_ge(act_half, q * HALF_Q + HALF[n])
                    if name == "K":
                        for kv in range(NKV):
                            for d in range(2):
                                kc = slice(W + c * CW, W + c * CW + pc)
                                r = slice(d * HD, (d + 1) * HD)
                                last = sub(k_ll[r, kv, kc], ps[kv * HD:(kv + 1) * HD, 0:pc], k_hh[r, kv, kc])
                        if c == 1:
                            dve.tensor_copy(k_raw[:], ps[:, CW - TS - P:CW])
                            for s in range(SQ):
                                last = dve.tensor_copy(kt_s[:, s, P:P + TS], ps[:, pc:CW])
                    elif name[0] in "QM":
                        for a in range(2):
                            r = slice(a * HD, (a + 1) * HD)
                            h = a * G + int(name[1]) if name[0] == "Q" else 2 * int(name[1]) + a
                            st = q_st if name[0] == "Q" else mq_st
                            last = sub(st[HD:P, h, cols], ps[r, 0:pc], st[0:HD, h, cols])
                            if c == 1:
                                new = ps[r, pc:CW].rearrange("p (s t) -> p s t", s=SQ)
                                dst = (q_bd[r, :, h * ST:(h + 1) * ST] if name[0] == "Q" else
                                       mq_bd[r, :, int(name[1]), h * ST:(h + 1) * ST])
                                last = dve.tensor_copy(dst, new)
                    elif name[0] == "Z":
                        last = dve.scalar_tensor_tensor(out=gate[:, int(name[1]), chunk_cols(c)], in0=tanh_t[:, c, :],
                                                        scalar=1.0, in1=ps[:, 0:CW], op0=ALU.add, op1=ALU.mult)
                    elif name[:2] == "CH":
                        j = int(name[2])
                        dve.wait_ge(free_act, 1 + q * FREE_ACT[-1] + FREE_ACT[n])
                        last = dve.tensor_tensor(u_buf[:, j, 2 + c * CW:2 + c * CW + pc], ps[:, 0:pc], cc_t[:, cols],
                                                 ALU.mult)
                        if c == 1:
                            last = dve.tensor_tensor(u_s[:, j, :, 2:2 + ST], ps[:, pc:CW].rearrange(
                                "p (s t) -> p s t", s=SQ), cc_t[:, TP:T].rearrange("p (s t) -> p s t", s=SQ), ALU.mult)
                    elif name[:2] == "CB":
                        need(taps[-1])
                        last = dve.tensor_tensor(c_t[:, chunk_cols(c)], ps[:, 0:CW], c_t[:, chunk_cols(c)], ALU.mult)
                    else:
                        last = dve.scalar_tensor_tensor(out=g_t[:, chunk_cols(c)], in0=tanh_t[:, c, :], scalar=1.0,
                                                        in1=ps[:, 0:CW], op0=ALU.add, op1=ALU.mult)
                    last.then_inc(free_dve, 1)

                taps = []

                def conv(j):
                    dve.wait_ge(free_dve, 1 + q * FREE_DVE[-1] + FREE_DVE[CH_END[j]])
                    for tap in range(3):
                        for out, src in ((c_t[:, 0:TP], u_buf[:, j, tap:tap + TP]),
                                         (c_t[:, TP:T].rearrange("p (s t) -> p s t", s=SQ),
                                          u_s[:, j, :, tap:tap + ST])):
                            w = cwt[:, j, tap:tap + 1]
                            if tap == 0:
                                tok = step(dve.tensor_scalar(out, src, w, None, ALU.mult))
                            else:
                                tok = step(dve.scalar_tensor_tensor(out=out, in0=src, scalar=w, in1=out, op0=ALU.mult,
                                                                    op1=ALU.add))
                        if tap < 2:
                            need(tok)
                    taps.append(tok)
                    dve.tensor_copy(tail[:, j, 0:2], u_buf[:, j, TP:TP + 2])
                    last = dve.tensor_copy(tail[:, j, 2:2 + 2 * SQ].rearrange("p (s t) -> p s t", s=SQ),
                                           u_s[:, j, :, ST:ST + 2])
                    tok = step(last)
                    if j == 2:
                        need(tok)
                        dve.tensor_copy(u_buf[:, :, 0:2], u_buf[:, :, TP:TP + 2]).then_inc(tail_ready, 1)

                def conv_y(j):
                    dve.wait_ge(free_dve, 1 + q * FREE_DVE[-1] + FREE_DVE[CONV_END[j]])
                    dve.scalar_tensor_tensor(out=g_t[:], in0=g_t[:], scalar=0.5, in1=c_t[:], op0=ALU.mult,
                                             op1=ALU.mult).then_inc(y32, 1)

                def conv_lo(j):
                    dve.wait_ge(y_his, q * 7 + YHI["c", j])
                    sub(y_lo[:, j, :], g_t[:], y_hi[:, j, :]).then_inc(y_ready, 1)

                def states():
                    dve.wait_ge(cache_turned, q + 1)
                    dve.tensor_copy(u_s[:, :, :, 0:2], pa[1][:, 0:3 * 2 * SQ].rearrange(
                        "p (j s t) -> p j s t", j=3, s=SQ)).then_inc(state_out, 1)

                def naturals():
                    dve.wait_ge(nat_turned, q + 1)
                    dve.wait_ge(s_stored, 1 + q * 5 * 16)
                    dve.tensor_copy(vn_s[:], pa[3][0:TS, 0:P])
                    dve.tensor_copy(k_nat[:], pa[3][:, P:2 * P])
                    dve.tensor_copy(kn_s[:], pa[3][0:TS, 2 * P:3 * P])
                    dve.wait_ge(v_his, q + 1)
                    for b in range(NBLK):
                        sub(v_st[:, 1 + b, :, HD:2 * HD], pa[2][:, b * P:(b + 1) * P].rearrange(
                            "p (v d) -> p v d", v=NKV), v_st[:, 1 + b, :, 0:HD])
                    dve.tensor_copy(v_nat[:], pa[2][:, (NBLK - 1) * P:NBLK * P]).then_inc(nat_out, 1)

                def sample_max():
                    dve.wait_ge(ss_done, q + 1)
                    need(step(dve.scalar_tensor_tensor(out=prob_s[:], in0=pa[0][0:SR, 0:P + TS], scalar=SCALE,
                                                       in1=bias_s[:], op0=ALU.mult, op1=ALU.add)))
                    a = step(dve.tensor_reduce(smx[:], prob_s[:], AX.X, ALU.max))
                    b = step(dve.tensor_reduce(tmx[:], pa[1][0:SR, 0:NM], AX.X, ALU.max))
                    need(b)
                    need(step(dve.tensor_tensor(smx[:], smx[:], sink_s[:], ALU.max)))
                    dve.tensor_scalar(snmx[:], smx[:], -1.0, None, ALU.mult)
                    dve.tensor_scalar(tnmx[:], tmx[:], -SCALE, None, ALU.mult).then_inc(ss_max, 1)

                def sample_norm():
                    dve.wait_ge(ss_exp, q + 1)
                    need(step(dve.tensor_tensor(sden[:], ssum[:], ssexp[:], ALU.add)))
                    step(dve.reciprocal(srden[:], sden[:]))
                    need(step(dve.reciprocal(trden[:], tsum[:])))
                    dve.tensor_scalar(prob_s[:], prob_s[:], srden[:], None, ALU.mult)
                    dve.tensor_scalar(mprob_s[:], mprob_s[:], trden[:], None, ALU.mult).then_inc(sp_ready, 1)

                def sample_pt():
                    dve.wait_ge(sp_turned, q + 1)
                    dve.tensor_copy(pt_s[:], pa[4][:, 0:SR])
                    dve.tensor_copy(ptn_s[:], pa[4][0:TS, SR:2 * SR])
                    dve.tensor_copy(mpt_s[:], pa[4][:, 2 * SR:4 * SR].rearrange("p (k r) -> p k r", k=2)).then_inc(
                        spt_ready, 1)

                def sample_select():
                    dve.wait_ge(so_turned, q + 1)
                    for kv in range(NKV):
                        r = slice(kv * HD, (kv + 1) * HD)
                        for s in range(SQ):
                            a = s * 32 + kv * G * ST
                            dve.tensor_copy(osel[r, :, s * ST:(s + 1) * ST], pa[4][r, a:a + G * ST].rearrange(
                                "p (g t) -> p g t", g=G))
                    for hh in range(2):
                        r = slice(hh * HD, (hh + 1) * HD)
                        for p in range(2):
                            a = (1 + p) * SR + (2 * p + hh) * ST
                            last = dve.tensor_copy(mosel[r, p, :].rearrange("p (s t) -> p s t", s=SQ), pa[4][
                                r, a:a + SR].rearrange("p (s t) -> p s t", s=SQ)[:, :, 0:ST])
                    last.then_inc(so_sel, 1)

                def sample_y():
                    dve.wait_ge(so_sel, q + 1)
                    dve.wait_ge(free_dve, 1 + q * FREE_DVE[-1] + FREE_DVE[23])
                    step(dve.scalar_tensor_tensor(out=osel[:], in0=osel[:], scalar=0.5, in1=gate[:, 0:3, TP:T],
                                                  op0=ALU.mult, op1=ALU.mult))
                    need(step(dve.scalar_tensor_tensor(out=mosel[:], in0=mosel[:], scalar=0.5, in1=gate[:, 3:5, TP:T],
                                                       op0=ALU.mult, op1=ALU.mult)))
                    step(dve.tensor_copy(y_hi[:, 3:6, TP:T], osel[:]))
                    need(step(dve.tensor_copy(y_hi[:, 6:8, TP:T], mosel[:])))
                    sub(y_lo[:, 3:6, TP:T], osel[:], y_hi[:, 3:6, TP:T])
                    sub(y_lo[:, 6:8, TP:T], mosel[:], y_hi[:, 6:8, TP:T]).then_inc(y_ready, 1)

                def soft_max(i):
                    dve.wait_ge(s_done, q * 2 * NBLK + (2 * i + 1))
                    if i == 0:
                        dve.wait_ge(y_stored, 1 + q * 5 * 16)
                        dve.wait_ge(mkv_stored, 32)
                    for a in range(3):
                        ps = pa[a][:].rearrange("p (h k) -> p h k", h=2)
                        hs = slice(2 * a, 2 * a + 2)
                        if i == 0:
                            dve.scalar_tensor_tensor(out=prob[:, hs, 0:W], in0=ps[:, :, 0:W], scalar=SCALE,
                                                     in1=bias_first[:, hs, :], op0=ALU.mult, op1=ALU.add)
                            last = dve.scalar_tensor_tensor(out=prob[:, hs, W:2 * W], in0=ps[:, :, W:2 * W],
                                                            scalar=SCALE, in1=bias[:, hs, W:2 * W], op0=ALU.mult,
                                                            op1=ALU.add)
                        else:
                            last = dve.scalar_tensor_tensor(out=prob[:, hs, :], in0=ps, scalar=SCALE, in1=bias[:, hs, :],
                                                            op0=ALU.mult, op1=ALU.add)
                    tok = step(last)
                    dve.wait_ge(s_done, q * 2 * NBLK + (2 * i + 2))
                    for hh in range(2):
                        last = dve.tensor_reduce(mmx[:, 2 * hh:2 * hh + 2], pa[3 + hh][:].rearrange(
                            "p (t k) -> p t k", t=2), AX.X, ALU.max)
                    mtok = step(last)
                    need(tok)
                    tok = step(dve.tensor_reduce(mx[:], prob[:], AX.X, ALU.max))
                    need(tok)
                    need(step(dve.tensor_tensor(mx[:], mx[:], sink[:], ALU.max)))
                    dve.tensor_scalar(nmx[:], mx[:], -1.0, None, ALU.mult)
                    dve.tensor_tensor(sexp[:], sink[:], mx[:], ALU.subtract).then_inc(s_max, 1)
                    dve.tensor_scalar(nmmx[:], mmx[:], -SCALE, None, ALU.mult).then_inc(s_max, 1)
                    if i == 0:
                        dve.tensor_copy(bias_first[:], bias[:, :, 0:W])

                def soft_norm(i):
                    dve.wait_ge(exps, q * 2 * NBLK + (2 * i + 1))
                    need(step(dve.tensor_tensor(den[:], sums[:], sexp[:], ALU.add)))
                    need(step(dve.reciprocal(rden[:], den[:])))
                    for h in range(NH):
                        last = dve.tensor_scalar(prob[:, h, :], prob[:, h, :], rden[:, h:h + 1], None, ALU.mult)
                    last.then_inc(p_ready, 1)
                    dve.wait_ge(exps, q * 2 * NBLK + (2 * i + 2))
                    need(step(dve.reciprocal(mrden[:], msums[:])))
                    for u in range(4):
                        last = dve.tensor_scalar(mprob[:, u, :], mprob[:, u, :], mrden[:, u:u + 1], None, ALU.mult)
                    last.then_inc(p_ready, 1)

                def pt_lo_of(i):
                    dve.wait_ge(pt_his, q * 2 * NBLK + (2 * i + 1))
                    for a in range(3):
                        s = slice(4 * a, 4 * a + 4)
                        last = sub(pt_lo[:, s, :], pa[a][:].rearrange("p (a b) -> p a b", a=4), pt_hi[:, s, :])
                    last.then_inc(pt_ready, 1)
                    dve.wait_ge(pt_his, q * 2 * NBLK + (2 * i + 2))
                    for a in range(2):
                        s = slice(4 * a, 4 * a + 4)
                        last = sub(mpt_lo[:, s, :], pa[3 + a][:].rearrange("p (a b) -> p a b", a=4), mpt_hi[:, s, :])
                    last.then_inc(pt_ready, 1)

                def attn_y(i):
                    gr, p = i // 2, i % 2
                    dve.wait_ge(o_halves, q * NBLK + (i + 1))
                    for kv in range(NKV):
                        r = slice(kv * HD, (kv + 1) * HD)
                        tok = step(dve.tensor_tensor(o_sum[r, :, :], pa[kv][0:HD, 0:G * P].rearrange(
                            "p (g t) -> p g t", g=G), o_half[r, :, :], ALU.add))
                    for hh in range(2):
                        r = slice(hh * HD, (hh + 1) * HD)
                        last = dve.tensor_tensor(mo_sum[r, :], pa[2][0:HD, hh * 2 * P:(hh + 1) * 2 * P], mo_half[r, :],
                                                 ALU.add)
                    last.then_inc(o_taken, 1)
                    need(tok)
                    dve.scalar_tensor_tensor(out=o_sum[:], in0=o_sum[:], scalar=0.5, in1=gate[:, 0:3, i * P:(i + 1) * P],
                                             op0=ALU.mult, op1=ALU.mult).then_inc(y32, 1)
                    dve.wait_ge(o_taken, q * NBLK + (i + 1))
                    dve.scalar_tensor_tensor(out=mo_sum[:], in0=mo_sum[:], scalar=0.5, in1=gate[
                        :, 3 + p, gr * 2 * P:(gr + 1) * 2 * P], op0=ALU.mult, op1=ALU.mult).then_inc(y32, 1)

                def attn_lo(i):
                    gr, p = i // 2, i % 2
                    dve.wait_ge(y_his, q * 7 + YHI["a", i])
                    cols, mcols = slice(i * P, (i + 1) * P), slice(gr * 2 * P, (gr + 1) * 2 * P)
                    sub(y_lo[:, 3:6, cols], o_sum[:], y_hi[:, 3:6, cols])
                    sub(y_lo[:, 6 + p, mcols], mo_sum[:], y_hi[:, 6 + p, mcols]).then_inc(y_ready, 1)

                def carry():
                    for t in (k_hh, k_ll):
                        dve.tensor_copy(t[:, :, 0:W].bitcast(F32) if False else t[:, :, 0:W], t[:, :, TP:TP + W])
                    dve.tensor_copy(v_st[:, 0, :, :], v_st[:, NBLK, :, :]).then_inc(y_ready, 1)

                def out_rows(f):
                    dve.wait_ge(o_squares, q * NOUT + (f + 1))
                    cols = slice(f * P, (f + 1) * P)
                    last = dve.tensor_tensor(o_nat[:, :, cols], pa[f % 2][:].rearrange("p (b c) -> p b c", b=NBLK),
                                             g_post[:, cols].unsqueeze(1).to_broadcast([P, NBLK, P]), ALU.mult)
                    if f % 4 == 3:
                        cols = slice((f - 3) * P, (f + 1) * P)
                        last = dve.tensor_tensor(o_nat_s[:, cols], pa[4][0:TS, :], g_post[0:TS, cols], ALU.mult)
                    last.then_inc(o_rows, 1)

                for n in range(NC):
                    evac(n)
                    for j in range(3):
                        if n == CH_END[j]:
                            conv(j)
                        if n == CONV_END[j]:
                            conv_y(j)
                            conv_lo(j)
                    if n == AT_CACHE:
                        states()
                    if n == AT_NAT:
                        naturals()
                    if n == AT_SAMPLE[0]:
                        sample_max()
                    if n == AT_SAMPLE[0] + 1:
                        sample_norm()
                    if n == AT_SAMPLE[1]:
                        sample_pt()
                    if n == AT_SAMPLE[3]:
                        sample_select()
                    if n == 23:
                        sample_y()
                    for i in range(NBLK):
                        if n == AT_S[i]:
                            soft_max(i)
                        if n == AT_S[i] + 1:
                            soft_norm(i)
                        if n == AT_T[i]:
                            pt_lo_of(i)
                        if n == AT_PV[i]:
                            attn_y(i)
                            attn_lo(i)
                    if n == 2 * NIN - 1:
                        carry()
                    if n == 2 * NIN:
                        dve.wait_ge(tail_turned, q + 1)
                        dve.tensor_copy(tail_nat[:], pa[4][0:2 + 2 * SQ, 0:DC]).then_inc(tail_out, 1)
                    f = (n - 2 * NIN) // 2 - 1
                    if f >= 0 and n % 2 == 0:
                        out_rows(f)
                    for b in range(NX):
                        if n == AT_NORM[b]:
                            norm_rows(b, rows_of(b), g_pre, (q + 1) * NX + (2 + b + 1))
                        if n == AT_TURN[b]:
                            lo_of(h_hi, h_lo, b, 2, rows_of(b), (q + 1) * NX + (2 + b + 1))
                out_rows(NOUT - 1)

                need(step(dve.tensor_reduce(o_mean[:], o_parts[:], AX.X, ALU.add)))
                dve.tensor_scalar(o_mean[:], o_mean[:], 1.0 / D, EPS, ALU.mult, ALU.add).then_inc(o_means, 1)
                dve.wait_ge(res_loaded, (q + 1) * NX * 16)
                dve.wait_ge(o_rstds, q + 1)
                dve.wait_ge(o_rows, 1 + (q + 1) * NOUT)
                for b in range(NX):
                    o = o_nat[:, b, :] if b < NBLK else o_nat_s[:]
                    dve.scalar_tensor_tensor(out=o, in0=o, scalar=o_rstd[0:rows_of(b), b:b + 1], in1=residual[b],
                                             op0=ALU.mult, op1=ALU.add).then_inc(y_rows, 1)
                assert n_[0] == DVE_Q, n_


W_DMAS = [2 if name[0] == "Q" or name in ("Z0", "Z1", "Z2") else 1 for name in TILES] + [4] * NOUT
LOADS_Q = [sum(W_DMAS[slot::2]) for slot in range(2)]


def loads_of(slot, t):
    return 2 + sum(W_DMAS[m % NW] for m in range(slot, t + 1, 2))


POWER_AFTER = [25, 25, 27, 28, 29]
FIRST_X = [(0,), (1,), (2, 3), (4,)]
CH_END = [2 * TILES.index(f"CH{j}") + 1 for j in range(3)]
CONV_END = [2 * TILES.index(f"CZ{j}") + 1 for j in range(3)]


def _order():
    y32, yhi, a, b = {}, {}, 0, 0
    for n in range(NC):
        for j in range(3):
            if n == CONV_END[j]:
                a, b = a + 1, b + 1
                y32["c", j], yhi["c", j] = a, b
        for i in range(NBLK):
            if n == AT_PV[i]:
                a, b = a + 2, b + 1
                y32["a", i], yhi["a", i] = a, b
    return y32, yhi


Y32, YHI = _order()
HALF, _n = {}, 0
for _c in range(2 * NIN):
    if not freed_by_act(_c) and role(_c)[:2] not in ("CH", "CB"):
        _n += 1
        HALF[_c] = _n
HALF_Q = _n


def constants():
    slopes = np.power(np.float32(2.0), -8.0 * np.arange(1, NH + 1, dtype=np.float32) / NH).astype(np.float32)

    def table(dist, valid):
        b = -(slopes[:, None, None] * np.abs(dist).astype(np.float32)[None])
        return np.where(valid[None], b, np.float32(NEG)).astype(np.float32)

    i, c = np.arange(W)[:, None], np.arange(2 * W)[None]
    dist = i + W - c
    bias = table(dist, (dist >= 0) & (dist < W)).transpose(1, 0, 2)
    bias_s = np.zeros((32 * SQ, P + TS), np.float32)
    t = np.arange(ST)[:, None]
    for s in range(SQ):
        old = W + t - np.arange(W)[None]
        new = t - np.arange(TS)[None] % ST
        d = np.concatenate([old, new], 1)
        own = np.concatenate([np.ones((1, W), bool), np.arange(TS)[None] // ST == s], 1)
        bias_s[32 * s:32 * s + NH * ST] = table(d, (d >= 0) & (d < W) & own).reshape(NH * ST, P + TS)
    return {"ident": np.eye(P, dtype=np.float32), "bias": np.ascontiguousarray(bias), "bias_s": bias_s}


_INS = ["x_prompt", "x_sample", "mem_prompt", "state_conv", "cache_swa_k", "cache_swa_v", "cache_mem_k", "cache_mem_v",
        "pre_norm_g", "post_norm_g", "w_in", "conv_w", "attn_sinks", "mem_norm_g", "w_mem_k", "w_mem_v", "w_out"]
_OUTS = [(1, 2048, 1024), (8, 4, 1024), (1, 1, 2, 384), (1, 1, 128, 2, 64), (1, 1, 128, 2, 64), (1, 1, 256, 4, 64),
         (1, 1, 256, 4, 64), (1, 8, 2, 384), (1, 8, 128, 2, 64), (1, 8, 128, 2, 64)]


def kernel(**inputs):
    import concourse.bacc as bacc
    from concourse.bass_utils import run_bass_kernel_spmd

    nc = bacc.Bacc("TRN2", target_bir_lowering=False, num_devices=1, dynamic_dma_scratch_size=1024)
    arrays, args = {}, []
    given = {name: np.ascontiguousarray(inputs[name]) for name in _INS}
    for name, a in list(given.items()) + list(constants().items()):
        arrays[f"in_{name}"] = a
        args.append(nc.dram_tensor(f"in_{name}", a.shape, mybir.dt.from_np(a.dtype), kind="ExternalInput").ap())
    for i, shape in enumerate(_OUTS):
        args.append(nc.dram_tensor(f"out_{i}", shape, F32, kind="ExternalOutput").ap())
    layer(nc, *args)
    r = run_bass_kernel_spmd(nc, [arrays], core_ids=[0])
    return tuple(r.results[0][f"out_{i}"] for i in range(len(_OUTS)))
```

```python
from contextlib import ExitStack

import concourse.bass as bass
import numpy as np
from concourse import mybir

F32 = mybir.dt.float32
F32R = mybir.dt.float32r
ALU = mybir.AluOpType
ACT = mybir.ActivationFunctionType
AX = mybir.AxisListType

P = 128
D = 1024
KT = D // P
HD = 64
NQ = 4
TP = 512
NBLK = TP // P
SQ = 2
ST = 4
TS = SQ * ST
T = TP + TS
CW = T // 2
NH, NKV, G = 6, 2, 3
MH = 4
NM = 256
W = 128
DC = 384
EPS = 1e-6
SCALE = HD ** -0.5
NEG = -1e30

TILES = ["V0", "K0", "M0", "M1", "Q0", "Q1", "Q2", "Z3", "Z0", "Z1", "Z2", "Z4"]
for _j in range(3):
    TILES += [f"CC{_j}", f"CH{_j}", f"CZ{_j}", f"CB{_j}"]
NIN = len(TILES)
NOUT = D // P
NW = NIN + NOUT
NC = 2 * NW
GATES_END = 2 * TILES.index("Z4") + 1
OFF = {"CB": 0, "CC": DC, "CH": 2 * DC, "CZ": 3 * DC, "Q": 4 * DC, "K": 5 * DC, "V": 5 * DC + P, "Z": 5 * DC + 2 * P,
       "M": 6 * DC + 2 * P}
W_IN_AT = {f"Z{j}": 6 * DC + 2 * P + NM + (j - 3) * P for j in (3, 4)}

AT_CACHE, AT_NAT = 9, 11
AT_SAMPLE = [14, 16, 17]
AT_S = [18 + 7 * i for i in range(NBLK)]
AT_T = [22 + 7 * i for i in range(NBLK)]
AT_PV = [24 + 7 * i for i in range(NBLK)]
AT_NORM = [49, 50, 52, 54, 56]
AT_TURN = [52, 54, 56, 58, 60]

HALF_OF = [slice(0, HD), slice(HD, P)]
PLACES = [[(slice(0, 3, 2), HALF_OF[kv], slice(kv, kv + 2)), (slice(1, 2), HALF_OF[1 - kv], slice(2 * kv, 2 * kv + 1))]
          for kv in range(NKV)]


def role(n):
    return TILES[n // 2] if n < 2 * NIN else f"O{n // 2 - NIN}"


def freed_by_act(n):
    return role(n)[0] in "VO" or role(n)[:2] == "CC"


FREE_ACT = [sum(freed_by_act(m) for m in range(n + 1)) for n in range(NC)]
FREE_DVE = [n + 1 - FREE_ACT[n] for n in range(NC)]

Y_PARTS = 3 * 2 + NBLK + 1 + 1
NX = NBLK + 1
N_CACHES = 2 * SQ + 1
N_STATES = 2 * SQ + 1
PRO_W = 4
DVE_Q, POOL_Q = 77, NW


def layer(nc, x_prompt, x_sample, mem_prompt, state_conv, cache_k, cache_v, cache_mk, cache_mv, pre_g, post_g, w_in,
          conv_w, sinks, mem_g, w_mk, w_mv, w_out, ident_d, bias_d, bias_s_d, y_prompt, y_sample, conv_p, k_p, v_p,
          mk_p, mv_p, conv_s, k_s, v_s):
    with ExitStack() as ctx:
        def sb(name, shape, dt=F32):
            return ctx.enter_context(nc.sbuf_tensor(name, shape, dt))

        def at(name, shape, dt, offset):
            return nc.alloc_sbuf_tensor_at(name, shape, dt, offset=offset)

        def sem(name):
            return ctx.enter_context(nc.semaphore(name))

        h_hi, h_lo = sb("h_hi", [P, KT, T], F32R), sb("h_lo", [P, KT, T], F32R)
        y_at = nc.sbuf_base
        y_hi, y_lo = sb("y_hi", [P, KT, T], F32R), sb("y_lo", [P, KT, T], F32R)
        memk_c = at("memk_c", [P, 2, SQ, NM], F32, y_at)
        memv_c = at("memv_c", [P, 2, SQ, NM], F32, y_at + KT * T * 4)
        SR = 32 * SQ
        spot = [y_at + 3 * T * 4]

        def early(name, shape):
            t = at(name, shape, F32, spot[0])
            spot[0] += -(-int(np.prod(shape[1:])) * 4 // 32) * 32
            return t

        mkt_s = early("mkt_s", [P, SQ, 2, NM])
        kt_s = early("kt_s", [P, SQ, P + TS])
        prob_s, mprob_s = early("prob_s", [SR, P + TS]), early("mprob_s", [SR, NM])
        pt_s, ptn_s, mpt_s = early("pt_s", [P, SR]), early("ptn_s", [TS, SR]), early("mpt_s", [P, 2, SR])
        assert spot[0] <= y_at + KT * T * 4
        spot = [y_at + (KT + 3) * T * 4]
        k_raw, v_raw = early("k_raw", [P, P + TS]), early("v_raw", [P, T])
        w_raw = [sb(f"w_raw{s}", [P, KT, P]) for s in range(2)]
        w_hi = [sb(f"w_hi{s}", [P, KT, P], F32R) for s in range(2)]
        w_lo = [sb(f"w_lo{s}", [P, KT, P], F32R) for s in range(2)]
        q_st = sb("q_st", [P, NH, TP], F32R)
        mq_st = sb("mq_st", [P, MH, TP], F32R)
        k_hh, k_ll = sb("k_hh", [P, NKV, W + TP], F32R), sb("k_ll", [P, NKV, W + TP], F32R)
        v_st = sb("v_st", [P, 1 + NBLK, NKV, 2 * HD], F32R)
        mk_hh, mk_ll = sb("mk_hh", [P, MH, NM], F32R), sb("mk_ll", [P, MH, NM], F32R)
        mv_st = sb("mv_st", [P, 2, MH, 2 * HD], F32R)
        bias = sb("bias", [P, NH, 2 * W])
        bias_first = sb("bias_first", [P, NH, W])
        att_at = nc.sbuf_base
        prob = sb("prob", [P, NH, 2 * W])
        mprob = sb("mprob", [P, 4, NM])
        pt_hi, pt_lo = sb("pt_hi", [P, 2 * NH, P], F32R), sb("pt_lo", [P, 2 * NH, P], F32R)
        mpt_hi, mpt_lo = sb("mpt_hi", [P, 8, P], F32R), sb("mpt_lo", [P, 8, P], F32R)
        o_nat = at("o_nat", [P, NBLK, D], F32, att_at)
        o_nat_s = at("o_nat_s", [TS, D], F32, att_at + NBLK * D * 4)
        o_t = at("o_t", [P, 2, T], F32, att_at + (NBLK + 1) * D * 4)
        xs_res = at("xs_res", [TS, D], F32, att_at + (NBLK + 1) * D * 4 + 2 * T * 4)
        mkv_raw = at("mkv_raw", [P, 4, NM], F32, att_at)
        mkv_nat = at("mkv_nat", [P, 2, 2 * NM], F32, att_at + 4 * NM * 4)
        g_mem = at("g_mem", [P, D], F32, att_at + 8 * NM * 4)
        assert (NBLK + 2) * D * 4 + 2 * T * 4 <= nc.sbuf_base - att_at
        gate_at = nc.sbuf_base
        gate = sb("gate", [P, 5, T])
        cc_t, c_t, g_t = sb("cc_t", [P, T]), sb("c_t", [P, T]), sb("g_t", [P, T])
        x_rows = at("x_rows", [P, 2, D], F32, gate_at)
        x_norm = at("x_norm", [P, 2, D], F32, gate_at + 2 * D * 4)
        assert 4 * D * 4 <= nc.sbuf_base - gate_at
        residual = [x_rows[:, 1, :], x_norm[:, 1, :], x_rows[:, 0, :], x_norm[:, 0, :], xs_res[:]]
        tanh_at = nc.sbuf_base
        tanh_t = sb("tanh_t", [P, 2, CW])
        squared = at("squared", [P, NBLK, P], F32, tanh_at)
        u_buf = sb("u_buf", [P, 3, 2 + TP])
        u_s = sb("u_s", [P, 3, SQ, 2 + ST])
        cwt = sb("cwt", [P, 3, 3])
        g_pre, g_post = sb("g_pre", [P, D]), sb("g_post", [P, D])
        sq_sum, mean, rstd = (sb(n, [P, 1]) for n in ("sq_sum", "mean", "rstd"))
        o_parts = sb("o_parts", [P, NX, NOUT])
        o_mean, o_rstd, neg_half = (sb(n, [P, NX]) for n in ("o_mean", "o_rstd", "neg_half"))
        ident = sb("ident", [P, P])
        sink = sb("sink", [P, NH])
        mx, nmx, sums, sexp, den, rden = (sb(n, [P, NH]) for n in ("mx", "nmx", "sums", "sexp", "den", "rden"))
        mmx, nmmx, msums, mrden = (sb(n, [P, 4]) for n in ("mmx", "nmmx", "msums", "mrden"))
        o_half, o_sum = sb("o_half", [P, G, P]), sb("o_sum", [P, G, P])
        mo_half, mo_sum = sb("mo_half", [P, 2 * P]), sb("mo_sum", [P, 2 * P])
        k_nat, v_nat = sb("k_nat", [P, P]), sb("v_nat", [P, P])
        kn_s, vn_s = sb("kn_s", [TS, P]), sb("vn_s", [TS, P])
        tail = sb("tail", [P, 3, 2 + 2 * SQ])
        tail_nat = sb("tail_nat", [2 + 2 * SQ, DC])
        st_c = sb("st_c", [2 * SQ, DC])
        k_c, v_c = sb("k_c", [P, SQ, P]), sb("v_c", [P, SQ, P])
        q_bd = sb("q_bd", [P, SQ, 32])
        mq_bd = sb("mq_bd", [P, SQ, 2, 32])
        bias_s = sb("bias_s", [SR, P + TS])
        sink_s = sb("sink_s", [SR, 1])
        smx, snmx, ssum, ssexp, sden, srden = (sb("s_" + n, [SR, 1]) for n in (
            "mx", "nmx", "sum", "sexp", "den", "rden"))
        tmx, tnmx, tsum, trden = (sb("t_" + n, [SR, 1]) for n in ("mx", "nmx", "sum", "rden"))
        osel, mosel = sb("osel", [P, G, TS]), sb("mosel", [P, 2, TS])

        pj = [ctx.enter_context(nc.psum_tensor(f"pj{i}", [P, 512], F32)) for i in range(3)]
        pa = [ctx.enter_context(nc.psum_tensor(f"pa{i}", [P, 512], F32)) for i in range(5)]

        const_loaded, mem_g_loaded = sem("const_loaded"), sem("mem_g_loaded")
        ident_loaded, g_pre_loaded, res_loaded = sem("ident_loaded"), sem("g_pre_loaded"), sem("res_loaded")
        x_loaded = [sem(f"x_loaded{s}") for s in range(2)]
        w_loaded = [sem(f"w_loaded{s}") for s in range(2)]
        cache_loaded, memc_loaded = sem("cache_loaded"), sem("memc_loaded")
        zeroed = sem("zeroed")
        w_split = sem("w_split")
        squares, means, rstds, normed = sem("squares"), sem("means"), sem("rstds"), sem("normed")
        x_turned, h_his, h_ready = sem("x_turned"), sem("h_his"), sem("h_ready")
        proj_done, free_act, free_dve = sem("proj_done"), sem("free_act"), sem("free_dve")
        act_half = sem("act_half")
        mkv_evac, mkv_turned, mkv_nat_done, mkv_hi, mkv_ready = (sem(n) for n in (
            "mkv_evac", "mkv_turned", "mkv_nat_done", "mkv_hi", "mkv_ready"))
        cache_turned, cache_out, state_out = sem("cache_turned"), sem("cache_out"), sem("state_out")
        nat_turned, v_his, nat_out = sem("nat_turned"), sem("v_his"), sem("nat_out")
        s_done, s_max, exps, p_ready = sem("s_done"), sem("s_max"), sem("exps"), sem("p_ready")
        p_turned, pt_his, pt_ready, pv_done = sem("p_turned"), sem("pt_his"), sem("pt_ready"), sem("pv_done")
        o_halves, o_taken, y32, y_his, y_ready = (sem(n) for n in ("o_halves", "o_taken", "y32", "y_his", "y_ready"))
        ss_done, ss_max, ss_exp, sp_ready = sem("ss_done"), sem("ss_max"), sem("ss_exp"), sem("sp_ready")
        sp_turned, spt_ready, so_done, so_sel = (sem(n) for n in ("sp_turned", "spt_ready", "so_done", "so_sel"))
        tail_ready, tail_turned, tail_out = sem("tail_ready"), sem("tail_turned"), sem("tail_out")
        o_turned, o_rows, o_squares, o_means, o_rstds, y_rows = (sem(n) for n in (
            "o_turned", "o_rows", "o_squares", "o_means", "o_rstds", "y_rows"))
        os_squares = sem("os_squares")
        y_stored, s_stored, mkv_stored, last_stored = (sem(n) for n in (
            "y_stored", "s_stored", "mkv_stored", "last_stored"))
        dve_step, pool_step = sem("dve_step"), sem("pool_step")

        pe_past, pool_past, sp_past = sem("pe_past"), sem("pool_past"), sem("sp_past")

        def chain(eng, semaphore, base):
            n = [0]

            def step(ins):
                n[0] += 1
                ins.then_inc(semaphore, 1)
                return n[0]

            def need(token):
                eng.wait_ge(semaphore, base + token)

            return step, need, n

        def chunk_cols(c):
            return slice(c * CW, (c + 1) * CW)

        def xl(qx, b):
            return (qx * (3 - b % 2) + (1 + b // 2 + 1)) * 16

        def xn(qx, b):
            return qx * NX + (2 + b + 1)

        def rows_of(b):
            return P if b < NBLK else TS

        block = ctx.enter_context(nc.Block())

        @block.sync
        def _(sp):
            def w_tile(t):
                if t < NIN:
                    name = TILES[t]
                    a = W_IN_AT.get(name, OFF[name[:-1]] + int(name[-1]) * P)
                    src = w_in[0, :, a:a + P]
                else:
                    src = w_out[0, :, (t - NIN) * P:(t - NIN + 1) * P]
                sp.dma_start(w_raw[t % 2][:], src.rearrange("(k p) f -> p k f", p=P)).then_inc(w_loaded[t % 2], 16)

            def load_x(qx, b):
                if b < NBLK:
                    sp.dma_start(x_rows[:, b % 2, :],
                                 x_prompt[0, bass.ds(qx * TP + b * P, P), :]).then_inc(x_loaded[b % 2], 16)
                else:
                    sp.dma_start(x_rows[0:TS, b % 2, :], x_sample[bass.ds(qx * SQ, SQ), :, :].rearrange(
                        "s t d -> (s t) d")).then_inc(x_loaded[b % 2], 16)

            sp.dma_start(x_rows[:, 0, :], mem_prompt[0, 0:P, :]).then_inc(x_loaded[0], 16)
            sp.dma_start(g_mem[:], mem_g.to_broadcast([P, D])).then_inc(mem_g_loaded, 16)
            sp.dma_start(x_rows[:, 1, :], mem_prompt[0, P:2 * P, :]).then_inc(x_loaded[1], 16)
            sp.dma_start(ident[:], ident_d).then_inc(ident_loaded, 16)

            def load_mem_w(i):
                src = (w_mk if i < 2 else w_mv)[0, :, (i % 2) * P:(i % 2 + 1) * P]
                sp.dma_start(w_raw[i % 2][:], src.rearrange("(k p) f -> p k f", p=P)).then_inc(w_loaded[i % 2], 16)

            load_mem_w(0)
            load_mem_w(1)
            sp.dma_start(g_pre[:], pre_g.to_broadcast([P, D])).then_inc(g_pre_loaded, 16)
            for b in range(2):
                sp.wait_ge(normed, b + 1)
                load_x(0, b)
            for i in range(2, PRO_W + 4):
                sp.wait_ge(w_split, i - 1)
                if i < PRO_W:
                    load_mem_w(i)
                else:
                    w_tile(i - PRO_W)
                for b in (2,) if i == 2 else (3, 4) if i == 3 else ():
                    sp.wait_ge(normed, xn(0, b - 2))
                    load_x(0, b)
                if i == PRO_W:
                    sp.dma_start(sink[:], sinks.to_broadcast([P, NH])).then_inc(const_loaded, 16)
                    sp.dma_start(bias[:], bias_d).then_inc(const_loaded, 16)
                    sp.dma_start(bias_s[:], bias_s_d).then_inc(const_loaded, 16)
            sp.dma_start(g_post[:], post_g.to_broadcast([P, D])).then_inc(const_loaded, 16)
            with nc.allow_non_contiguous_dma(reason="a few hundred single values, once"):
                for j in range(3):
                    sp.dma_start(cwt[:, j, :], conv_w[0, :, j * P:(j + 1) * P].rearrange("w c -> c w")).then_inc(
                        const_loaded, 16)
                sp.wait_ge(zeroed, 1)
                for s in range(SQ):
                    for t in range(ST):
                        sp.dma_start(sink_s[32 * s + t:32 * s + t + ST * (NH - 1) + 1:ST, :],
                                     sinks.rearrange("a h -> h a")).then_inc(const_loaded, 16)
            sp.wait_ge(mkv_nat_done, 2)
            sp.dma_start(mk_p[0, 0].rearrange("(t p) h d -> p t (h d)", p=P), mkv_nat[:, :, 0:NM]).then_inc(
                mkv_stored, 16)
            sp.dma_start(mv_p[0, 0].rearrange("(t p) h d -> p t (h d)", p=P), mkv_nat[:, :, NM:2 * NM]).then_inc(
                mkv_stored, 16)
            sp.dma_start(k_s[0, :, 0:W - ST].rearrange("n w k d -> n w (k d)"),
                         cache_k[0, :, ST:W].rearrange("n w k d -> n w (k d)")).then_inc(last_stored, 16)
            sp.dma_start(v_s[0, :, 0:W - ST].rearrange("n w k d -> n w (k d)"),
                         cache_v[0, :, ST:W].rearrange("n w k d -> n w (k d)")).then_inc(last_stored, 16)

            with sp.Fori(0, NQ) as q:
                def load_caches(s, part):
                    one = bass.ds(q * SQ + s, 1)
                    if part == 0:
                        sp.dma_start(memk_c[:, :, s, :], cache_mk[0, one].rearrange(
                            "n (t p) h d -> p (n t) (h d)", p=P)).then_inc(memc_loaded, 16)
                        sp.dma_start(k_c[:, s, :], cache_k[0, one].rearrange("n w k d -> (n w) (k d)")).then_inc(
                            cache_loaded, 16)
                    else:
                        sp.dma_start(memv_c[:, :, s, :], cache_mv[0, one].rearrange(
                            "n (t p) h d -> p (n t) (h d)", p=P)).then_inc(memc_loaded, 16)
                        sp.dma_start(v_c[:, s, :], cache_v[0, one].rearrange("n w k d -> (n w) (k d)")).then_inc(
                            cache_loaded, 16)

                def load_residual(b):
                    src = (x_prompt[0, bass.ds(q * TP + b * P, P), :] if b < NBLK else
                           x_sample[bass.ds(q * SQ, SQ), :, :].rearrange("s t d -> (s t) d"))
                    sp.dma_start(residual[b], src).then_inc(res_loaded, 16)

                qn = (q + 1) % NQ
                for t in range(4, NW + 4):
                    sp.wait_ge(w_split, q * NW + (PRO_W + t - 1))
                    w_tile(t % NW)
                    if t == 4:
                        sp.wait_ge(proj_done, q * NC + PRO_W)
                        sp.sem_inc(sp_past, 1)
                        load_caches(0, 0)
                        load_caches(1, 0)
                        sp.dma_start(st_c[:], state_conv[0, bass.ds(q * SQ, SQ)].rearrange(
                            "n j c -> (n j) c")).then_inc(cache_loaded, 16)
                    if t in (NW, NW + 1):
                        sp.wait_ge(normed, (q + 1) * NX + (2 + NBLK + t - NW))
                        load_residual(2 * (t - NW))
                        sp.wait_ge(x_turned, (q + 1) * NX + (2 + NBLK + t - NW))
                        load_residual(2 * (t - NW) + 1)
                    if t == NW + 1:
                        load_residual(NBLK)
                    if t in (4, 5):
                        load_caches(t - 4, 1)
                    if t == AT_NAT // 2 + 3:
                        sp.wait_ge(nat_out, q + 1)
                        for s in range(SQ):
                            for dst, src in ((k_s, kn_s), (v_s, vn_s)):
                                sp.dma_start(dst[0, bass.ds(q * SQ + s, 1), W - ST:W].rearrange(
                                    "n w k d -> (n w) (k d)"), src[s * ST:(s + 1) * ST, :]).then_inc(s_stored, 16)
                    if t == NIN + 1:
                        sp.wait_ge(y_ready, 1 + (q + 1) * Y_PARTS)
                        sp.sem_inc(sp_past, 1)
                        load_x(qn, 0)
                        load_x(qn, 1)
                    if t == NIN + 2:
                        sp.wait_ge(tail_out, q + 1)
                        sp.dma_start(conv_s[0, bass.ds(q * SQ, SQ)].rearrange("n j c -> (n j) c"),
                                     tail_nat[2:2 + 2 * SQ, :]).then_inc(s_stored, 16)
                    b = t - NIN - 1
                    if 2 <= b < NX:
                        sp.wait_ge(normed, (q + 1) * NX + (2 + b - 1))
                        load_x(qn, b)
                for b in range(NX):
                    sp.wait_ge(y_rows, 1 + q * NX + (b + 1))
                    if b < NBLK:
                        sp.dma_start(y_prompt[0, bass.ds(q * TP + b * P, P), :], o_nat[:, b, :]).then_inc(y_stored, 16)
                    else:
                        sp.dma_start(y_sample[bass.ds(q * SQ, SQ), :, :].rearrange("s t d -> (s t) d"),
                                     o_nat_s[:]).then_inc(y_stored, 16)

            sp.dma_start(conv_p[0, 0], tail_nat[0:2, :]).then_inc(last_stored, 16)
            sp.dma_start(k_p[0, 0].rearrange("w k d -> w (k d)"), k_nat[:]).then_inc(last_stored, 16)
            sp.dma_start(v_p[0, 0].rearrange("w k d -> w (k d)"), v_nat[:]).then_inc(last_stored, 16)
            for slot in range(2):
                sp.wait_ge(w_loaded[slot], loads_of(NQ * NW + 2 + slot) * 16)
            sp.wait_ge(y_stored, 1 + NQ * NX * 16)
            sp.wait_ge(s_stored, 1 + NQ * N_STATES * 16)
            sp.wait_ge(mkv_stored, 2 * 16)
            sp.wait_ge(last_stored, 5 * 16)

        N_CONST = (4 + 3 + SQ * ST) * 16

        @block.gpsimd
        def _(pool):
            def split_tile(slot, loaded, used, step, need):
                pool.wait_ge(w_loaded[slot], loaded)
                if used is not None:
                    pool.wait_ge(proj_done, used)
                pool.sem_inc(pool_past, 1)
                need(step(pool.tensor_scalar(w_hi[slot][:], w_raw[slot][:], 1.0, 1.0, ALU.mult, ALU.mult)))
                pool.tensor_tensor(w_lo[slot][:], w_raw[slot][:], w_hi[slot][:].bitcast(F32),
                                   ALU.subtract).then_inc(w_split, 1)

            def power(mean_count):
                pool.wait_ge(means, mean_count)
                pool.tensor_tensor(rstd[:], mean[:], neg_half[:, 0:1], ALU.pow).then_inc(rstds, 1)

            step, need, n = chain(pool, pool_step, 0)
            need(step(pool.memset(neg_half[:], -0.5)))
            power(1)
            power(2)
            split_tile(0, 16, None, step, need)
            split_tile(1, 16, None, step, need)
            power(xn(0, 0))
            power(xn(0, 1))
            split_tile(0, 32, 1, step, need)
            power(xn(0, 2))
            split_tile(1, 32, 2, step, need)
            power(xn(0, 3))
            power(xn(0, 4))
            for t in range(2):
                split_tile(t, loads_of(t) * 16, 3 + t, step, need)
            n_pro = n[0]

            with pool.Fori(0, NQ) as q:
                step, need, n = chain(pool, pool_step, q * POOL_Q + n_pro)
                for t in range(2, NW + 2):
                    split_tile(t % 2, q * (NW // 2) * 16 + loads_of(t) * 16,
                               q * NC + (PRO_W + 2 * (t - 1)), step, need)
                    for b, after in enumerate(POWER_AFTER):
                        if t == after:
                            power((q + 1) * NX + (2 + b + 1))
                pool.wait_ge(o_means, q + 1)
                pool.tensor_tensor(o_rstd[:], o_mean[:], neg_half[:], ALU.pow).then_inc(o_rstds, 1)
                assert n[0] == POOL_Q, n

        @block.tensor
        def _(pe):
            def mm(out, lhsT, rhs, start, stop):
                return pe.matmul(out, lhsT, rhs, start=start, stop=stop)

            def project(bank, slot, hi, lo, cols, width):
                for k in range(KT):
                    for n, (w, a) in enumerate(((w_hi, hi), (w_hi, lo), (w_lo, hi))):
                        last = mm(pj[bank][:, 0:width], w[slot][:, k, :], a[:, k, cols], k == 0 and n == 0,
                                  k == KT - 1 and n == 2)
                last.then_inc(proj_done, 1)

            def turn_x(slot, at_bank):
                for k in range(KT):
                    last = pe.transpose(pa[at_bank + k // 4][:, (k % 4) * P:(k % 4 + 1) * P],
                                        x_norm[:, slot, k * P:(k + 1) * P], ident[:])
                last.then_inc(x_turned, 1)

            def turn_sample_x(at_bank):
                alone()
                for k in range(KT):
                    last = pe.transpose(pa[at_bank][:, k * TS:(k + 1) * TS], x_norm[0:TS, NBLK % 2, k * P:(k + 1) * P],
                                        ident[0:TS, 0:TS])
                last.then_inc(x_turned, 1)

            def alone():
                pe.sem_inc(pe_past, 1)

            pe.wait_ge(ident_loaded, 16)
            for b in range(2):
                pe.wait_ge(normed, b + 1)
                turn_x(b, 2 * b)

            def first_x(b):
                pe.wait_ge(normed, xn(0, b))
                if b < NBLK:
                    pe.wait_ge(h_ready, 1 + b + 1)
                    turn_x(b % 2, 2)
                else:
                    turn_sample_x(4)

            for i in range(PRO_W):
                pe.wait_ge(w_split, i + 1)
                if i == 0:
                    pe.wait_ge(h_ready, 2)
                if i == 3:
                    pe.wait_ge(mkv_evac, 1)
                project(i % 3, i % 2, y_hi, y_lo, slice(0, NM), NM)
                for b in FIRST_X[i]:
                    first_x(b)
            for half in range(2):
                for i in range(2):
                    for kt in range(2):
                        if half == 0 and i == 0 and kt == 0:
                            pe.wait_ge(mkv_evac, PRO_W)
                        last = pe.transpose(pa[kt][:, (2 * half + i) * P:(2 * half + i + 1) * P],
                                            mkv_raw[:, 2 * half + i, kt * P:(kt + 1) * P], ident[:])
            last.then_inc(mkv_turned, 1)

            with pe.Fori(0, NQ) as q:
                def cache_turn():
                    pe.wait_ge(cache_loaded, (q + 1) * N_CACHES * 16)
                    pe.wait_ge(memc_loaded, (q + 1) * 2 * SQ * 16)
                    pe.wait_ge(mkv_nat_done, 2)
                    pe.wait_ge(o_rows, 1 + q * NOUT)
                    pe.wait_ge(h_ready, q * NX + (2 + NX))
                    for s in range(SQ):
                        for p in range(2):
                            for kt in range(2):
                                pe.transpose(pa[2 + s][:, (p * 2 + kt) * P:(p * 2 + kt + 1) * P],
                                             memk_c[:, kt, s, p * P:(p + 1) * P], ident[:])
                    for j in range(3):
                        pe.transpose(pa[1][:, j * 4:(j + 1) * 4], st_c[:, j * P:(j + 1) * P], ident[0:4, 0:4])
                    for s in range(SQ):
                        last = pe.transpose(pa[4][:, s * P:(s + 1) * P], k_c[:, s, :], ident[:])
                    last.then_inc(cache_turned, 1)

                def nat_turn():
                    pe.wait_ge(free_act, 1 + q * FREE_ACT[-1] + FREE_ACT[2 * TILES.index("V0") + 1])
                    pe.wait_ge(cache_out, q + 1)
                    for b in range(NBLK):
                        pe.transpose(pa[2][:, b * P:(b + 1) * P], v_raw[:, b * P:(b + 1) * P], ident[:])
                    pe.transpose(pa[3][0:TS, 0:P], v_raw[:, TP:T], ident[:])
                    pe.transpose(pa[3][:, P:2 * P], k_raw[:, 0:P], ident[:])
                    pe.transpose(pa[3][0:TS, 2 * P:3 * P], k_raw[:, P:P + TS], ident[:]).then_inc(nat_turned, 1)

                def sample_scores():
                    pe.wait_ge(free_dve, 1 + q * FREE_DVE[-1] + FREE_DVE[2 * TILES.index("Q2") + 1])
                    pe.wait_ge(cache_out, q + 1)
                    pe.wait_ge(state_out, q + 1)
                    for s in range(SQ):
                        mm(pa[0][32 * s:32 * s + 32, 0:P + TS], q_bd[:, s, :], kt_s[:, s, :], True, True)
                    for s in range(SQ):
                        for p in range(2):
                            last = mm(pa[1][32 * s:32 * s + 32, 0:NM], mq_bd[:, s, p, :], mkt_s[:, s, p, :], p == 0,
                                      p == 1)
                    last.then_inc(ss_done, 1)

                def sample_turn():
                    pe.wait_ge(sp_ready, q + 1)
                    alone()
                    pe.transpose(pa[4][:, 0:SR], prob_s[:, 0:P], ident[0:SR, 0:SR])
                    pe.transpose(pa[4][0:TS, SR:2 * SR], prob_s[:, P:P + TS], ident[0:SR, 0:SR])
                    for kt in range(2):
                        last = pe.transpose(pa[4][:, (2 + kt) * SR:(3 + kt) * SR], mprob_s[:, kt * P:(kt + 1) * P],
                                            ident[0:SR, 0:SR])
                    last.then_inc(sp_turned, 1)

                def sample_values():
                    pe.wait_ge(spt_ready, q + 1)
                    pe.wait_ge(nat_out, q + 1)
                    for s in range(SQ):
                        r = slice(32 * s, 32 * s + 32)
                        mm(pa[0][:, r], v_c[:, s, :], pt_s[:, r], True, False)
                        mm(pa[0][:, r], vn_s[:], ptn_s[:, r], False, True)
                    for s in range(SQ):
                        r = slice(32 * s, 32 * s + 32)
                        for p in range(2):
                            at_c = p * SR + 32 * s
                            for kt in range(2):
                                last = mm(pa[1][:, at_c:at_c + 32], memv_c[:, kt, s, p * P:(p + 1) * P],
                                          mpt_s[:, kt, r], kt == 0, kt == 1)
                    last.then_inc(so_done, 1)

                def scores(i):
                    if i == 0:
                        pe.wait_ge(so_sel, q + 1)
                        pe.wait_ge(v_his, q + 1)
                        pe.wait_ge(nat_out, q + 1)
                    else:
                        pe.wait_ge(o_taken, q * NBLK + i)
                    for h in range(NH):
                        out = pa[h // 2][:, (h % 2) * 2 * W:(h % 2 + 1) * 2 * W]
                        for n, keys in enumerate((k_hh, k_ll)):
                            last = mm(out, q_st[:, h, i * P:(i + 1) * P], keys[:, h // G, i * P:i * P + 2 * W], n == 0,
                                      n == 1)
                    last.then_inc(s_done, 1)
                    gr, p = i // 2, i % 2
                    for hh in range(2):
                        for tb in range(2):
                            at_q = gr * 2 * P + tb * P
                            for n, keys in enumerate((mk_hh, mk_ll)):
                                last = mm(pa[3 + hh][:, tb * NM:(tb + 1) * NM], mq_st[:, 2 * p + hh, at_q:at_q + P],
                                          keys[:, 2 * p + hh, :], n == 0, n == 1)
                    last.then_inc(s_done, 1)

                def turn_probs(i):
                    pe.wait_ge(p_ready, q * 2 * NBLK + (2 * i + 1))
                    for kt in range(2):
                        for h in range(NH):
                            n = kt * NH + h
                            last = pe.transpose(pa[n // 4][:, (n % 4) * P:(n % 4 + 1) * P],
                                                prob[:, h, kt * P:(kt + 1) * P], ident[:])
                    last.then_inc(p_turned, 1)
                    pe.wait_ge(p_ready, q * 2 * NBLK + (2 * i + 2))
                    for kt in range(2):
                        for u in range(4):
                            last = pe.transpose(pa[3 + kt][:, u * P:(u + 1) * P], mprob[:, u, kt * P:(kt + 1) * P],
                                                ident[:])
                    last.then_inc(p_turned, 1)

                def values(i):
                    pe.wait_ge(pt_ready, q * 2 * NBLK + (2 * i + 1))
                    for kv in range(NKV):
                        for kt in range(2):
                            for n, pt in enumerate((pt_hi, pt_lo)):
                                a = kt * NH + kv * G
                                last = mm(pa[kv][:, 0:G * P], v_st[:, i + kt, kv, :], pt[:, a:a + G, :].rearrange(
                                    "p a b -> p (a b)"), kt == 0 and n == 0, kt == 1 and n == 1)
                    last.then_inc(pv_done, 1)
                    pe.wait_ge(pt_ready, q * 2 * NBLK + (2 * i + 2))
                    p = i % 2
                    for hh in range(2):
                        for kt in range(2):
                            for n, pt in enumerate((mpt_hi, mpt_lo)):
                                a = kt * 4 + hh * 2
                                last = mm(pa[2][:, hh * 2 * P:(hh + 1) * 2 * P], mv_st[:, kt, 2 * p + hh, :],
                                          pt[:, a:a + 2, :].rearrange("p a b -> p (a b)"), kt == 0 and n == 0,
                                          kt == 1 and n == 1)
                    last.then_inc(pv_done, 1)

                def tail_turn():
                    pe.wait_ge(tail_ready, q + 1)
                    pe.wait_ge(o_taken, q * NBLK + NBLK)
                    for j in range(3):
                        last = pe.transpose(pa[4][0:2 + 2 * SQ, j * P:(j + 1) * P], tail[:, j, :], ident[:])
                    last.then_inc(tail_turned, 1)

                def out_turn(f):
                    if f >= 2:
                        pe.wait_ge(o_rows, 1 + q * NOUT + (f - 1))
                    if f == 0:
                        pe.wait_ge(tail_out, q + 1)
                    for b in range(NBLK):
                        if b % 2 == 0:
                            pe.wait_ge(free_act, 1 + q * FREE_ACT[-1] + FREE_ACT[2 * (NIN + f) + b // 2])
                        pe.transpose(pa[f % 2][:, b * P:(b + 1) * P], o_t[:, f % 2, b * P:(b + 1) * P], ident[:])
                    if f == NOUT // 2:
                        pe.wait_ge(o_rows, 1 + q * NOUT + f)
                    pe.transpose(pa[4][0:TS, (f % 4) * P:(f % 4 + 1) * P], o_t[:, f % 2, TP:T], ident[:]).then_inc(
                        o_turned, 1)

                def next_x(b):
                    pe.wait_ge(normed, (q + 1) * NX + (2 + b + 1))
                    if b:
                        pe.wait_ge(h_ready, (q + 1) * NX + (2 + b))
                    if b < NBLK:
                        turn_x(b % 2, 2)
                    else:
                        turn_sample_x(2)

                for n in range(NC):
                    t, c = n // 2, n % 2
                    if c == 0:
                        pe.wait_ge(w_split, q * NW + (PRO_W + t + 1))
                    if n == 0:
                        pe.wait_ge(h_ready, q * NX + (2 + 3))
                    if n == 1:
                        pe.wait_ge(h_ready, q * NX + (2 + NX))
                    if n == 2 * NIN:
                        pe.wait_ge(y_ready, 1 + q * Y_PARTS + (Y_PARTS - 1))
                    if n == 2 * NIN + 1:
                        pe.wait_ge(y_ready, 1 + (q + 1) * Y_PARTS)
                    if n < 3:
                        if n == 0:
                            pe.wait_ge(free_act, 1 + q * FREE_ACT[-1])
                            pe.wait_ge(free_dve, 1 + q * FREE_DVE[-1])
                    elif freed_by_act(n - 3):
                        pe.wait_ge(free_act, 1 + q * FREE_ACT[-1] + FREE_ACT[n - 3])
                    else:
                        pe.wait_ge(free_dve, 1 + q * FREE_DVE[-1] + FREE_DVE[n - 3])
                    if n < 2 * NIN:
                        project(n % 3, t % 2, h_hi, h_lo, chunk_cols(c), CW)
                    else:
                        project(n % 3, t % 2, y_hi, y_lo, chunk_cols(c), CW)
                    if n == AT_CACHE:
                        cache_turn()
                    if n == AT_NAT:
                        nat_turn()
                    for stage, fn in zip(AT_SAMPLE, (sample_scores, sample_turn, sample_values)):
                        if n == stage:
                            fn()
                    for i in range(NBLK):
                        if n == AT_PV[i]:
                            values(i)
                        if n == AT_S[i]:
                            scores(i)
                        if n == AT_T[i]:
                            turn_probs(i)
                    if n == 2 * NIN:
                        tail_turn()
                    f = (n - 2 * NIN) // 2 - 1
                    if f >= 0 and c == 0:
                        out_turn(f)
                    for b in range(NX):
                        if n == AT_TURN[b]:
                            next_x(b)
                out_turn(NOUT - 1)

        @block.scalar
        def _(act):
            def copy(out, in_):
                return act.activation(out, in_, ACT.Copy)

            def square(b, rows):
                act.activation(x_norm[0:rows, b % 2, :], x_rows[0:rows, b % 2, :], ACT.Square,
                               accum_out=sq_sum[0:rows, :]).then_inc(squares, 1)

            def hi_of(dst, b, at_bank):
                for half in range(2):
                    last = copy(dst[:, 4 * half:4 * half + 4, b * P:(b + 1) * P],
                                pa[at_bank + half][:].rearrange("p (k t) -> p k t", k=4))
                last.then_inc(h_his, 1)

            def sample_hi(at_bank):
                copy(h_hi[:, :, TP:T], pa[at_bank][:, 0:KT * TS].rearrange("p (k t) -> p k t", k=KT)).then_inc(
                    h_his, 1)

            for b in range(2):
                act.wait_ge(x_loaded[b], 16)
                if b == 1:
                    act.wait_ge(means, 1)
                square(b, P)
            for b in range(2):
                act.wait_ge(x_turned, b + 1)
                hi_of(y_hi, b, 2 * b)

            def first_sq(b):
                act.wait_ge(x_loaded[b % 2], xl(0, b))
                act.wait_ge(means, 2 + b)
                act.wait_ge(x_turned, 2 + max(b - 1, 0))
                square(b, P if b < NBLK else TS)

            def first_hi(b):
                act.wait_ge(x_turned, xn(0, b))
                if b < NBLK:
                    hi_of(h_hi, b, 2)
                else:
                    sample_hi(4)

            first_sq(0)
            first_sq(1)
            for i in range(PRO_W):
                act.wait_ge(proj_done, i + 1)
                copy(mkv_raw[:, i, :], pj[i % 3][:, 0:NM]).then_inc(mkv_evac, 1)
                for b in FIRST_X[i]:
                    first_hi(b)
                    if b + 2 < NX:
                        first_sq(b + 2)
            act.wait_ge(mkv_evac, PRO_W)
            for h in range(MH):
                for d in range(2):
                    last = copy(mk_hh[d * HD:(d + 1) * HD, h, :], mkv_raw[(h % 2) * HD:(h % 2 + 1) * HD, h // 2, :])
            last.then_inc(mkv_hi, 1)
            act.wait_ge(mkv_nat_done, 2)
            for kt in range(2):
                last = copy(mv_st[:, kt, :, 0:HD], mkv_nat[:, kt, NM:2 * NM].rearrange("p (h d) -> p h d", h=MH))
            last.then_inc(mkv_hi, 1)

            with act.Fori(0, NQ) as q:
                def next_sq(b):
                    act.wait_ge(x_loaded[b % 2], (q + 1) * (3 - b % 2) * 16 + (1 + b // 2 + 1) * 16)
                    act.wait_ge(means, (q + 1) * NX + (2 + b))
                    act.wait_ge(x_turned, (q + 1) * NX + (2 + max(b - 1, 0)))
                    square(b, P if b < NBLK else TS)

                def next_hi(b):
                    act.wait_ge(x_turned, (q + 1) * NX + (2 + b + 1))
                    if b < NBLK:
                        hi_of(h_hi, b, 2)
                    else:
                        sample_hi(2)

                def evac(n):
                    name, c, ps = role(n), n % 2, pj[n % 3]
                    act.wait_ge(proj_done, q * NC + (PRO_W + n + 1))
                    pc = CW if c == 0 else CW - TS
                    cols = slice(c * CW, c * CW + pc)
                    if name == "K0":
                        if c == 0:
                            act.wait_ge(y_ready, 1 + q * Y_PARTS)
                        for kv in range(NKV):
                            for d in range(2):
                                last = copy(k_hh[d * HD:(d + 1) * HD, kv, W + c * CW:W + c * CW + pc],
                                            ps[kv * HD:(kv + 1) * HD, 0:pc])
                        last.then_inc(act_half, 1)
                    elif name[0] in "QM":
                        for a in range(2):
                            h = 2 * int(name[1]) + a
                            st = q_st if name[0] == "Q" else mq_st
                            last = copy(st[0:HD, h, cols], ps[a * HD:(a + 1) * HD, 0:pc])
                        last.then_inc(act_half, 1)
                    elif name == "V0":
                        copy(v_raw[:, chunk_cols(c)], ps[:, 0:CW]).then_inc(free_act, 1)
                    elif name[0] == "Z" or name[:2] == "CZ":
                        prev = max(m for m in range(n) if m % 2 == c and (role(m)[0] == "Z" or role(m)[:2] == "CZ")
                                   ) if n > 15 else None
                        if prev is not None:
                            act.wait_ge(free_dve, 1 + q * FREE_DVE[-1] + FREE_DVE[prev])
                        act.activation(tanh_t[:, c, :], ps[:, 0:CW], ACT.Tanh, scale=0.5).then_inc(act_half, 1)
                    elif name[:2] == "CC":
                        if name != "CC0":
                            act.wait_ge(free_dve, 1 + q * FREE_DVE[-1] + FREE_DVE[n - 6])
                        copy(cc_t[:, chunk_cols(c)], ps[:, 0:CW]).then_inc(free_act, 1)
                    elif name[0] == "O":
                        f = int(name[1])
                        if f >= 2:
                            act.wait_ge(o_turned, q * NOUT + (f - 1))
                        copy(o_t[:, f % 2, chunk_cols(c)], ps[:, 0:CW]).then_inc(free_act, 1)

                def caches():
                    act.wait_ge(cache_turned, q + 1)
                    for s in range(SQ):
                        copy(mkt_s[:, s, :, :], pa[2 + s][:].rearrange("p (a m) -> p a m", a=2))
                    copy(kt_s[:, :, 0:P], pa[4][:, 0:SQ * P].rearrange("p (s k) -> p s k", s=SQ)).then_inc(
                        cache_out, 1)

                def v_hi():
                    act.wait_ge(nat_turned, q + 1)
                    for b in range(NBLK):
                        last = copy(v_st[:, 1 + b, :, 0:HD], pa[2][:, b * P:(b + 1) * P].rearrange(
                            "p (v d) -> p v d", v=NKV))
                    last.then_inc(v_his, 1)

                def sample_exp():
                    act.wait_ge(ss_max, q + 1)
                    act.activation(prob_s[:], prob_s[:], ACT.Exp, bias=snmx[:], accum_out=ssum[:])
                    act.activation(ssexp[:], sink_s[:], ACT.Exp, bias=snmx[:])
                    act.activation(mprob_s[:], pa[1][0:SR, 0:NM], ACT.Exp, bias=tnmx[:], scale=SCALE,
                                   accum_out=tsum[:]).then_inc(ss_exp, 1)

                def exp(i):
                    act.wait_ge(s_max, q * 2 * NBLK + (2 * i + 1))
                    for h in range(NH):
                        act.activation(prob[:, h, :], prob[:, h, :], ACT.Exp, bias=nmx[:, h:h + 1],
                                       accum_out=sums[:, h:h + 1])
                    act.activation(sexp[:], sexp[:], ACT.Exp).then_inc(exps, 1)
                    act.wait_ge(s_max, q * 2 * NBLK + (2 * i + 2))
                    for u in range(4):
                        last = act.activation(mprob[:, u, :], pa[3 + u // 2][:, (u % 2) * NM:(u % 2 + 1) * NM], ACT.Exp,
                                              bias=nmmx[:, u:u + 1], scale=SCALE, accum_out=msums[:, u:u + 1])
                    last.then_inc(exps, 1)

                def pt_hi_of(i):
                    act.wait_ge(p_turned, q * 2 * NBLK + (2 * i + 1))
                    for a in range(3):
                        last = copy(pt_hi[:, 4 * a:4 * a + 4, :], pa[a][:].rearrange("p (a b) -> p a b", a=4))
                    last.then_inc(pt_his, 1)
                    act.wait_ge(p_turned, q * 2 * NBLK + (2 * i + 2))
                    for a in range(2):
                        last = copy(mpt_hi[:, 4 * a:4 * a + 4, :], pa[3 + a][:].rearrange("p (a b) -> p a b", a=4))
                    last.then_inc(pt_his, 1)

                def halves(i):
                    act.wait_ge(pv_done, q * 2 * NBLK + (2 * i + 1))
                    for kv in range(NKV):
                        src = pa[kv][HD:P, 0:G * P].rearrange("p (g t) -> p g t", g=G)
                        for gs, half, tiles in PLACES[kv]:
                            last = copy(o_half[half, tiles, :], src[:, gs, :])
                    last.then_inc(o_halves, 1)
                    act.wait_ge(pv_done, q * 2 * NBLK + (2 * i + 2))
                    for hh in range(2):
                        last = copy(mo_half[hh * HD:(hh + 1) * HD, :], pa[2][HD:P, hh * 2 * P:(hh + 1) * 2 * P])
                    last.then_inc(o_halves, 1)

                def y_hi_of(i):
                    act.wait_ge(y32, q * Y32_Q + Y32["a", i])
                    copy(y_hi[:, 3:6, i * P:(i + 1) * P], o_sum[:])
                    gr, p = i // 2, i % 2
                    copy(y_hi[:, 6 + p, gr * 2 * P:(gr + 1) * 2 * P], mo_sum[:]).then_inc(y_his, 1)

                def conv_hi(n):
                    act.wait_ge(y32, q * Y32_Q + Y32["c", n])
                    cols = chunk_cols(n % 2)
                    copy(y_hi[:, int(role(n)[2]), cols], g_t[:, cols]).then_inc(y_his, 1)

                def out_squares(f):
                    act.wait_ge(o_turned, q * NOUT + (f + 1))
                    if f:
                        act.wait_ge(o_squares, q * NOUT + f)
                    for b in range(NBLK):
                        last = act.activation(squared[:, b, :], pa[f % 2][:, b * P:(b + 1) * P], ACT.Square,
                                              accum_out=o_parts[:, b, f:f + 1])
                    last.then_inc(o_squares, 1)
                    if f % 4 == 3:
                        for k, dump in enumerate((mo_half, mo_sum)):
                            last = act.activation(dump[0:TS, :], pa[4][0:TS, k * 2 * P:(k + 1) * 2 * P], ACT.Square,
                                                  accum_out=o_parts[0:TS, NBLK, f - 3 + k:f - 2 + k])
                        last.then_inc(os_squares, 1)

                for n in range(NC):
                    evac(n)
                    if n == AT_CACHE:
                        caches()
                    if n == AT_NAT:
                        v_hi()
                    if n == AT_SAMPLE[0]:
                        sample_exp()
                    if role(n)[:2] == "CB":
                        conv_hi(n)
                    for i in range(NBLK):
                        if n == AT_S[i] + 1:
                            exp(i)
                        if n == AT_T[i]:
                            pt_hi_of(i)
                        if n == AT_PV[i]:
                            halves(i)
                            y_hi_of(i)
                    f = (n - 2 * NIN) // 2 - 1
                    if f >= 0 and n % 2 == 0:
                        out_squares(f)
                    for b in range(NX):
                        if n == AT_NORM[b]:
                            next_sq(b)
                        if n == AT_TURN[b]:
                            next_hi(b)
                out_squares(NOUT - 1)

        @block.vector
        def _(dve):
            def sub(out, whole, high):
                return dve.tensor_tensor(out, whole, high.bitcast(F32), ALU.subtract)

            def norm_rows(b, rows, g, count, g_loaded=None):
                dve.wait_ge(squares, count)
                dve.tensor_scalar(mean[0:rows, :], sq_sum[0:rows, :], 1.0 / D, EPS, ALU.mult, ALU.add).then_inc(
                    means, 1)
                if g_loaded is not None:
                    dve.wait_ge(g_loaded, 16)
                dve.wait_ge(rstds, count)
                dve.scalar_tensor_tensor(out=x_norm[0:rows, b % 2, :], in0=x_rows[0:rows, b % 2, :],
                                         scalar=rstd[0:rows, :], in1=g[0:rows, :], op0=ALU.mult,
                                         op1=ALU.mult).then_inc(normed, 1)

            def lo_of(hi, lo, b, at_bank, count):
                dve.wait_ge(h_his, count)
                for half in range(2):
                    a, cols = slice(4 * half, 4 * half + 4), slice(b * P, (b + 1) * P)
                    last = sub(lo[:, a, cols], pa[at_bank + half][:].rearrange("p (k t) -> p k t", k=4), hi[:, a, cols])
                last.then_inc(h_ready, 1)

            def sample_lo(at_bank, count):
                dve.wait_ge(h_his, count)
                sub(h_lo[:, :, TP:T], pa[at_bank][:, 0:KT * TS].rearrange("p (k t) -> p k t", k=KT),
                    h_hi[:, :, TP:T]).then_inc(h_ready, 1)

            for started in (y_rows, o_rows, free_act, free_dve, y_ready, y_stored, s_stored):
                dve.sem_inc(started, 1)
            dve.memset(sink_s[:], 0.0)
            dve.memset(mean[:], 1.0)
            dve.memset(o_parts[:], 0.0)
            for z in (k_hh[:, :, 0:W], k_ll[:, :, 0:W], v_st[:, 0, :, :]):
                dve.memset(z.bitcast(F32), 0.0)
            dve.memset(u_buf[:, :, 0:2], 0.0)
            dve.memset(q_bd[:], 0.0)
            dve.memset(mq_bd[:], 0.0)
            dve.memset(bias_first[:], NEG).then_inc(zeroed, 1)
            dve.wait_ge(zeroed, 1)
            step, need, n_ = chain(dve, dve_step, 0)
            for b in range(2):
                norm_rows(b, P, g_mem, b + 1, mem_g_loaded)
            for b in range(2):
                lo_of(y_hi, y_lo, b, 2 * b, b + 1)
            norm_rows(0, P, g_pre, xn(0, 0), g_pre_loaded)
            norm_rows(1, P, g_pre, xn(0, 1))
            for b in range(NX):
                if b < NBLK:
                    lo_of(h_hi, h_lo, b, 2, xn(0, b))
                else:
                    sample_lo(4, xn(0, b))
                if b + 2 < NX:
                    norm_rows(b + 2, rows_of(b + 2), g_pre, xn(0, b + 2))
            dve.wait_ge(mkv_hi, 1)
            for h in range(MH):
                src = mkv_raw[(h % 2) * HD:(h % 2 + 1) * HD, h // 2, :]
                r = slice((h % 2) * HD, (h % 2 + 1) * HD)
                for d in range(2):
                    last = sub(mk_ll[d * HD:(d + 1) * HD, h, :], src, mk_hh[r, h, :])
            dve.wait_ge(mkv_turned, 1)
            for kt in range(2):
                dve.tensor_copy(mkv_nat[:, kt, :], pa[kt][:]).then_inc(mkv_nat_done, 1)
            dve.wait_ge(mkv_hi, 2)
            dve.wait_ge(mkv_nat_done, 2)
            for kt in range(2):
                last = sub(mv_st[:, kt, :, HD:2 * HD], mkv_nat[:, kt, NM:2 * NM].rearrange("p (h d) -> p h d", h=MH),
                           mv_st[:, kt, :, 0:HD])
            last.then_inc(mkv_ready, 1)

            with dve.Fori(0, NQ) as q:
                step, need, n_ = chain(dve, dve_step, q * DVE_Q)

                def evac(n):
                    name, c, ps = role(n), n % 2, pj[n % 3]
                    pc = CW if c == 0 else CW - TS
                    cols = slice(c * CW, c * CW + pc)
                    if freed_by_act(n):
                        return
                    if name[:2] in ("CH", "CB"):
                        dve.wait_ge(proj_done, q * NC + (PRO_W + n + 1))
                    else:
                        dve.wait_ge(act_half, q * HALF_Q + HALF[n])
                    if name == "K0":
                        for kv in range(NKV):
                            for d in range(2):
                                kc = slice(W + c * CW, W + c * CW + pc)
                                r = slice(d * HD, (d + 1) * HD)
                                last = sub(k_ll[r, kv, kc], ps[kv * HD:(kv + 1) * HD, 0:pc], k_hh[r, kv, kc])
                        if c == 1:
                            dve.tensor_copy(k_raw[:], ps[:, CW - TS - P:CW])
                            for s in range(SQ):
                                last = dve.tensor_copy(kt_s[:, s, P:P + TS], ps[:, pc:CW])
                    elif name[0] in "QM":
                        for a in range(2):
                            r = slice(a * HD, (a + 1) * HD)
                            h = 2 * int(name[1]) + a
                            st = q_st if name[0] == "Q" else mq_st
                            last = sub(st[HD:P, h, cols], ps[r, 0:pc], st[0:HD, h, cols])
                            if c == 1:
                                new = ps[r, pc:CW].rearrange("p (s t) -> p s t", s=SQ)
                                kv = slice(h // G * HD, (h // G + 1) * HD)
                                dst = (q_bd[kv, :, h * ST:(h + 1) * ST] if name[0] == "Q" else
                                       mq_bd[r, :, int(name[1]), h * ST:(h + 1) * ST])
                                last = dve.tensor_copy(dst, new)
                    elif name[0] == "Z":
                        last = dve.scalar_tensor_tensor(out=gate[:, int(name[1]), chunk_cols(c)], in0=tanh_t[:, c, :],
                                                        scalar=1.0, in1=ps[:, 0:CW], op0=ALU.add, op1=ALU.mult)
                    elif name[:2] == "CH":
                        j = int(name[2])
                        dve.wait_ge(free_act, 1 + q * FREE_ACT[-1] + FREE_ACT[n])
                        last = dve.tensor_tensor(u_buf[:, j, 2 + c * CW:2 + c * CW + pc], ps[:, 0:pc], cc_t[:, cols],
                                                 ALU.mult)
                        if c == 1:
                            last = dve.tensor_tensor(u_s[:, j, :, 2:2 + ST], ps[:, pc:CW].rearrange(
                                "p (s t) -> p s t", s=SQ), cc_t[:, TP:T].rearrange("p (s t) -> p s t", s=SQ), ALU.mult)
                    elif name[:2] == "CB":
                        need(taps[-1])
                        last = dve.tensor_tensor(c_t[:, chunk_cols(c)], ps[:, 0:CW], c_t[:, chunk_cols(c)], ALU.mult)
                    else:
                        last = dve.scalar_tensor_tensor(out=g_t[:, chunk_cols(c)], in0=tanh_t[:, c, :], scalar=1.0,
                                                        in1=ps[:, 0:CW], op0=ALU.add, op1=ALU.mult)
                    last.then_inc(free_dve, 1)

                taps = []

                def conv(j):
                    dve.wait_ge(free_dve, 1 + q * FREE_DVE[-1] + FREE_DVE[CH_END[j]])
                    for tap in range(3):
                        for out, src in ((c_t[:, 0:TP], u_buf[:, j, tap:tap + TP]),
                                         (c_t[:, TP:T].rearrange("p (s t) -> p s t", s=SQ),
                                          u_s[:, j, :, tap:tap + ST])):
                            w = cwt[:, j, tap:tap + 1]
                            if tap == 0:
                                tok = step(dve.tensor_scalar(out, src, w, None, ALU.mult))
                            else:
                                tok = step(dve.scalar_tensor_tensor(out=out, in0=src, scalar=w, in1=out, op0=ALU.mult,
                                                                    op1=ALU.add))
                        if tap < 2:
                            need(tok)
                    taps.append(tok)
                    dve.tensor_copy(tail[:, j, 0:2], u_buf[:, j, TP:TP + 2])
                    last = dve.tensor_copy(tail[:, j, 2:2 + 2 * SQ].rearrange("p (s t) -> p s t", s=SQ),
                                           u_s[:, j, :, ST:ST + 2])
                    tok = step(last)
                    if j == 2:
                        need(tok)
                        dve.tensor_copy(u_buf[:, :, 0:2], u_buf[:, :, TP:TP + 2]).then_inc(tail_ready, 1)

                def conv_y(n):
                    cols, j = chunk_cols(n % 2), int(role(n)[2])
                    dve.wait_ge(free_dve, 1 + q * FREE_DVE[-1] + FREE_DVE[n])
                    dve.scalar_tensor_tensor(out=g_t[:, cols], in0=g_t[:, cols], scalar=0.5, in1=c_t[:, cols],
                                             op0=ALU.mult, op1=ALU.mult).then_inc(y32, 1)

                def conv_lo(n):
                    cols, j = chunk_cols(n % 2), int(role(n)[2])
                    dve.wait_ge(y_his, q * YHI_Q + YHI["c", n])
                    sub(y_lo[:, j, cols], g_t[:, cols], y_hi[:, j, cols]).then_inc(y_ready, 1)

                def states():
                    dve.wait_ge(cache_turned, q + 1)
                    dve.tensor_copy(u_s[:, :, :, 0:2], pa[1][:, 0:3 * 2 * SQ].rearrange(
                        "p (j s t) -> p j s t", j=3, s=SQ)).then_inc(state_out, 1)

                def naturals():
                    dve.wait_ge(nat_turned, q + 1)
                    dve.wait_ge(s_stored, 1 + q * N_STATES * 16)
                    dve.tensor_copy(vn_s[:], pa[3][0:TS, 0:P])
                    dve.tensor_copy(k_nat[:], pa[3][:, P:2 * P])
                    dve.tensor_copy(kn_s[:], pa[3][0:TS, 2 * P:3 * P])
                    dve.wait_ge(v_his, q + 1)
                    for b in range(NBLK):
                        sub(v_st[:, 1 + b, :, HD:2 * HD], pa[2][:, b * P:(b + 1) * P].rearrange(
                            "p (v d) -> p v d", v=NKV), v_st[:, 1 + b, :, 0:HD])
                    dve.tensor_copy(v_nat[:], pa[2][:, (NBLK - 1) * P:NBLK * P]).then_inc(nat_out, 1)

                def sample_max():
                    dve.wait_ge(ss_done, q + 1)
                    dve.wait_ge(const_loaded, N_CONST)
                    need(step(dve.scalar_tensor_tensor(out=prob_s[:], in0=pa[0][0:SR, 0:P + TS], scalar=SCALE,
                                                       in1=bias_s[:], op0=ALU.mult, op1=ALU.add)))
                    a = step(dve.tensor_reduce(smx[:], prob_s[:], AX.X, ALU.max))
                    b = step(dve.tensor_reduce(tmx[:], pa[1][0:SR, 0:NM], AX.X, ALU.max))
                    need(b)
                    need(step(dve.tensor_tensor(smx[:], smx[:], sink_s[:], ALU.max)))
                    dve.tensor_scalar(snmx[:], smx[:], -1.0, None, ALU.mult)
                    dve.tensor_scalar(tnmx[:], tmx[:], -SCALE, None, ALU.mult).then_inc(ss_max, 1)

                def sample_norm():
                    dve.wait_ge(ss_exp, q + 1)
                    need(step(dve.tensor_tensor(sden[:], ssum[:], ssexp[:], ALU.add)))
                    step(dve.reciprocal(srden[:], sden[:]))
                    need(step(dve.reciprocal(trden[:], tsum[:])))
                    dve.tensor_scalar(prob_s[:], prob_s[:], srden[:], None, ALU.mult)
                    dve.tensor_scalar(mprob_s[:], mprob_s[:], trden[:], None, ALU.mult).then_inc(sp_ready, 1)

                def sample_pt():
                    dve.wait_ge(sp_turned, q + 1)
                    dve.tensor_copy(pt_s[:], pa[4][:, 0:SR])
                    dve.tensor_copy(ptn_s[:], pa[4][0:TS, SR:2 * SR])
                    dve.tensor_copy(mpt_s[:], pa[4][:, 2 * SR:4 * SR].rearrange("p (k r) -> p k r", k=2)).then_inc(
                        spt_ready, 1)

                def sample_select():
                    dve.wait_ge(so_done, q + 1)
                    for kv in range(NKV):
                        r = slice(kv * HD, (kv + 1) * HD)
                        for s in range(SQ):
                            a = s * 32 + kv * G * ST
                            src = pa[0][r, a:a + G * ST].rearrange("p (g t) -> p g t", g=G)
                            for gs, half, tiles in PLACES[kv]:
                                dve.tensor_copy(osel[half, tiles, s * ST:(s + 1) * ST], src[:, gs, :])
                    for hh in range(2):
                        r = slice(hh * HD, (hh + 1) * HD)
                        for p in range(2):
                            a = p * SR + (2 * p + hh) * ST
                            last = dve.tensor_copy(mosel[r, p, :].rearrange("p (s t) -> p s t", s=SQ), pa[1][
                                r, a:a + SR].rearrange("p (s t) -> p s t", s=SQ)[:, :, 0:ST])
                    last.then_inc(so_sel, 1)

                def sample_y():
                    dve.wait_ge(so_sel, q + 1)
                    dve.wait_ge(free_dve, 1 + q * FREE_DVE[-1] + FREE_DVE[GATES_END])
                    step(dve.scalar_tensor_tensor(out=osel[:], in0=osel[:], scalar=0.5, in1=gate[:, 0:3, TP:T],
                                                  op0=ALU.mult, op1=ALU.mult))
                    need(step(dve.scalar_tensor_tensor(out=mosel[:], in0=mosel[:], scalar=0.5, in1=gate[:, 3:5, TP:T],
                                                       op0=ALU.mult, op1=ALU.mult)))
                    step(dve.tensor_copy(y_hi[:, 3:6, TP:T], osel[:]))
                    need(step(dve.tensor_copy(y_hi[:, 6:8, TP:T], mosel[:])))
                    sub(y_lo[:, 3:6, TP:T], osel[:], y_hi[:, 3:6, TP:T])
                    sub(y_lo[:, 6:8, TP:T], mosel[:], y_hi[:, 6:8, TP:T]).then_inc(y_ready, 1)

                def soft_max(i):
                    dve.wait_ge(s_done, q * 2 * NBLK + (2 * i + 1))
                    if i == 0:
                        dve.wait_ge(y_stored, 1 + q * NX * 16)
                        dve.wait_ge(mkv_stored, 32)
                    for a in range(3):
                        ps = pa[a][:].rearrange("p (h k) -> p h k", h=2)
                        hs = slice(2 * a, 2 * a + 2)
                        if i == 0:
                            dve.scalar_tensor_tensor(out=prob[:, hs, 0:W], in0=ps[:, :, 0:W], scalar=SCALE,
                                                     in1=bias_first[:, hs, :], op0=ALU.mult, op1=ALU.add)
                            last = dve.scalar_tensor_tensor(out=prob[:, hs, W:2 * W], in0=ps[:, :, W:2 * W],
                                                            scalar=SCALE, in1=bias[:, hs, W:2 * W], op0=ALU.mult,
                                                            op1=ALU.add)
                        else:
                            last = dve.scalar_tensor_tensor(out=prob[:, hs, :], in0=ps, scalar=SCALE,
                                                            in1=bias[:, hs, :], op0=ALU.mult, op1=ALU.add)
                    need(step(last))
                    need(step(dve.tensor_reduce(mx[:], prob[:], AX.X, ALU.max)))
                    need(step(dve.tensor_tensor(mx[:], mx[:], sink[:], ALU.max)))
                    dve.tensor_scalar(nmx[:], mx[:], -1.0, None, ALU.mult)
                    dve.tensor_tensor(sexp[:], sink[:], mx[:], ALU.subtract).then_inc(s_max, 1)
                    dve.wait_ge(s_done, q * 2 * NBLK + (2 * i + 2))
                    for hh in range(2):
                        last = dve.tensor_reduce(mmx[:, 2 * hh:2 * hh + 2], pa[3 + hh][:].rearrange(
                            "p (t k) -> p t k", t=2), AX.X, ALU.max)
                    need(step(last))
                    dve.tensor_scalar(nmmx[:], mmx[:], -SCALE, None, ALU.mult).then_inc(s_max, 1)
                    if i == 0:
                        dve.tensor_copy(bias_first[:], bias[:, :, 0:W])

                def soft_norm(i):
                    dve.wait_ge(exps, q * 2 * NBLK + (2 * i + 1))
                    need(step(dve.tensor_tensor(den[:], sums[:], sexp[:], ALU.add)))
                    need(step(dve.reciprocal(rden[:], den[:])))
                    for h in range(NH):
                        last = dve.tensor_scalar(prob[:, h, :], prob[:, h, :], rden[:, h:h + 1], None, ALU.mult)
                    last.then_inc(p_ready, 1)

                def mem_norm(i):
                    dve.wait_ge(exps, q * 2 * NBLK + (2 * i + 2))
                    need(step(dve.reciprocal(mrden[:], msums[:])))
                    for u in range(4):
                        last = dve.tensor_scalar(mprob[:, u, :], mprob[:, u, :], mrden[:, u:u + 1], None, ALU.mult)
                    last.then_inc(p_ready, 1)

                def pt_lo_of(i):
                    dve.wait_ge(pt_his, q * 2 * NBLK + (2 * i + 1))
                    for a in range(3):
                        s = slice(4 * a, 4 * a + 4)
                        last = sub(pt_lo[:, s, :], pa[a][:].rearrange("p (a b) -> p a b", a=4), pt_hi[:, s, :])
                    last.then_inc(pt_ready, 1)
                    dve.wait_ge(pt_his, q * 2 * NBLK + (2 * i + 2))
                    for a in range(2):
                        s = slice(4 * a, 4 * a + 4)
                        last = sub(mpt_lo[:, s, :], pa[3 + a][:].rearrange("p (a b) -> p a b", a=4), mpt_hi[:, s, :])
                    last.then_inc(pt_ready, 1)

                def attn_y(i):
                    gr, p = i // 2, i % 2
                    dve.wait_ge(o_halves, q * 2 * NBLK + (2 * i + 1))
                    for kv in range(NKV):
                        src = pa[kv][0:HD, 0:G * P].rearrange("p (g t) -> p g t", g=G)
                        for gs, half, tiles in PLACES[kv]:
                            tok = step(dve.tensor_tensor(o_sum[half, tiles, :], src[:, gs, :], o_half[half, tiles, :],
                                                         ALU.add))
                    dve.wait_ge(o_halves, q * 2 * NBLK + (2 * i + 2))
                    for hh in range(2):
                        r = slice(hh * HD, (hh + 1) * HD)
                        last = dve.tensor_tensor(mo_sum[r, :], pa[2][0:HD, hh * 2 * P:(hh + 1) * 2 * P], mo_half[r, :],
                                                 ALU.add)
                    last.then_inc(o_taken, 1)
                    need(tok)
                    dve.scalar_tensor_tensor(out=o_sum[:], in0=o_sum[:], scalar=0.5,
                                             in1=gate[:, 0:3, i * P:(i + 1) * P], op0=ALU.mult,
                                             op1=ALU.mult).then_inc(y32, 1)
                    dve.wait_ge(o_taken, q * NBLK + (i + 1))
                    dve.scalar_tensor_tensor(out=mo_sum[:], in0=mo_sum[:], scalar=0.5, in1=gate[
                        :, 3 + p, gr * 2 * P:(gr + 1) * 2 * P], op0=ALU.mult, op1=ALU.mult).then_inc(y32, 1)

                def attn_lo(i):
                    gr, p = i // 2, i % 2
                    dve.wait_ge(y_his, q * YHI_Q + YHI["a", i])
                    cols, mcols = slice(i * P, (i + 1) * P), slice(gr * 2 * P, (gr + 1) * 2 * P)
                    sub(y_lo[:, 3:6, cols], o_sum[:], y_hi[:, 3:6, cols])
                    sub(y_lo[:, 6 + p, mcols], mo_sum[:], y_hi[:, 6 + p, mcols]).then_inc(y_ready, 1)

                def carry():
                    for t in (k_hh, k_ll):
                        dve.tensor_copy(t[:, :, 0:W], t[:, :, TP:TP + W])
                    dve.tensor_copy(v_st[:, 0, :, :], v_st[:, NBLK, :, :]).then_inc(y_ready, 1)

                def out_rows(f):
                    dve.wait_ge(o_squares, q * NOUT + (f + 1))
                    cols = slice(f * P, (f + 1) * P)
                    last = dve.tensor_tensor(o_nat[:, :, cols], pa[f % 2][:].rearrange("p (b c) -> p b c", b=NBLK),
                                             g_post[:, cols].unsqueeze(1).to_broadcast([P, NBLK, P]), ALU.mult)
                    if f % 4 == 3:
                        dve.wait_ge(os_squares, q * 2 + (f // 4 + 1))
                        cols = slice((f - 3) * P, (f + 1) * P)
                        last = dve.tensor_tensor(o_nat_s[:, cols], pa[4][0:TS, :], g_post[0:TS, cols], ALU.mult)
                    last.then_inc(o_rows, 1)

                for n in range(NC):
                    evac(n)
                    for j in range(3):
                        if n == CH_END[j]:
                            conv(j)
                    if n and role(n - 1)[:2] == "CB" and n - 1 < CB_LAST:
                        conv_lo(n - 1)
                    if role(n)[:2] == "CB":
                        conv_y(n)
                        if n >= CB_LAST:
                            conv_lo(n)
                    if n == AT_CACHE:
                        states()
                    if n == AT_NAT:
                        naturals()
                    if n == AT_SAMPLE[0]:
                        sample_max()
                    if n == AT_SAMPLE[0] + 1:
                        sample_norm()
                    if n == AT_SAMPLE[1]:
                        sample_pt()
                    if n == AT_SAMPLE[2]:
                        sample_select()
                    if n == GATES_END:
                        sample_y()
                    for i in range(NBLK):
                        if n == AT_S[i]:
                            soft_max(i)
                        if n == AT_S[i] + 1:
                            soft_norm(i)
                            mem_norm(i)
                        if n == AT_T[i]:
                            pt_lo_of(i)
                        if n == AT_PV[i]:
                            attn_y(i)
                        if n == AT_PV[i] + 1:
                            attn_lo(i)
                    if n == AT_PV[2] + 1:
                        carry()
                    if n == 2 * NIN:
                        dve.wait_ge(tail_turned, q + 1)
                        dve.tensor_copy(tail_nat[:], pa[4][0:2 + 2 * SQ, 0:DC]).then_inc(tail_out, 1)
                    f = (n - 2 * NIN) // 2 - 1
                    if f >= 0 and n % 2 == 0:
                        out_rows(f)
                    for b in range(NX):
                        if n == AT_NORM[b]:
                            norm_rows(b, rows_of(b), g_pre, (q + 1) * NX + (2 + b + 1))
                        if n == AT_TURN[b] and b < NBLK:
                            lo_of(h_hi, h_lo, b, 2, (q + 1) * NX + (2 + b + 1))
                        if n == AT_TURN[b] and b == NBLK:
                            sample_lo(2, (q + 1) * NX + (2 + b + 1))
                out_rows(NOUT - 1)

                need(step(dve.tensor_reduce(o_mean[:], o_parts[:], AX.X, ALU.add)))
                dve.tensor_scalar(o_mean[:], o_mean[:], 1.0 / D, EPS, ALU.mult, ALU.add).then_inc(o_means, 1)
                dve.wait_ge(res_loaded, (q + 1) * NX * 16)
                dve.wait_ge(o_rstds, q + 1)
                dve.wait_ge(o_rows, 1 + (q + 1) * NOUT)
                for b in range(NX):
                    o = o_nat[:, b, :] if b < NBLK else o_nat_s[:]
                    dve.scalar_tensor_tensor(out=o, in0=o, scalar=o_rstd[0:rows_of(b), b:b + 1], in1=residual[b],
                                             op0=ALU.mult, op1=ALU.add).then_inc(y_rows, 1)
                assert n_[0] == DVE_Q, n_


def loads_of(t):
    return (PRO_W + t) // 2 + 1


POWER_AFTER = [26, 26, 27, 28, 29]
FIRST_X = [(0,), (1,), (2,), (3, 4)]
CH_END = [2 * TILES.index(f"CH{j}") + 1 for j in range(3)]


def _order():
    y32, yhi, a, b = {}, {}, 0, 0
    for n in range(NC):
        if role(n)[:2] == "CB":
            a, b = a + 1, b + 1
            y32["c", n], yhi["c", n] = a, b
        for i in range(NBLK):
            if n == AT_PV[i]:
                a, b = a + 2, b + 1
                y32["a", i], yhi["a", i] = a, b
    return y32, yhi, a, b


CB_LAST = 2 * TILES.index("CB2")
Y32, YHI, Y32_Q, YHI_Q = _order()
HALF, _n = {}, 0
for _c in range(2 * NIN):
    if not freed_by_act(_c) and role(_c)[:2] not in ("CH", "CB"):
        _n += 1
        HALF[_c] = _n
HALF_Q = _n


def constants():
    slopes = np.power(np.float32(2.0), -8.0 * np.arange(1, NH + 1, dtype=np.float32) / NH).astype(np.float32)

    def table(dist, valid):
        b = -(slopes[:, None, None] * np.abs(dist).astype(np.float32)[None])
        return np.where(valid[None], b, np.float32(NEG)).astype(np.float32)

    i, c = np.arange(W)[:, None], np.arange(2 * W)[None]
    dist = i + W - c
    bias = table(dist, (dist >= 0) & (dist < W)).transpose(1, 0, 2)
    bias_s = np.zeros((32 * SQ, P + TS), np.float32)
    t = np.arange(ST)[:, None]
    for s in range(SQ):
        old = W + t - np.arange(W)[None]
        new = t - np.arange(TS)[None] % ST
        d = np.concatenate([old, new], 1)
        own = np.concatenate([np.ones((1, W), bool), np.arange(TS)[None] // ST == s], 1)
        bias_s[32 * s:32 * s + NH * ST] = table(d, (d >= 0) & (d < W) & own).reshape(NH * ST, P + TS)
    return {"ident": np.eye(P, dtype=np.float32), "bias": np.ascontiguousarray(bias), "bias_s": bias_s}


_INS = ["x_prompt", "x_sample", "mem_prompt", "state_conv", "cache_swa_k", "cache_swa_v", "cache_mem_k", "cache_mem_v",
        "pre_norm_g", "post_norm_g", "w_in", "conv_w", "attn_sinks", "mem_norm_g", "w_mem_k", "w_mem_v", "w_out"]
_OUTS = [(1, 2048, 1024), (8, 4, 1024), (1, 1, 2, 384), (1, 1, 128, 2, 64), (1, 1, 128, 2, 64), (1, 1, 256, 4, 64),
         (1, 1, 256, 4, 64), (1, 8, 2, 384), (1, 8, 128, 2, 64), (1, 8, 128, 2, 64)]


def kernel(**inputs):
    import concourse.bacc as bacc
    from concourse.bass_utils import run_bass_kernel_spmd

    nc = bacc.Bacc("TRN2", target_bir_lowering=False, num_devices=1, dynamic_dma_scratch_size=1024)
    arrays, args = {}, []
    given = {name: np.ascontiguousarray(inputs[name]) for name in _INS}
    for name, a in list(given.items()) + list(constants().items()):
        arrays[f"in_{name}"] = a
        args.append(nc.dram_tensor(f"in_{name}", a.shape, mybir.dt.from_np(a.dtype), kind="ExternalInput").ap())
    for i, shape in enumerate(_OUTS):
        args.append(nc.dram_tensor(f"out_{i}", shape, F32, kind="ExternalOutput").ap())
    layer(nc, *args)
    r = run_bass_kernel_spmd(nc, [arrays], core_ids=[0])
    return tuple(r.results[0][f"out_{i}"] for i in range(len(_OUTS)))
```
